# Optimizing a Trainium2 kernel written in Bass

```python
import math
import jax
import jax.numpy as jnp
from jax import lax
import numpy as np

D_MODEL = 1024
BATCH = 1
SEQ = 2048
DEPTH = 1
DEC_BATCH = 8
DEC_SEQ = 4
PAST_LEN = 16384
PAGE_SIZE = 128

S5_WIDTH = D_MODEL // 2
S5_GROUP = 16
S5_GROUPS = S5_WIDTH // S5_GROUP
S5_STATE = 64
GLA_HEADS = 4
GLA_KEY_WIDTH = D_MODEL // 4
GLA_VAL_WIDTH = D_MODEL // 2
GLA_DK = GLA_KEY_WIDTH // GLA_HEADS
GLA_DV = GLA_VAL_WIDTH // GLA_HEADS
GLA_GATE_RANK = 16
GLA_TAU = 16.0
GLA_CHUNK = 64
D_FF = 4 * D_MODEL
EPS = 1e-6

OFF_U = 0
OFF_Q = OFF_U + S5_WIDTH
OFF_K = OFF_Q + GLA_KEY_WIDTH
OFF_V = OFF_K + GLA_KEY_WIDTH
OFF_R = OFF_V + GLA_VAL_WIDTH
OFF_A = OFF_R + GLA_VAL_WIDTH
OFF_GS = OFF_A + GLA_GATE_RANK
OFF_GG = OFF_GS + D_MODEL
IN_WIDTH = OFF_GG + D_MODEL

kernel_name = "s5_gla_gated_hybrid_step"

def rmsnorm(x, g):
    xf = x.astype(jnp.float32)
    y = xf * lax.rsqrt(jnp.mean(xf * xf, axis=-1, keepdims=True) + EPS) * g.astype(jnp.float32)
    return y.astype(x.dtype)

def _complex_combine(e1, e2):
    a1r, a1i, b1r, b1i = e1
    a2r, a2i, b2r, b2i = e2
    return (a2r * a1r - a2i * a1i,
            a2r * a1i + a2i * a1r,
            a2r * b1r - a2i * b1i + b2r,
            a2r * b1i + a2i * b1r + b2i)

def s5_mixer(u, x0_re, x0_im, lam_re, lam_im, log_dt, b_re, b_im, c_re, c_im, d_skip):
    n, l, _ = u.shape
    ug = u.astype(jnp.float32).reshape(n, l, S5_GROUPS, S5_GROUP)
    dt = jnp.exp(log_dt.astype(jnp.float32))[:, None]
    lr = jnp.minimum(lam_re.astype(jnp.float32), -1e-4)
    li = lam_im.astype(jnp.float32)
    mag = jnp.exp(lr * dt)
    ar = mag * jnp.cos(li * dt)
    ai = mag * jnp.sin(li * dt)
    den = lr * lr + li * li
    fr = ((ar - 1.0) * lr + ai * li) / den
    fi = (ai * lr - (ar - 1.0) * li) / den
    br = b_re.astype(jnp.float32)
    bi = b_im.astype(jnp.float32)
    bb_r = fr[:, :, None] * br - fi[:, :, None] * bi
    bb_i = fr[:, :, None] * bi + fi[:, :, None] * br
    bu_r = jnp.einsum('nlgh,gph->nlgp', ug, bb_r)
    bu_i = jnp.einsum('nlgh,gph->nlgp', ug, bb_i)
    x0r = x0_re.astype(jnp.float32)
    x0i = x0_im.astype(jnp.float32)
    bu_r = bu_r.at[:, 0].add(ar * x0r - ai * x0i)
    bu_i = bu_i.at[:, 0].add(ar * x0i + ai * x0r)
    a_r = jnp.broadcast_to(ar, bu_r.shape)
    a_i = jnp.broadcast_to(ai, bu_i.shape)
    _, _, xs_r, xs_i = lax.associative_scan(_complex_combine, (a_r, a_i, bu_r, bu_i), axis=1)
    y = (jnp.einsum('nlgp,ghp->nlgh', xs_r, c_re.astype(jnp.float32))
         - jnp.einsum('nlgp,ghp->nlgh', xs_i, c_im.astype(jnp.float32))
         + d_skip.astype(jnp.float32) * ug)
    y = y.reshape(n, l, S5_WIDTH).astype(u.dtype)
    return y, xs_r[:, -1].astype(x0_re.dtype), xs_i[:, -1].astype(x0_im.dtype)

def gla_mixer(q, k, v, glog, s0):
    n, l = q.shape[0], q.shape[1]
    c = min(GLA_CHUNK, l)
    nc = -(-l // c)
    pad = nc * c - l

    def prep(a):
        a = jnp.pad(a.astype(jnp.float32), ((0, 0), (0, pad), (0, 0), (0, 0)))
        a = a.reshape(n, nc, c, a.shape[2], a.shape[3])
        return jnp.transpose(a, (1, 0, 3, 2, 4))

    qs, ks, vs, gs = prep(q), prep(k), prep(v), prep(glog)
    mask = jnp.tril(jnp.ones((c, c), dtype=bool))[None, None, :, :, None]

    def step(s, inp):
        qc, kc, vc, gc = inp
        b = jnp.cumsum(gc, axis=2)
        o_inter = jnp.einsum('nhcd,nhde->nhce', qc * jnp.exp(b), s)
        diff = b[:, :, :, None, :] - b[:, :, None, :, :]
        dec = jnp.exp(jnp.where(mask, diff, -jnp.inf))
        att = jnp.einsum('nhid,nhjd,nhijd->nhij', qc, kc, dec)
        o_intra = jnp.einsum('nhij,nhje->nhie', att, vc)
        b_last = b[:, :, -1:, :]
        s_new = (jnp.exp(b_last[:, :, 0, :])[..., None] * s
                 + jnp.einsum('nhcd,nhce->nhde', kc * jnp.exp(b_last - b), vc))
        return s_new, o_inter + o_intra

    s_fin, outs = lax.scan(step, s0.astype(jnp.float32), (qs, ks, vs, gs))
    o = jnp.transpose(outs, (1, 0, 3, 2, 4)).reshape(n, nc * c, GLA_HEADS, GLA_DV)[:, :l]
    return o, s_fin.astype(s0.dtype)

def hybrid_layer(x, s5_re0, s5_im0, gla_s0,
                 g_mix, w_in, lam_re, lam_im, log_dt, b_re, b_im, c_re, c_im, d_skip,
                 w_s5_glu, w_gate_up, b_gate, g_gla_norm, w_s5_br, w_gla_br, w_out,
                 g_ffn, w_ff1, w_ff2, g_final):
    n, l, _ = x.shape
    h = rmsnorm(x, g_mix)
    z = h @ w_in
    u = z[..., OFF_U:OFF_Q]
    q = z[..., OFF_Q:OFF_K].reshape(n, l, GLA_HEADS, GLA_DK) * (GLA_DK ** -0.5)
    k = z[..., OFF_K:OFF_V].reshape(n, l, GLA_HEADS, GLA_DK)
    v = z[..., OFF_V:OFF_R].reshape(n, l, GLA_HEADS, GLA_DV)
    r = z[..., OFF_R:OFF_A]
    a_low = z[..., OFF_A:OFF_GS]
    gate_s5 = z[..., OFF_GS:OFF_GG]
    gate_gla = z[..., OFF_GG:IN_WIDTH]

    y5, s5_re, s5_im = s5_mixer(u, s5_re0, s5_im0, lam_re, lam_im, log_dt,
                                b_re, b_im, c_re, c_im, d_skip)
    z5 = jax.nn.gelu(y5)
    o5 = z5 * jax.nn.sigmoid(z5 @ w_s5_glu)

    glog = (jax.nn.log_sigmoid((a_low @ w_gate_up + b_gate).astype(jnp.float32)) / GLA_TAU)
    glog = glog.reshape(n, l, GLA_HEADS, GLA_DK)
    og, gla_s = gla_mixer(q, k, v, glog, gla_s0)
    og = og * lax.rsqrt(jnp.mean(og * og, axis=-1, keepdims=True) + EPS) * g_gla_norm.astype(jnp.float32)
    og = og.reshape(n, l, GLA_VAL_WIDTH).astype(x.dtype) * jax.nn.silu(r)

    merged = jax.nn.sigmoid(gate_s5) * (o5 @ w_s5_br) + jax.nn.sigmoid(gate_gla) * (og @ w_gla_br)
    x = x + merged @ w_out

    h2 = rmsnorm(x, g_ffn)
    x = x + jnp.square(jax.nn.relu(h2 @ w_ff1)) @ w_ff2
    return rmsnorm(x, g_final), s5_re, s5_im, gla_s

def setup_inputs(seed: int = 0) -> dict:
    key = jax.random.key(seed)
    ks = jax.random.split(key, 32)
    f32 = jnp.float32
    nrm = lambda i, shape, scale: jax.random.normal(ks[i], shape, f32) * scale
    n_idx = jnp.arange(S5_STATE, dtype=f32)[None, :]
    return {
        "x_prompt": nrm(0, (BATCH, SEQ, D_MODEL), 1.0),
        "x_sample": nrm(1, (DEC_BATCH, DEC_SEQ, D_MODEL), 1.0),
        "state_s5_re": nrm(2, (DEC_BATCH, S5_GROUPS, S5_STATE), 1.0),
        "state_s5_im": nrm(3, (DEC_BATCH, S5_GROUPS, S5_STATE), 1.0),
        "state_gla": nrm(4, (DEC_BATCH, GLA_HEADS, GLA_DK, GLA_DV), 0.5),
        "g_mix": 1.0 + nrm(5, (D_MODEL,), 0.02),
        "w_in": nrm(6, (D_MODEL, IN_WIDTH), D_MODEL ** -0.5),
        "lam_re": -0.5 + nrm(7, (S5_GROUPS, S5_STATE), 0.01),
        "lam_im": jnp.pi * n_idx + nrm(8, (S5_GROUPS, S5_STATE), 0.01),
        "log_dt": jax.random.uniform(ks[9], (S5_GROUPS,), f32, math.log(1e-3), math.log(1e-1)),
        "b_re": nrm(10, (S5_GROUPS, S5_STATE, S5_GROUP), (2.0 * S5_GROUP) ** -0.5),
        "b_im": nrm(11, (S5_GROUPS, S5_STATE, S5_GROUP), (2.0 * S5_GROUP) ** -0.5),
        "c_re": nrm(12, (S5_GROUPS, S5_GROUP, S5_STATE), (2.0 * S5_STATE) ** -0.5),
        "c_im": nrm(13, (S5_GROUPS, S5_GROUP, S5_STATE), (2.0 * S5_STATE) ** -0.5),
        "d_skip": nrm(14, (S5_GROUPS, S5_GROUP), 1.0),
        "w_s5_glu": nrm(15, (S5_WIDTH, S5_WIDTH), S5_WIDTH ** -0.5),
        "w_gate_up": nrm(16, (GLA_GATE_RANK, GLA_KEY_WIDTH), GLA_GATE_RANK ** -0.5),
        "b_gate": nrm(17, (GLA_KEY_WIDTH,), 0.01),
        "g_gla_norm": 1.0 + nrm(18, (GLA_DV,), 0.02),
        "w_s5_br": nrm(19, (S5_WIDTH, D_MODEL), S5_WIDTH ** -0.5),
        "w_gla_br": nrm(20, (GLA_VAL_WIDTH, D_MODEL), GLA_VAL_WIDTH ** -0.5),
        "w_out": nrm(21, (D_MODEL, D_MODEL), D_MODEL ** -0.5),
        "g_ffn": 1.0 + nrm(22, (D_MODEL,), 0.02),
        "w_ff1": nrm(23, (D_MODEL, D_FF), D_MODEL ** -0.5),
        "w_ff2": nrm(24, (D_FF, D_MODEL), D_FF ** -0.5),
        "g_final": 1.0 + nrm(25, (D_MODEL,), 0.02),
    }

def reference(x_prompt, x_sample, state_s5_re, state_s5_im, state_gla,
              g_mix, w_in, lam_re, lam_im, log_dt, b_re, b_im, c_re, c_im, d_skip,
              w_s5_glu, w_gate_up, b_gate, g_gla_norm, w_s5_br, w_gla_br, w_out,
              g_ffn, w_ff1, w_ff2, g_final):
    weights = (g_mix, w_in, lam_re, lam_im, log_dt, b_re, b_im, c_re, c_im, d_skip,
               w_s5_glu, w_gate_up, b_gate, g_gla_norm, w_s5_br, w_gla_br, w_out,
               g_ffn, w_ff1, w_ff2, g_final)
    p_re0 = jnp.zeros((x_prompt.shape[0], S5_GROUPS, S5_STATE), state_s5_re.dtype)
    p_im0 = jnp.zeros((x_prompt.shape[0], S5_GROUPS, S5_STATE), state_s5_im.dtype)
    p_gla0 = jnp.zeros((x_prompt.shape[0], GLA_HEADS, GLA_DK, GLA_DV), state_gla.dtype)
    y_prompt = x_prompt
    y_sample = x_sample
    for _ in range(DEPTH):
        y_prompt, p_re, p_im, p_gla = hybrid_layer(y_prompt, p_re0, p_im0, p_gla0, *weights)
        y_sample, s_re, s_im, s_gla = hybrid_layer(y_sample, state_s5_re, state_s5_im, state_gla, *weights)
    return (y_prompt, y_sample, p_re, p_im, p_gla, s_re, s_im, s_gla)


_drawn_inputs = setup_inputs


def setup_inputs(seed=0):
    import zlib

    import numpy as np

    out = dict(_drawn_inputs(seed))
    spreads = {}
    factors = {'lam_re': 4.161, 'b_gate': 8.0, 'g_gla_norm': 8.0, 'g_ffn': 3.249, 'g_final': 2.777}
    for name, (base, spread) in spreads.items():
        noise = np.random.default_rng([zlib.crc32(name.encode()), seed]).standard_normal(out[name].shape)
        drawn = base * np.exp(spread * noise) if base else spread * noise
        out[name] = jnp.asarray(drawn.astype(out[name].dtype))
    for name, factor in factors.items():
        out[name] = (out[name] * factor).astype(out[name].dtype)
    return out
```

```python
from contextlib import ExitStack

import concourse.bass as bass
import numpy as np
from concourse import mybir

F32 = mybir.dt.float32
F32R = mybir.dt.float32r
U8 = mybir.dt.uint8
ALU = mybir.AluOpType
ACT = mybir.ActivationFunctionType

P = 128
D_MODEL = 1024
SEQ = 2048
DEC_BATCH, DEC_SEQ = 8, 4
S5_WIDTH, S5_GROUP, S5_GROUPS, S5_STATE = 512, 16, 32, 64
HEADS, DK, DV = 4, 64, 128
RANK = 16
TAU = 16.0
D_FF = 4096
EPS = 1e-6

HALVES = 2
TP = SEQ // HALVES
DS = DEC_BATCH // HALVES
DT = DS * DEC_SEQ
N = TP + DT
BLK = [(0, 352), (352, 344), (696, 344)]
KT_D = D_MODEL // P
KT_S = S5_WIDTH // P
WB = 4 * P
RING = 4

J = 8
PAIRS = S5_GROUPS // 2
NC = TP // J
UC = NC + 2 * DS
YC = NC + DS
EC = NC + 2
C_T, C_PR, C_PI, C_QR, C_QI, C_EC, C_ES = 0, 256, 384, 512, 640, 768, 768 + EC
C_W = 768 + 2 * EC
CR = 4

C = 128
CHUNKS = TP // C
LEVELS = [64, 32, 16, 8, 4, 2, 1]
NL = len(LEVELS)
DEC_LEVELS = [l for l, s in enumerate(LEVELS) if 2 * s <= DEC_SEQ]
DE_R, DE_L, DE_K, DE_Q = 0, NL * 128, 2 * NL * 128, 2 * NL * 128 + 256
DE_W = 2 * NL * 128 + 512

IT_A = 0
IT_GLU = IT_A + 6
IT_M1 = IT_GLU + 1
IT_R = IT_M1 + 6
IT_M2 = IT_R + 2
IT_OUT = IT_M2 + 6
IT_FF = IT_OUT + 4
ITERS = IT_FF + 32
FF_GROUPS = 8

A_H = 0
A_O = A_H + 16 * N
A_Z = A_O + 8 * N
A_M = A_Z + 8 * N
A_G = A_M + 8 * N
A_END = A_G + 2 * N
REGIONS = [("h0", A_H, 8 * N), ("h1", A_H + 8 * N, 8 * N), ("o", A_O, 8 * N), ("z", A_Z, 8 * N), ("m", A_M, 8 * N),
           ("g", A_G, 2 * N)]
M_U = A_M
M_TMP = A_M + S5_GROUPS * UC
M_C0 = M_TMP + 1400
O_UP = A_O
O_A = A_O + 4352
O_AH, O_AL = O_A + N, O_A + N + 1024
O_T = O_A + N
O_C0 = A_O + 4352
C_SLOT = [M_C0, M_C0 + C_W, O_C0, O_C0 + C_W]
O_TAB, TAB_W = A_O + 7440, 27
O_STG = O_T + N
O_ST = A_O
O_DE = [A_O + 1024, A_O + 1024 + DE_W]
O_KT = A_O + 1024 + 2 * DE_W
O_ATT = O_KT + NL * 256
O_S0 = O_DE[1]

SETS = {"nx": (1, 0), "a": (6, 6), "low": (1, 1), "glu": (2, 2), "m1": (8, 8), "r": (4, 4), "m2": (8, 8),
        "out": (4, 4), "nf": (1, 0), "ff": (48, 48), "ny": (1, 0)}
SET_BASE, SET_TOTAL = {}, [0, 0]
for _name, _n in SETS.items():
    SET_BASE[_name] = tuple(SET_TOTAL)
    SET_TOTAL = [SET_TOTAL[0] + _n[0], SET_TOTAL[1] + _n[1]]
SP_X, SP_Z5, SP_O5, SP_OG, SP_MG, SP_H2, SP_ALL = 0, 8, 12, 16, 20, 28, 36

V_MIX, V_FFN, V_FIN, V_BG, V_GLA, V_SEQ = 0, 8, 16, 24, 26, 27
V_ALL = V_SEQ + DS
MAGIC = 12582912.0
PI2_1, PI2_2, PI2_3 = 6.28125, 0.0019350051879882812, 3.019916050e-07


def ff_before(g, part):
    if part == "down":
        return (min(g + 2, FF_GROUPS) if isinstance(g, int) else g + 2), g
    return g, (max(g - 1, 0) if isinstance(g, int) else g - 1)


def ff_set(g, part):
    ups, downs = ff_before(g, part)
    return ups * 2 + downs * 4


def ff_it(g, part):
    ups, downs = ff_before(g, part)
    return ups * 2 + downs * 2


class Arena:

    def __init__(self, tensors):
        self.tensors = tensors

    def find(self, col):
        for tensor, (_, start, width) in zip(self.tensors, REGIONS):
            if start <= col < start + width:
                return tensor, start
        raise IndexError(col)

    def __getitem__(self, key):
        rows, span = key
        tensor, start = self.find(span.start)
        return tensor[rows, span.start - start:span.stop - start]

    def at(self, col, offset, n):
        tensor, start = self.find(col)
        return tensor[:, bass.ds(col - start + offset, n)]


def build(nc, xT, wpack, wa, wgu_d, vec_d, ident_d, masks_d, dmask_d, s5small, b_d, c_d, cbd_d, dcol_d,
          s5dec_d, gladec_d, yT, s5_prompt, gla_prompt, s5_dec_out, gla_dec_out):
    u_dram = nc.dram_tensor("u_scratch", (KT_S, P, J, UC), F32, kind="Internal").ap()
    y_dram = nc.dram_tensor("y_scratch", (KT_S, P, J, YC), F32, kind="Internal").ap()
    c_dram = nc.dram_tensor("s5_constants", (PAIRS, P, C_W), F32, kind="Internal").ap()

    with ExitStack() as ctx:
        slab_at = (nc.sbuf_usable_end - A_END * 4) // 64 * 64

        def regions(kind, dt):
            return Arena([nc.alloc_sbuf_tensor_at(f"{kind}_{name}", [P, width], dt, offset=slab_at + start * 4)
                          for name, start, width in REGIONS])
        fa, ra = regions("f", F32), regions("r", F32R)

        def sb(name, shape, dt=F32):
            return ctx.enter_context(nc.sbuf_tensor(name, shape, dt))

        def sem(name):
            return ctx.enter_context(nc.semaphore(name))

        w_raw = sb("w_raw", [P, RING, WB])
        w_hi = sb("w_hi", [P, RING, WB], F32R)
        w_lo = sb("w_lo", [P, RING, WB], F32R)
        vT = sb("vT", [P, 512])
        khT = sb("khT", [P, 256])
        masks = sb("masks", [P, NL * 256 + 512], U8)
        dmask = sb("dmask", [DT, len(DEC_LEVELS) * 32 + 64], U8)
        ident = sb("ident", [P, P])
        ones = sb("ones", [P, P])
        vec = sb("vec", [P, V_ALL])
        wgu = sb("wgu", [RANK, 2 * P])
        dcol = sb("dcol", [P, S5_GROUPS])
        gla_s = sb("gla_s", [P, 2, DV])
        decay = sb("decay", [P, 8])
        s5_carry = sb("s5_carry", [P, 2, PAIRS])
        s5_m8 = sb("s5_m8", [P, PAIRS])
        s5_a4 = sb("s5_a4", [P, 2, PAIRS])
        s5_dec = sb("s5_dec", [P, 2, PAIRS, DS])
        s5_new = sb("s5_new", [P, 2, PAIRS, DS])
        s5_tmp = sb("s5_tmp", [P, 2, PAIRS, DS])
        zero = sb("zero", [P, 1])
        sml = sb("s5_small", [P, len(SMALL), PAIRS])
        assert nc.sbuf_base <= slab_at, (nc.sbuf_base, slab_at)
        ps = ctx.enter_context(nc.psum_tensor("ps", [P, 8, 512], F32))

        w_landed = [sem(f"w_landed{s}") for s in range(RING)]
        w_split = [sem(f"w_split{s}") for s in range(RING)]
        w_used = [sem(f"w_used{s}") for s in range(RING)]
        set_read = [sem("set0_read"), sem("set1_read")]
        const_landed, s5in_landed, bc_landed, cbd_landed = (sem("const_landed"), sem("s5in_landed"),
                                                            sem("bc_landed"), sem("cbd_landed"))
        x_landed, res_landed, wa_landed = sem("x_landed"), sem("res_landed"), sem("wa_landed")
        ones_ready = sem("ones_ready")
        sq_ready, ssum_ready, ms_done, std_ready = sem("sq_ready"), sem("ssum_ready"), sem("ms_done"), sem("std_ready")
        full_ready, hi_ready, split_ready = sem("full_ready"), sem("hi_ready"), sem("split_ready")
        u_pad, u_stored, u_landed = sem("u_pad"), sem("u_stored"), sem("u_landed")
        wa_split, low_done, low_ready, gpre_done = sem("wa_split"), sem("low_done"), sem("low_ready"), sem("gpre_done")
        gln_ready, gmin_ready, b_ready = sem("gln_ready"), sem("gmin_ready"), sem("b_ready")
        dt_ready, trig_in, trig_out = sem("dt_ready"), sem("trig_in"), sem("trig_out")
        qe_ready, qe_stored, g_ready = sem("qe_ready"), sem("qe_stored"), sem("g_ready")
        tp_done, p_ready, t_ready, tp_stored = sem("tp_done"), sem("p_ready"), sem("t_ready"), [sem("tp_stored0"), sem("tp_stored1")]
        c_landed = [sem(f"c_landed{s}") for s in range(CR)]
        chunk_in_done, chunk_in_read = sem("chunk_in_done"), sem("chunk_in_read")
        state_ready, yrow_done, yrow_read = sem("state_ready"), sem("yrow_done"), sem("yrow_read")
        yrow_stored, yperm_landed, gelu_ready = sem("yrow_stored"), sem("yperm_landed"), sem("gelu_ready")
        s5dec_landed, s5dec_ready = sem("s5dec_landed"), sem("s5dec_ready")
        stage_ready, diff_ready, exp_ready, mul_ready = (sem("stage_ready"), sem("diff_ready"), sem("exp_ready"),
                                                         sem("mul_ready"))
        vt_done, kht_done, level_done = sem("vt_done"), sem("kht_done"), sem("level_done")
        vt_ready, kht_ready, att_ready = sem("vt_ready"), sem("kht_ready"), sem("att_ready")
        o_done, o_read, sup_done, s_ready = sem("o_done"), sem("o_read"), sem("sup_done"), sem("s_ready")
        s0_landed, ktm_ready, s0_ready = sem("s0_landed"), sem("ktm_ready"), sem("s0_ready")
        osq_ready, gms_done, gstd_ready = sem("osq_ready"), sem("gms_done"), sem("gstd_ready")
        hidden_hi, hidden_split = sem("hidden_hi"), sem("hidden_split")
        y_ready, y_stored, out_stored = sem("y_ready"), sem("y_stored"), sem("out_stored")

        def tile(arena, at, k):
            return arena.at(at + k * N, 0, N) if isinstance(k, int) else arena.at(at, k * N, N)

        def ft(at, k=0):
            return tile(fa, at, k)

        def rt(at, k=0):
            return tile(ra, at, k)

        def hf(at, k=0):
            return tile(ra, at, k).bitcast(F32)

        def fv(at, n):
            return fa[:, at:at + n]

        def cols(tile):
            return [tile[:, 0:352], tile[:, 352:N].rearrange("p (b n) -> p b n", b=2)]

        def psum_cols(s):
            return [ps[:, 3 * s, 0:352], ps[:, 3 * s + 1:3 * s + 3, 0:344]]

        def set_count(half, s, stage, n):
            return half * SET_TOTAL[s] + SET_BASE[stage][s] + n

        def full_count(half, n):
            before_z5 = isinstance(n, int) and n <= SP_Z5
            return half * (SP_ALL - KT_S) + n - (0 if before_z5 else KT_S)

        def small(name, n=1):
            k = SMALL.index(name)
            return sml[:, k:k + n, :] if n > 1 else sml[:, k, :]

        def rows_of(h):
            return slice(64 * (h % 2), 64 * (h % 2) + 64), h // 2, 2 * (h % 2) + h // 2

        consts = [(vec[:, :], vec_d), (ident[:, :], ident_d), (fv(A_Z, NL * 256 + 512), masks_d),
                  (fa[0:DT, A_Z + 4096:A_Z + 4096 + dmask.shape[1]], dmask_d),
                  (wgu[:, :], wgu_d), (dcol[:, :], dcol_d)]
        block = ctx.enter_context(nc.Block())

        @block.sync
        def _(sp):
            def load(s, it):
                block = wpack[it * RING + s] if isinstance(it, int) else wpack[bass.ds(it * RING + s, 1)].rearrange(
                    "o p n -> p (o n)")
                sp.dma_start(w_raw[:, s, :], block).then_inc(w_landed[s], 16)

            for s in range(RING):
                load(s, 0)
            for half in range(HALVES):
                with sp.Fori(0 if half else 1, ITERS) as it:
                    for s in range(RING):
                        sp.wait_ge(w_split[s], half * ITERS + it)
                        load(s, it)

        @block.gpsimd
        def _(pool):
            pool.memset(zero[:, :], 0.0)
            pool.drain()

            def split(s, n):
                pool.wait_ge(w_landed[s], (n + 1) * 16)
                if not isinstance(n, int):
                    pool.wait_ge(w_used[s], n)
                pool.tensor_tensor(w_hi[:, s, :], w_raw[:, s, :], zero[:, :].to_broadcast([P, WB]), ALU.subtract)
                pool.drain()
                pool.tensor_tensor(w_lo[:, s, :], w_raw[:, s, :], w_hi[:, s, :].bitcast(F32),
                                   ALU.subtract).then_inc(w_split[s], 1)

            for s in range(RING):
                split(s, 0)
            with pool.Fori(1, HALVES * ITERS) as n:
                for s in range(RING):
                    split(s, n)

        @block.tensor
        def _(pe):
            def set_free(half, s, stage, n):
                pe.wait_ge(set_read[s], set_count(half, s, stage, n))

            def tiles_of(s, k, total, wh, wl, hi, lo):
                for b, (c0, cn) in enumerate(BLK):
                    out = ps[:, 3 * s + b, 0:cn]
                    h, l = hi(k)[:, c0:c0 + cn], lo(k)[:, c0:c0 + cn]
                    pe.matmul(out, wh, h, start=(k == 0), stop=False)
                    pe.matmul(out, wh, l, start=False, stop=False)
                    last = pe.matmul(out, wl, h, start=False, stop=(k == total - 1))
                return last

            def product(s, blocks, hi, lo):
                for n, (place, it) in enumerate(blocks):
                    pe.wait_ge(w_split[place], it + 1)
                    for q in range(4):
                        last = tiles_of(s, 4 * n + q, 4 * len(blocks), w_hi[:, place, q * P:(q + 1) * P],
                                        w_lo[:, place, q * P:(q + 1) * P], hi, lo)
                    last.then_inc(w_used[place], 1)

            def row_sums(half, stage, n):
                set_free(half, 0, stage, 0)
                pe.wait_ge(ssum_ready, half * 3 + n + 1)
                for b, (c0, cn) in enumerate(BLK):
                    last = pe.matmul(ps[:, b, 0:cn], ones[:, :], fv(A_O + c0, cn), start=True, stop=True)
                last.then_inc(ms_done, 1)

            def tile_pair(half, stage, n, it, hi, lo):
                for s in range(2):
                    set_free(half, s, stage, n)
                    product(s, [(2 * s, it), (2 * s + 1, it)], hi, lo)

            def s5_setup():
                pe.wait_ge(g_ready, 1)
                g_re = fv(A_M, 3840).rearrange("p (t s) -> p t s", t=PAIRS)
                g_im = fv(A_M + 3840, 3840).rearrange("p (t s) -> p t s", t=PAIRS)
                c_re = fv(A_G, 512).rearrange("p (t c) -> p t c", t=PAIRS)
                c_im = fv(A_G + 512, 512).rearrange("p (t c) -> p t c", t=PAIRS)
                set_free(0, 0, "low", 0)
                set_free(0, 1, "low", 0)
                for t in range(PAIRS):
                    if t >= 2:
                        pe.wait_ge(p_ready, t - 1)
                        pe.wait_ge(t_ready, t - 1)
                    for j in range(J):
                        out = ps[:, t % 2, 32 * j:32 * j + 32]
                        w0 = S5_GROUP * (J - 1 - j)
                        pe.matmul(out, g_re[:, t, w0:w0 + P], c_re[:, t, :], start=True, stop=False)
                        pe.matmul(out, g_im[:, t, w0:w0 + P], c_im[:, t, :], start=False, stop=True)
                    pe.transpose(ps[:, 4 + t % 2, 0:128], g_re[:, t, 0:P], ident[:, :])
                    pe.transpose(ps[:, 4 + t % 2, 128:256], g_im[:, t, 0:P], ident[:, :]).then_inc(tp_done, 1)
                pe.wait_ge(p_ready, PAIRS)
                pe.wait_ge(t_ready, PAIRS)

            def s5_in(half, t):
                r = t % CR
                pe.wait_ge(c_landed[r], (half * (PAIRS // CR) + t // CR + 1) * 16)
                pe.wait_ge(chunk_in_read, half * PAIRS + max(t - 1, 0))
                for g in range(2):
                    for q, c0 in ((0, C_PR), (1, C_PI)):
                        last = pe.matmul(ps[64 * g:64 * g + 64, 6 + t % 2, q * UC:(q + 1) * UC],
                                         fv(C_SLOT[r] + c0 + 64 * g, 64), fv(M_U + (t * 2 + g) * UC, UC),
                                         start=True, stop=True)
                last.then_inc(chunk_in_done, 1)

            def s5_rows(half, t):
                pe.wait_ge(state_ready, half * PAIRS + t + 1)
                pe.wait_ge(yrow_read, half * PAIRS + max(t - 1, 0))
                at, st = C_SLOT[t % CR], M_TMP + 800 + (t % 2) * 2 * YC
                for g in range(2):
                    out, rows = ps[:, 2 * (t % 2) + g, 0:YC], slice(64 * g, 64 * g + 64)
                    pe.matmul(out, fv(at + C_T + P * g, P), fv(M_U + (t * 2 + g) * UC, YC), start=True, stop=False)
                    pe.matmul(out, fa[rows, at + C_QR:at + C_QR + P], fa[rows, st:st + YC], start=False, stop=False)
                    last = pe.matmul(out, fa[rows, at + C_QI:at + C_QI + P], fa[rows, st + YC:st + 2 * YC],
                                     start=False, stop=True)
                last.then_inc(yrow_done, 1)

            def s5(half):
                set_free(half, 0, "glu", 0)
                set_free(half, 1, "glu", 0)
                pe.wait_ge(u_landed, (half + 1) * 16 * J)
                s5_in(half, 0)
                s5_in(half, 1)
                for t in range(PAIRS):
                    s5_rows(half, t)
                    if t + 2 < PAIRS:
                        s5_in(half, t + 2)
                pe.wait_ge(yrow_read, (half + 1) * PAIRS)

            def merge_products(half, it0, stage, split_count):
                with pe.Fori(0, 2) as i:
                    for q in range(4):
                        b = [((3 * q + x) % RING, half * ITERS + it0 + i * 3 + (3 * q + x) // RING) for x in range(3)]
                        set_free(half, 0, stage, i * 4 + q)
                        product(0, b[0:2], lambda k: rt(A_H, k), lambda k: rt(A_H, 8 + k))
                        pe.wait_ge(split_ready, half * SP_ALL + split_count)
                        set_free(half, 1, stage, i * 4 + q)
                        product(1, b[2:3], lambda k: rt(A_O, k), lambda k: rt(A_O, 4 + k))

            def gla(half, c, par):
                dec = isinstance(c, int) and c == CHUNKS
                L = DT if dec else C
                n = half * (CHUNKS + 1) + c
                de = O_DE[par]
                pe.wait_ge(stage_ready, n + 1)
                pe.wait_ge(vt_ready, n)
                pe.wait_ge(att_ready, n)
                for h in range(HEADS):
                    o = ps[0:L, 2 + 3 * (h % 2), 256 + (h // 2) * DV:256 + (h // 2 + 1) * DV]
                    pe.transpose(o, fv(O_ST + 4 * L + h * L, L), ident[:, :])
                for h in (0, 2, 1, 3):
                    rows, t, _ = rows_of(h)
                    last = pe.matmul(ps[0:L, 2 + 3 * (h % 2), t * L:t * L + L],
                                     fa[rows, O_ST + 2 * L + t * L:O_ST + 3 * L + t * L],
                                     fa[rows, O_ST + t * L:O_ST + t * L + L], start=True, stop=True)
                last.then_inc(vt_done, 1)
                pe.wait_ge(mul_ready, n + 1)
                pe.wait_ge(kht_ready, n)
                for t in range(2):
                    last = pe.transpose(ps[0:L, 7, 256 + t * P:384 + t * P], fv(de + DE_K + t * L, L), ident[:, :])
                last.then_inc(kht_done, 1)
                pe.wait_ge(vt_ready, n + 1)
                for l in (DEC_LEVELS if dec else range(NL)):
                    for h in (0, 2, 1, 3):
                        rows, t, _ = rows_of(h)
                        col = l * 128 + t * (L // 2)
                        kk, qq = O_KT + l * 256 + t * L, de + DE_R + l * 128 + t * (L // 2)
                        last = pe.matmul(ps[0:L, 3 * (h % 2) + col // 512, col % 512:col % 512 + L // 2],
                                         fa[rows, kk:kk + L], fa[rows, qq:qq + L // 2], start=True, stop=True)
                last.then_inc(level_done, 1)
                pe.wait_ge(att_ready, n + 1)
                pe.wait_ge(o_read, n)
                pe.wait_ge(kht_ready, n + 1)
                if dec:
                    pe.wait_ge(s0_landed, (half + 1) * 16)
                else:
                    pe.wait_ge(s_ready, half * CHUNKS + c + 1)
                for h in range(HEADS):
                    rows, t, slot = rows_of(h)
                    o, qq = ps[:, 6 + h % 2, t * L:(t + 1) * L], de + DE_Q + t * L
                    vr, att = vT[0:L, slot * DV:(slot + 1) * DV], fa[0:L, O_ATT + slot * L:O_ATT + (slot + 1) * L]
                    if dec:
                        last = pe.matmul(o, vr, att, start=True, stop=False, skip_group_check=True)
                        for s in range(DS):
                            s0, a = O_S0 + (s * 2 + t) * DV, s * DEC_SEQ
                            last = pe.matmul(ps[:, 6 + h % 2, t * L + a:t * L + a + DEC_SEQ], fa[rows, s0:s0 + DV],
                                             fa[rows, qq + a:qq + a + DEC_SEQ], start=False, stop=(s == DS - 1),
                                             skip_group_check=True)
                    else:
                        pe.matmul(o, gla_s[rows, t, :], fa[rows, qq:qq + L], start=True, stop=False)
                        last = pe.matmul(o, vr, att, start=False, stop=True)
                last.then_inc(o_done, 1)
                pe.wait_ge(o_read, n + 1)
                if dec:
                    pe.wait_ge(ktm_ready, half + 1)
                for s in range(DS if dec else 1):
                    for h in range(HEADS):
                        _, t, slot = rows_of(h)
                        kk = t * P + (h % 2) * 64
                        keys = fa[0:L, O_KT + s * 256 + kk:O_KT + s * 256 + kk + 64] if dec else khT[0:L, kk:kk + 64]
                        bank, col = ((s * 2 + t) * DV // 512, (s * 2 + t) * DV % 512) if dec else (6, 256 + t * DV)
                        last = pe.matmul(ps[64 * (h % 2):64 * (h % 2) + 64, bank, col:col + DV],
                                         keys, vT[0:L, slot * DV:(slot + 1) * DV], start=True, stop=True)
                last.then_inc(sup_done, 1)

            def ff_up(half, g):
                for q in range(2):
                    tile_pair(half, "ff", ff_set(g, "up") + q, half * ITERS + IT_FF + ff_it(g, "up") + q,
                              lambda k: rt(A_Z, k), lambda k: rt(A_M, k))

            def ff_down(half, g, par):
                pe.wait_ge(hidden_split, half * FF_GROUPS * 4 + 4 * g + 4)
                hb = A_H + 8 * N if par == 0 else A_O
                for q in range(2):
                    for s in range(RING):
                        set_free(half, s % 2, "ff", ff_set(g, "down") + 2 * q + s // 2)
                        product(s % 2, [(s, half * ITERS + IT_FF + ff_it(g, "down") + q)],
                                lambda k: rt(hb, k), lambda k: rt(hb, 4 + k))

            def gate_products(half):
                pe.wait_ge(low_ready, half + 1)
                for t in range(2):
                    s = 1 - t
                    set_free(half, s, "low", 0)
                    for b, (c0, cn) in enumerate(BLK):
                        last = pe.matmul(ps[:, 3 * s + b, 0:cn], wgu[:, t * P:(t + 1) * P],
                                         fa[0:RANK, O_A + c0:O_A + c0 + cn], start=True, stop=True)
                    last.then_inc(gpre_done, 1)

            pe.wait_ge(ones_ready, 1)
            pe.wait_ge(const_landed, 16 * len(consts))
            for half in range(HALVES):
                x_hi, x_lo = (lambda k: rt(A_H, k)), (lambda k: rt(A_H, 8 + k))
                row_sums(half, "nx", 0)
                pe.wait_ge(split_ready, half * SP_ALL + SP_X + KT_D)
                tile_pair(half, "a", 0, half * ITERS + IT_A, x_hi, x_lo)
                with pe.Fori(1, 6) as i:
                    tile_pair(half, "a", i, half * ITERS + IT_A + i, x_hi, x_lo)
                set_free(half, 0, "low", 0)
                pe.wait_ge(wa_split, half + 1)
                for k in range(KT_D):
                    last = tiles_of(0, k, KT_D, ra[:, O_AH + k * P:O_AH + (k + 1) * P],
                                    ra[:, O_AL + k * P:O_AL + (k + 1) * P], x_hi, x_lo)
                last.then_inc(low_done, 1)
                if half == 0:
                    pe.wait_ge(low_ready, 1)
                    s5_setup()
                gate_products(half)
                s5(half)
                pe.wait_ge(split_ready, half * SP_ALL + SP_Z5 + KT_S)
                for s in range(RING):
                    set_free(half, s % 2, "glu", s // 2)
                    product(s % 2, [(s, half * ITERS + IT_GLU)], lambda k: rt(A_O, k), lambda k: rt(A_O, 4 + k))
                merge_products(half, IT_M1, "m1", SP_O5 + KT_S)
                set_free(half, 0, "r", 0)
                set_free(half, 1, "r", 0)
                for par in range(2):
                    gla(half, par, par)
                with pe.Fori(1, CHUNKS // 2 - 1) as i:
                    for par in range(2):
                        gla(half, i * 2 + par, par)
                for c in range(CHUNKS - 2, CHUNKS + 1):
                    gla(half, c, c % 2)
                pe.wait_ge(o_read, (half + 1) * (CHUNKS + 1))
                pe.wait_ge(s0_ready, half + 1)
                for h in range(HEADS):
                    set_free(half, 0, "r", h)
                    b, it = 2 * (h % 2), half * ITERS + IT_R + h // 2
                    product(0, [(b, it), (b + 1, it)], x_hi, x_lo)
                    set_free(half, 1, "r", h)
                    pe.wait_ge(osq_ready, half * HEADS + h + 1)
                    for b, (c0, cn) in enumerate(BLK):
                        last = pe.matmul(ps[:, 3 + b, 0:cn], ones[:, :], ft(A_O, h)[:, c0:c0 + cn],
                                         start=True, stop=True)
                    last.then_inc(gms_done, 1)
                merge_products(half, IT_M2, "m2", SP_OG + HEADS)
                pe.wait_ge(split_ready, half * SP_ALL + SP_MG + KT_D)
                with pe.Fori(0, 4) as i:
                    tile_pair(half, "out", i, half * ITERS + IT_OUT + i, lambda k: rt(A_Z, k), lambda k: rt(A_M, k))
                row_sums(half, "nf", 1)
                pe.wait_ge(split_ready, half * SP_ALL + SP_H2 + KT_D)
                ff_up(half, 0)
                ff_up(half, 1)
                with pe.Fori(0, FF_GROUPS // 2 - 1) as i:
                    for par in range(2):
                        ff_down(half, i * 2 + par, par)
                        ff_up(half, i * 2 + par + 2)
                ff_down(half, FF_GROUPS - 2, 0)
                ff_down(half, FF_GROUPS - 1, 1)
                row_sums(half, "ny", 2)

        @block.scalar
        def _(act):
            def evac(s, dst, func=ACT.Copy, **kw):
                for src, d in zip(psum_cols(s), cols(dst)):
                    last = act.activation(d, src, func, **kw)
                return last

            def block_used(half, place, it):
                act.wait_ge(w_used[place], half * ITERS + it + 1)

            def norm(half, n, stage, src, src_ready):
                for k in range(KT_D):
                    src_ready(k)
                    act.activation(ft(A_O, k), ft(src, k), ACT.Square).then_inc(sq_ready, 1)
                act.wait_ge(set_read[0], set_count(half, 0, stage, 1))
                act.activation(ft(A_G), ft(A_G), ACT.Sqrt).then_inc(std_ready, 1)

            def high_parts(half, first, count, src, dst):
                for k in range(count):
                    act.wait_ge(full_ready, full_count(half, first + k + 1))
                    act.activation(rt(dst, k), ft(src, k), ACT.Copy).then_inc(hi_ready, 1)

            def project(half):
                if half:
                    block_used(half - 1, 3, ITERS - 1)
                    act.wait_ge(ms_done, 3 * half)
                act.dma_start(fv(A_M, 8 * N), xT[half]).then_inc(x_landed, 16)
                act.wait_ge(x_landed, (half + 1) * 16)
                norm(half, 0, "nx", A_M, lambda k: None)
                if half:
                    act.wait_ge(y_stored, half * 16 * KT_D)
                high_parts(half, SP_X, KT_D, A_M, A_H)
                act.dma_start(fv(O_A, KT_D * P), wa).then_inc(wa_landed, 16)
                if half == 0:
                    act.wait_ge(split_ready, SP_X + KT_D)
                    act.dma_start(fv(A_G, 512), b_d).then_inc(bc_landed, 16)
                    act.dma_start(fv(A_G + 512, 512), c_d).then_inc(bc_landed, 16)
                up = fv(O_UP, KT_S * J * UC).rearrange("p (m j c) -> p m j c", m=KT_S, j=J)
                for m in range(KT_S):
                    s = m % 2
                    block_used(half, 2 * s + 1, IT_A + m // 2)
                    for b, (c0, cn) in enumerate(BLK):
                        pn = min(cn, TP - c0)
                        act.activation(up[:, m, :, c0 // J:(c0 + pn) // J],
                                       ps[:, 3 * s + b, 0:pn].rearrange("p (c j) -> p j c", j=J), ACT.Copy)
                    dec = ps[:, 3 * s + 2, TP - BLK[2][0]:N - BLK[2][0]].rearrange("p (q j) -> p j q", j=DEC_SEQ)
                    act.activation(up[:, m, 0:DEC_SEQ, NC:NC + DS], dec, ACT.Copy)
                    act.activation(up[:, m, DEC_SEQ:J, NC + DS:UC], dec, ACT.Copy).then_inc(set_read[s], 1)
                act.wait_ge(u_pad, 2 * (half + 1))
                act.wait_ge(set_read[0], set_count(half, 0, "a", 2))
                act.wait_ge(set_read[1], set_count(half, 1, "a", 2))
                act.dma_start(u_dram.rearrange("m p j c -> p m (j c)"),
                              fv(O_UP, KT_S * J * UC).rearrange("p (m n) -> p m n", m=KT_S)).then_inc(u_stored, 16)
                for m in range(KT_S, 12):
                    s = m % 2
                    block_used(half, 2 * s + 1, IT_A + m // 2)
                    evac(s, ft(A_Z, m - KT_S), scale=DK ** -0.5 if m < KT_S + 2 else 1.0).then_inc(set_read[s], 1)
                act.wait_ge(low_done, half + 1)
                for src, d in zip([ps[0:RANK, 0, 0:352], ps[0:RANK, 1:3, 0:344]],
                                  cols(fa[0:RANK, O_A:O_A + N])):
                    last = act.activation(d, src, ACT.Copy)
                last.then_inc(low_ready, 1)

            def log_gates(half):
                for t in range(2):
                    act.wait_ge(gpre_done, half * 2 + t + 1)
                    evac(1 - t, ft(A_G, t), ACT.Identity, bias=vec[:, V_BG + t:V_BG + t + 1]
                         ).then_inc(set_read[1 - t], 1)
                    act.wait_ge(gmin_ready, half * 2 + t)
                    act.drain()
                    act.activation(ft(O_T), ft(A_G, t), ACT.Abs)
                    act.drain()
                    act.activation(ft(O_T), ft(O_T), ACT.Exp, scale=-1.0)
                    act.drain()
                    act.activation(ft(O_T), ft(O_T), ACT.Ln, bias=1.0).then_inc(gln_ready, 1)

            def s5_tables_out():
                act.wait_ge(qe_ready, 1)
                by_pair = c_dram.rearrange("t p c -> p t c")
                act.dma_start(by_pair[:, :, C_QR:C_QR + 2 * P],
                              fv(A_M, 4096).rearrange("p (t c) -> p t c", t=PAIRS)).then_inc(qe_stored, 16)
                act.dma_start(by_pair[:, :, C_EC:C_EC + 2 * EC],
                              fv(A_M + 4096, PAIRS * 2 * EC).rearrange("p (t c) -> p t c", t=PAIRS)).then_inc(qe_stored, 16)
                act.dma_start(fv(A_G, 1024), cbd_d).then_inc(cbd_landed, 16)

            def s5_pairs_out():
                for t in range(PAIRS):
                    act.wait_ge(tp_done, t + 1)
                    stg = O_STG + 512 * (t % 2)
                    act.wait_ge(tp_stored[t % 2], 16 * (t // 2))
                    act.activation(fv(stg + 256, 256), ps[:, 4 + t % 2, 0:256], ACT.Copy).then_inc(p_ready, 1)
                    act.wait_ge(p_ready, t + 1)
                    act.wait_ge(t_ready, t + 1)
                    act.dma_start(c_dram[t, :, 0:512], fv(stg, 512)).then_inc(tp_stored[t % 2], 16)
                for q in range(2):
                    act.wait_ge(tp_stored[q], 16 * (PAIRS // 2))

            def s5(half):
                def load_consts(t, r):
                    src = c_dram[t] if isinstance(t, int) else c_dram[bass.ds(t, 1)].rearrange("o p c -> p (o c)")
                    act.dma_start(fv(C_SLOT[r], C_W), src).then_inc(c_landed[r], 16)

                act.wait_ge(u_stored, (half + 1) * 16)
                act.wait_ge(split_ready, half * SP_ALL + SP_X + KT_D)
                for j in range(J):
                    act.dma_start(fa[j * 16:(j + 1) * 16, M_U:M_U + S5_GROUPS * UC].rearrange("p (g c) -> p g c", c=UC),
                                  u_dram.rearrange("m (g h) j c -> j h (m g) c", h=S5_GROUP)[j]).then_inc(u_landed, 16)
                act.dma_start(s5_dec[:, :, :, :], s5dec_d[half]).then_inc(s5dec_landed, 16)
                act.wait_ge(b_ready, half + 1)
                for r in range(CR):
                    load_consts(r, r)

                def rows(i, r):
                    t = i * CR + r
                    act.wait_ge(yrow_done, half * PAIRS + t + 1)
                    act.activation(fa.at(O_UP, t * 2 * YC, 2 * YC).rearrange("p (g c) -> p g c", g=2),
                                   ps[:, 2 * (r % 2):2 * (r % 2) + 2, 0:YC], ACT.Copy).then_inc(yrow_read, 1)

                with act.Fori(0, PAIRS // CR - 1) as i:
                    for r in range(CR):
                        rows(i, r)
                        load_consts(i * CR + CR + r, r)
                for r in range(CR):
                    rows(PAIRS // CR - 1, r)
                act.wait_ge(yrow_read, (half + 1) * PAIRS)
                for j in range(J):
                    act.dma_start(y_dram.rearrange("m (g h) j c -> j h (m g) c", h=S5_GROUP)[j],
                                  fa[j * 16:(j + 1) * 16, O_UP:O_UP + S5_GROUPS * YC].rearrange("p (g c) -> p g c", c=YC)
                                  ).then_inc(yrow_stored, 16)
                act.wait_ge(yrow_stored, (half + 1) * 16 * J)
                act.dma_start(fv(O_UP, KT_S * J * YC).rearrange("p (m n) -> p m n", m=KT_S),
                              y_dram.rearrange("m p j c -> p m (j c)")).then_inc(yperm_landed, 16)
                act.wait_ge(s5dec_ready, half + 1)
                act.dma_start(s5_dec_out[half], s5_new[:, :, :, :]).then_inc(out_stored, 16)
                act.wait_ge(yperm_landed, (half + 1) * 16)
                yp = fv(O_UP, KT_S * J * YC).rearrange("p (m j c) -> p m j c", m=KT_S, j=J)
                for m in range(KT_S):
                    z = ft(A_M, m)
                    act.activation(z[:, 0:TP].rearrange("p (c j) -> p c j", j=J),
                                   yp[:, m, :, 0:NC].rearrange("p j c -> p c j"), ACT.Gelu_apprx_tanh)
                    act.activation(z[:, TP:N].rearrange("p (q j) -> p q j", j=DEC_SEQ),
                                   yp[:, m, 0:DEC_SEQ, NC:YC].rearrange("p j c -> p c j"),
                                   ACT.Gelu_apprx_tanh).then_inc(gelu_ready, 1)
                act.wait_ge(gelu_ready, (half + 1) * KT_S)
                for m in range(KT_S):
                    act.activation(rt(A_O, m), ft(A_M, m), ACT.Copy).then_inc(hi_ready, 1)
                for m in range(KT_S):
                    block_used(half, m, IT_GLU)
                    evac(m % 2, ft(A_M, 4 + m), ACT.Sigmoid).then_inc(set_read[m % 2], 1)
                high_parts(half, SP_O5, KT_S, A_M, A_O)
                act.wait_ge(split_ready, half * SP_ALL + SP_O5 + KT_S)
                with act.Fori(0, 2) as i:
                    for q in range(4):
                        block_used(half, (3 * q + 1) % RING, IT_M1 + i * 3 + (3 * q + 1) // RING)
                        evac(0, ft(A_M, i * 4 + q), ACT.Sigmoid).then_inc(set_read[0], 1)

            def gla_all(half):
                def stage(c, L):
                    src = fa[:, A_Z:A_Z + 8 * N].rearrange("p (k n) -> p k n", k=8)[:, :, bass.ds(c * C, L)]
                    act.activation(fv(O_ST, 8 * L).rearrange("p (k n) -> p k n", k=8), src, ACT.Copy
                                   ).then_inc(stage_ready, 1)

                def exps(n, par, dec):
                    act.wait_ge(diff_ready, n + 1)
                    de = O_DE[par]
                    spans = [(0, DE_W)]
                    if dec:
                        spans = [(a + l * 128, DT) for a in (DE_R, DE_L) for l in DEC_LEVELS] + [(DE_K, 2 * DT), (DE_Q, 2 * DT)]
                    for at, w in spans:
                        last = act.activation(fv(de + at, w), fv(de + at, w), ACT.Exp)
                    last.then_inc(exp_ready, 1)

                def chunk(c, par):
                    dec = isinstance(c, int) and c == CHUNKS
                    L = DT if dec else C
                    n = half * (CHUNKS + 1) + c
                    act.wait_ge(vt_done, n + 1)
                    act.wait_ge(sup_done, n)
                    act.activation(vT[0:L, :].rearrange("p (a n) -> p a n", a=2), ps[0:L, 2:6:3, 256:512], ACT.Copy
                                   ).then_inc(vt_ready, 1)
                    act.wait_ge(kht_done, n + 1)
                    act.activation(khT[0:L, :], ps[0:L, 7, 256:512], ACT.Copy).then_inc(kht_ready, 1)
                    if not dec:
                        last = isinstance(c, int) and c == CHUNKS - 1
                        act.wait_ge(mul_ready, n + 1)
                        stage(c + 1, DT if last else C)
                        exps(n + 1, 1 - par, last)
                    act.wait_ge(o_done, n + 1)
                    v_cols = fa[:, A_Z + 4 * N:A_Z + 8 * N].rearrange("p (k n) -> p k n", k=4)[:, :, bass.ds(c * C, L)]
                    act.activation(v_cols.rearrange("p (t a) n -> p a t n", a=2),
                                   ps[:, 6:8, 0:2 * L].rearrange("p a (t n) -> p a t n", t=2), ACT.Copy
                                   ).then_inc(o_read, 1)

                block_used(half, 3, IT_M1 + 5)
                stage(0, C)
                exps(half * (CHUNKS + 1), 0, False)
                for par in range(2):
                    chunk(par, par)
                with act.Fori(1, CHUNKS // 2 - 1) as i:
                    for par in range(2):
                        chunk(i * 2 + par, par)
                chunk(CHUNKS - 2, 0)
                chunk(CHUNKS - 1, 1)
                act.dma_start(fv(O_S0, DS * 2 * DV), gladec_d[half]).then_inc(s0_landed, 16)
                chunk(CHUNKS, 0)
                act.wait_ge(s0_ready, half + 1)
                act.dma_start(gla_dec_out[half], fv(O_S0, DS * 2 * DV)).then_inc(out_stored, 16)
                act.wait_ge(out_stored, (half + 1) * 32)
                act.wait_ge(o_read, (half + 1) * (CHUNKS + 1))
                for h in range(HEADS):
                    act.activation(ft(A_O, h), ft(A_Z, 4 + h), ACT.Square).then_inc(osq_ready, 1)
                for h in range(HEADS):
                    block_used(half, 2 * (h % 2) + 1, IT_R + h // 2)
                    if h:
                        act.wait_ge(full_ready, full_count(half, SP_OG + h))
                    evac(0, ft(A_G, 0), ACT.Silu).then_inc(set_read[0], 1)
                    act.wait_ge(set_read[1], set_count(half, 1, "r", h + 1))
                    act.activation(ft(A_G, 1), ft(A_G, 1), ACT.Sqrt).then_inc(gstd_ready, 1)
                    act.wait_ge(full_ready, full_count(half, SP_OG + h + 1))
                    act.activation(rt(A_O, h), ft(A_Z, 4 + h), ACT.Copy).then_inc(hi_ready, 1)
                act.wait_ge(split_ready, half * SP_ALL + SP_OG + HEADS)
                with act.Fori(0, 2) as i:
                    for q in range(4):
                        block_used(half, (3 * q + 1) % RING, IT_M2 + i * 3 + (3 * q + 1) // RING)
                        evac(0, ft(A_G, q % 2), ACT.Sigmoid).then_inc(set_read[0], 1)
                        act.wait_ge(full_ready, full_count(half, SP_MG + i * 4 + q + 1))
                        act.activation(rt(A_Z, i * 4 + q), ft(A_M, i * 4 + q), ACT.Copy).then_inc(hi_ready, 1)

            def out_and_ff(half):
                block_used(half, 3, IT_M2 + 5)
                act.dma_start(fv(A_H, 8 * N), xT[half]).then_inc(res_landed, 16)
                norm(half, 1, "nf", A_H,
                     lambda k: act.wait_ge(set_read[k % 2], set_count(half, k % 2, "out", k // 2 + 1)))
                high_parts(half, SP_H2, KT_D, A_M, A_Z)

                def hidden(g, par):
                    for q in range(4):
                        block_used(half, 2 * (q % 2) + 1, IT_FF + ff_it(g, "up") + q // 2)
                        before = max(4 * g + q - 1, 0) if isinstance(g, int) else 4 * g + q - 1
                        act.wait_ge(hidden_split, half * FF_GROUPS * 4 + before)
                        evac(q % 2, ft(A_G, q % 2), ACT.Relu).then_inc(set_read[q % 2], 1)
                        act.drain()
                        act.activation(rt(A_H + 8 * N if par == 0 else A_O, q), ft(A_G, q % 2), ACT.Square
                                       ).then_inc(hidden_hi, 1)

                act.wait_ge(split_ready, (half + 1) * SP_ALL)
                hidden(0, 0)
                hidden(1, 1)
                with act.Fori(0, FF_GROUPS // 2 - 1) as i:
                    for par in range(2):
                        hidden(i * 2 + par + 2, par)

                def x2_there(k):
                    if k == 0:
                        act.wait_ge(set_read[0], set_count(half, 0, "ny", 0))
                        act.wait_ge(set_read[1], set_count(half, 1, "ny", 0))
                norm(half, 2, "ny", A_H, x2_there)
                for k in range(KT_D):
                    act.wait_ge(y_ready, half * KT_D + k + 1)
                    act.dma_start(yT[half, :, k * N:(k + 1) * N], ft(A_H, k)).then_inc(y_stored, 16)

            for dst, src in consts:
                act.dma_start(dst, src).then_inc(const_landed, 16)
            act.dma_start(sml[:, 0:3, :], s5small).then_inc(s5in_landed, 16)
            act.wait_ge(s5in_landed, 16)
            act.activation(small("dt"), small("logdt"), ACT.Exp).then_inc(dt_ready, 1)
            act.wait_ge(const_landed, 16 * len(consts))
            act.wait_ge(trig_in, 1)
            act.activation(small("mag"), small("lrdt"), ACT.Exp)
            act.activation(small("sin"), small("ang"), ACT.Sin)
            act.activation(small("sinh"), small("ang"), ACT.Sin, scale=0.5).then_inc(trig_out, 1)
            for half in range(HALVES):
                project(half)
                if half == 0:
                    s5_tables_out()
                    s5_pairs_out()
                log_gates(half)
                s5(half)
                gla_all(half)
                out_and_ff(half)
            act.dma_start(s5_prompt, s5_carry[:, :, :]).then_inc(out_stored, 16)
            act.dma_start(gla_prompt, gla_s[:, :, :]).then_inc(out_stored, 16)
            act.wait_ge(out_stored, 16 * (2 * HALVES + 2))
            act.wait_ge(y_stored, 16 * HALVES * KT_D)

        @block.vector
        def _(dve):
            def tt(out, a, b, op):
                return dve.tensor_tensor(out, a, b, op)

            def block_used(half, place, it):
                dve.wait_ge(w_used[place], half * ITERS + it + 1)

            def low_part(half, n, full, hi, lo):
                dve.wait_ge(hi_ready, half * SP_ALL + n + 1)
                tt(lo, full, hi, ALU.subtract).then_inc(split_ready, 1)

            def mean_square(s, dst, width):
                for src, d in zip(psum_cols(s), cols(dst)):
                    last = dve.tensor_scalar(d, src, 1.0 / width, EPS, ALU.mult, ALU.add)
                last.then_inc(set_read[s], 1)

            def norm(half, n, src, full, gain, each):
                for k in range(KT_D):
                    dve.wait_ge(sq_ready, (half * 3 + n) * KT_D + k + 1)
                    if k:
                        dve.drain()
                        last = tt(ft(A_O), ft(A_O), ft(A_O, k), ALU.add)
                last.then_inc(ssum_ready, 1)
                dve.wait_ge(ms_done, half * 3 + n + 1)
                mean_square(0, ft(A_G), D_MODEL)
                dve.wait_ge(std_ready, half * 3 + n + 1)
                dve.reciprocal(ft(A_G), ft(A_G))
                dve.drain()
                for k in range(KT_D):
                    last = dve.scalar_tensor_tensor(ft(full, k), ft(src, k), vec[:, gain + k:gain + k + 1], ft(A_G),
                                                    ALU.mult, ALU.mult)
                    last.then_inc(full_ready if n < 2 else y_ready, 1)
                    if k:
                        each(k - 1)
                each(KT_D - 1)

            def trig():
                s = small
                dve.wait_ge(dt_ready, 1)
                steps = [
                    lambda: dve.tensor_scalar(s("lr"), s("lam_re"), -1e-4, None, ALU.min),
                    lambda: tt(s("lrdt"), s("lr"), s("dt"), ALU.mult),
                    lambda: tt(s("th"), s("lam_im"), s("dt"), ALU.mult),
                    lambda: dve.tensor_scalar(s("t0"), s("th"), float(0.5 / np.pi), MAGIC, ALU.mult, ALU.add),
                    lambda: dve.tensor_scalar(s("t0"), s("t0"), MAGIC, None, ALU.subtract),
                    lambda: dve.scalar_tensor_tensor(s("th"), s("t0"), -PI2_1, s("th"), ALU.mult, ALU.add),
                    lambda: dve.scalar_tensor_tensor(s("th"), s("t0"), -PI2_2, s("th"), ALU.mult, ALU.add),
                    lambda: dve.scalar_tensor_tensor(s("th"), s("t0"), -PI2_3, s("th"), ALU.mult, ALU.add),
                ]
                for f in steps:
                    f()
                    dve.drain()
                dve.tensor_scalar(s("ang"), s("th"), 3.1415925, -3.1415925, ALU.min, ALU.max).then_inc(trig_in, 1)
                dve.wait_ge(trig_out, 1)

                def seq(*ops):
                    for out, a, b, op in ops:
                        tt(out, a, b, op)
                        dve.drain()
                seq((s("t0"), s("sinh"), s("sinh"), ALU.mult))
                dve.tensor_scalar(s("cos"), s("t0"), -2.0, 1.0, ALU.mult, ALU.add)
                dve.drain()
                seq((s("ar"), s("mag"), s("cos"), ALU.mult), (s("ai"), s("mag"), s("sin"), ALU.mult),
                    (s("t0"), s("lr"), s("lr"), ALU.mult), (s("t1"), s("lam_im"), s("lam_im"), ALU.mult),
                    (s("t0"), s("t0"), s("t1"), ALU.add))
                dve.reciprocal(s("t0"), s("t0"))
                dve.tensor_scalar(s("t1"), s("ar"), -1.0, None, ALU.add)
                dve.drain()
                seq((s("fr"), s("t1"), s("lr"), ALU.mult), (s("t2"), s("ai"), s("lam_im"), ALU.mult),
                    (s("fr"), s("fr"), s("t2"), ALU.add), (s("fr"), s("fr"), s("t0"), ALU.mult),
                    (s("fi"), s("ai"), s("lr"), ALU.mult), (s("t2"), s("t1"), s("lam_im"), ALU.mult),
                    (s("fi"), s("fi"), s("t2"), ALU.subtract), (s("fi"), s("fi"), s("t0"), ALU.mult))
                pr, pi = (lambda k: sml[:, SMALL.index("pr") + k, :]), (lambda k: sml[:, SMALL.index("pi") + k, :])
                dve.memset(pr(0), 1.0)
                dve.memset(pi(0), 0.0)
                dve.drain()
                for k in range(J):
                    seq((s("t0"), pr(k), s("ar"), ALU.mult), (s("t1"), pi(k), s("ai"), ALU.mult),
                        (pr(k + 1), s("t0"), s("t1"), ALU.subtract),
                        (s("t0"), pr(k), s("ai"), ALU.mult), (s("t1"), pi(k), s("ar"), ALU.mult),
                        (pi(k + 1), s("t0"), s("t1"), ALU.add))
                for q, p4 in ((0, pr(4)), (1, pi(4))):
                    dve.tensor_copy(s5_a4[:, q, :], p4)
                seq((s5_m8[:, :], s("mag"), s("mag"), ALU.mult), (s5_m8[:, :], s5_m8[:, :], s5_m8[:, :], ALU.mult),
                    (s5_m8[:, :], s5_m8[:, :], s5_m8[:, :], ALU.mult))
                for _ in range(3):
                    square_phasor(s("cos"), s("sin"), s("cos"), s("sin"))

            def square_phasor(oc, os_, c, s_):
                t0, t1, t2 = small("t0"), small("t1"), small("t2")
                for out, a, b, op in ((t0, c, c, ALU.mult), (t1, s_, s_, ALU.mult), (t2, c, s_, ALU.mult),
                                      (t0, t0, t1, ALU.subtract)):
                    tt(out, a, b, op)
                    dve.drain()
                dve.tensor_scalar(t1, t2, 2.0, None, ALU.mult)
                dve.drain()
                tt(t2, t0, t0, ALU.mult)
                dve.drain()
                tt(small("t3"), t1, t1, ALU.mult)
                dve.drain()
                tt(t2, t2, small("t3"), ALU.add)
                dve.drain()
                dve.tensor_scalar(t2, t2, -0.5, 1.5, ALU.mult, ALU.add)
                dve.drain()
                tt(oc, t0, t2, ALU.mult)
                tt(os_, t1, t2, ALU.mult)
                dve.drain()

            def cmul(o_re, o_im, a_re, a_im, b_re, b_im, t0, t1, conj_sum=False):
                tt(t0, a_re, b_re, ALU.mult)
                tt(t1, a_im, b_im, ALU.mult)
                dve.drain()
                tt(o_re, t0, t1, ALU.subtract)
                dve.drain()
                tt(t0, a_re, b_im, ALU.mult)
                tt(t1, a_im, b_re, ALU.mult)
                dve.drain()
                tt(o_im, t0, t1, ALU.add)
                dve.drain()

            def s5_tables():
                pr, pi = (lambda k: sml[:, SMALL.index("pr") + k, :]), (lambda k: sml[:, SMALL.index("pi") + k, :])

                def g3(at):
                    return fv(at, 256).rearrange("p (t h) -> p t h", t=PAIRS)

                def over_h(a):
                    return a.unsqueeze(2).to_broadcast([P, PAIRS, S5_GROUP])
                b_re, b_im, c_re, c_im = (g3(A_G + 256 * q) for q in range(4))
                bb_re, bb_im, t0, t1 = (g3(A_G + 1024 + 256 * q) for q in range(4))
                dve.wait_ge(bc_landed, 32)
                cmul(bb_re, bb_im, over_h(small("fr")), over_h(small("fi")), b_re, b_im, t0, t1)
                q_all = fv(A_M, 4096).rearrange("p (t q j h) -> p t q j h", t=PAIRS, q=2, j=J)
                for j in range(J):
                    cmul(q_all[:, :, 0, j, :], q_all[:, :, 1, j, :], over_h(pr(j + 1)), over_h(pi(j + 1)),
                         c_re, c_im, t0, t1)
                    dve.tensor_scalar(q_all[:, :, 1, j, :], q_all[:, :, 1, j, :], -1.0, None, ALU.mult)
                e = fv(A_M + 4096, PAIRS * 2 * EC).rearrange("p (t q c) -> p t q c", t=PAIRS, q=2)
                dve.memset(e[:, :, 0, 0:1], 1.0)
                dve.memset(e[:, :, 1, 0:1], 0.0)
                cc, ss = small("cos"), small("sin")
                tmp = [fv(O_TAB + TAB_W * PAIRS * q, TAB_W * PAIRS) for q in range(2)]
                n = 1
                while n <= NC:
                    dve.tensor_copy(e[:, :, 0, n:n + 1], cc.unsqueeze(2))
                    dve.tensor_copy(e[:, :, 1, n:n + 1], ss.unsqueeze(2))
                    dve.drain()
                    for a in range(1, min(n, NC + 1 - n), TAB_W):
                        m = min(TAB_W, min(n, NC + 1 - n) - a)
                        wc, ws = (x.unsqueeze(2).to_broadcast([P, PAIRS, m]) for x in (cc, ss))
                        t0w, t1w = (x[:, 0:PAIRS * m].rearrange("p (t m) -> p t m", t=PAIRS) for x in tmp)
                        cmul(e[:, :, 0, n + a:n + a + m], e[:, :, 1, n + a:n + a + m], wc, ws,
                             e[:, :, 0, a:a + m], e[:, :, 1, a:a + m], t0w, t1w)
                    n *= 2
                    if n <= NC:
                        square_phasor(cc, ss, cc, ss)
                dve.memset(e[:, :, :, NC + 1:EC], 0.0).then_inc(qe_ready, 1)
                dve.wait_ge(qe_stored, 32)
                g_re, g_im = (fv(A_M + 3840 * q, 3840).rearrange("p (t s h) -> p t s h", t=PAIRS, s=15)
                              for q in range(2))
                dve.memset(fv(A_M, 2 * 3840), 0.0)
                dve.drain()
                for s in range(J):
                    cmul(g_re[:, :, s, :], g_im[:, :, s, :], over_h(pr(J - 1 - s)), over_h(pi(J - 1 - s)),
                         bb_re, bb_im, t0, t1)
                dve.wait_ge(cbd_landed, 16)
                dve.tensor_scalar(fv(A_G + 512, 512), fv(A_G + 512, 512), -1.0, None, ALU.mult).then_inc(g_ready, 1)

            def s5_pairs():
                for t in range(PAIRS):
                    dve.wait_ge(tp_done, t + 1)
                    dve.wait_ge(tp_stored[t % 2], 16 * (t // 2))
                    for g in range(2):
                        out = fv(O_STG + 512 * (t % 2) + P * g, P).rearrange("p (j h) -> p j h", j=J)
                        src = ps[:, t % 2, 0:256].rearrange("p (j g h) -> p j g h", j=J, g=2)[:, :, g, :]
                        last = dve.scalar_tensor_tensor(out, ident[:, :].rearrange("p (j h) -> p j h", j=J),
                                                        dcol[:, 2 * t + g:2 * t + g + 1], src, ALU.mult, ALU.add)
                    last.then_inc(t_ready, 1)

            def s5(half):
                T = [M_TMP + 130 * q for q in range(4)]
                W = [M_TMP + 520 + 130 * q for q in range(2)]

                def pair(i, r):
                    t = i * CR + r
                    st = M_TMP + 800 + (r % 2) * 2 * YC
                    at = C_SLOT[r]

                    def ec(a, n):
                        return fv(at + C_EC + a, n)

                    def es(a, n):
                        return fv(at + C_ES + a, n)
                    col = (lambda q: s5_carry[:, q, t:t + 1]) if isinstance(t, int) else (
                        lambda q: s5_carry[:, q, bass.ds(t, 1)])
                    dve.wait_ge(chunk_in_done, half * PAIRS + t + 1)
                    xr, xi = ps[:, 6 + r % 2, 0:NC], ps[:, 6 + r % 2, UC:UC + NC]
                    tt(fv(T[0], NC), ec(1, NC), xr, ALU.mult)
                    tt(fv(T[1], NC), es(1, NC), xi, ALU.mult)
                    tt(fv(T[2], NC), ec(1, NC), xi, ALU.mult)
                    tt(fv(T[3], NC), es(1, NC), xr, ALU.mult)
                    dx = ps[:, 6 + r % 2, 0:2 * UC].rearrange("p (q c) -> p q c", q=2)[:, :, NC + DS:UC]
                    tb = bass.ds(t, 1)
                    dve.tensor_copy(s5_new[:, :, tb, :].rearrange("p q o s -> p q (o s)"), dx
                                    ).then_inc(chunk_in_read, 1)
                    for q in range(2):
                        dve.tensor_copy(fv(W[q], 1), col(q))
                    dve.drain()
                    tt(fv(T[0], NC), fv(T[0], NC), fv(T[1], NC), ALU.add)
                    tt(fv(T[2], NC), fv(T[2], NC), fv(T[3], NC), ALU.subtract)
                    dve.drain()
                    m8 = s5_m8[:, bass.ds(t, 1)].to_broadcast([P, NC])
                    for q in range(2):
                        dve.tensor_tensor_scan(fv(W[q] + 1, NC), m8, fv(T[2 * q], NC), fv(W[q], 1), ALU.mult, ALU.add)
                    dve.drain()
                    tt(fv(T[0], NC + 1), ec(0, NC + 1), fv(W[0], NC + 1), ALU.mult)
                    tt(fv(T[1], NC + 1), es(0, NC + 1), fv(W[1], NC + 1), ALU.mult)
                    tt(fv(T[2], NC + 1), es(0, NC + 1), fv(W[0], NC + 1), ALU.mult)
                    tt(fv(T[3], NC + 1), ec(0, NC + 1), fv(W[1], NC + 1), ALU.mult)
                    dve.drain()
                    dve.wait_ge(yrow_done, half * PAIRS + (max(t - 1, 0) if isinstance(t, int) else t - 1))
                    for q, op in ((0, ALU.subtract), (1, ALU.add)):
                        tt(col(q), fv(T[2 * q] + NC, 1), fv(T[2 * q + 1] + NC, 1), op)
                        dve.tensor_copy(fv(st + q * YC + NC, DS), s5_dec[:, q, tb, :].rearrange("p o s -> p (o s)"))
                        last = tt(fv(st + q * YC, NC), fv(T[2 * q], NC), fv(T[2 * q + 1], NC), op)
                    last.then_inc(state_ready, 1)
                    dve.drain()

                dve.wait_ge(s5dec_landed, (half + 1) * 16)
                if half == 0:
                    dve.memset(s5_carry[:, :, :], 0.0)
                    dve.drain()
                else:
                    dve.wait_ge(out_stored, 32)
                for r in range(CR):
                    pair(0, r)
                with dve.Fori(1, PAIRS // CR) as i:
                    for r in range(CR):
                        pair(i, r)

                def wide(q):
                    return s5_a4[:, q, :].unsqueeze(2).to_broadcast([P, PAIRS, DS])
                dre, dim = s5_dec[:, 0, :, :], s5_dec[:, 1, :, :]
                nre, nim = s5_new[:, 0, :, :], s5_new[:, 1, :, :]
                t0, t1 = s5_tmp[:, 0, :, :], s5_tmp[:, 1, :, :]
                tt(t0, wide(0), dre, ALU.mult)
                tt(t1, wide(1), dim, ALU.mult)
                dve.drain()
                tt(nre, nre, t0, ALU.add)
                dve.drain()
                tt(nre, nre, t1, ALU.subtract)
                tt(t0, wide(0), dim, ALU.mult)
                dve.drain()
                tt(t1, wide(1), dre, ALU.mult)
                tt(nim, nim, t0, ALU.add)
                dve.drain()
                tt(nim, nim, t1, ALU.add).then_inc(s5dec_ready, 1)

            def gla_all(half):
                def halves(ap, s):
                    v = ap.rearrange("p (b two s) -> p b two s", two=2, s=s)
                    return v[:, :, 0, :], v[:, :, 1, :]

                def levels(dec):
                    return DEC_LEVELS if dec else range(NL)

                def diffs(c, par, dec, before_last=None):
                    L = DT if dec else C
                    de = O_DE[par]
                    b_in = fa[:, A_G:A_G + 2 * N].rearrange("p (t n) -> p t n", t=2)[:, :, bass.ds(c * C, L)]
                    b = fv(de + DE_Q, 2 * L)
                    dve.tensor_copy(b.rearrange("p (t n) -> p t n", t=2), b_in)
                    dve.drain()
                    for l in levels(dec):
                        s = LEVELS[l]
                        bl, br = halves(b, s)
                        mid = bl[:, :, s - 1:s].to_broadcast([P, L // s, s])
                        tt(fv(de + DE_R + l * 128, L).rearrange("p (b s) -> p b s", s=s), br, mid, ALU.subtract)
                        tt(fv(de + DE_L + l * 128, L).rearrange("p (b s) -> p b s", s=s), mid, bl, ALU.subtract)
                    w = DEC_SEQ if dec else C
                    bb = b.rearrange("p (b s) -> p b s", s=w)
                    if before_last:
                        before_last()
                    tt(fv(de + DE_K, 2 * L).rearrange("p (b s) -> p b s", s=w),
                       bb[:, :, w - 1:w].to_broadcast([P, 2 * L // w, w]), bb, ALU.subtract).then_inc(diff_ready, 1)

                def products(n, par, dec):
                    L = DT if dec else C
                    de = O_DE[par]
                    q, k = fv(O_ST, 2 * L), fv(O_ST + 2 * L, 2 * L)
                    dve.wait_ge(exp_ready, n + 1)
                    dve.wait_ge(stage_ready, n + 1)
                    w = DEC_SEQ if dec else C
                    dve.tensor_copy(decay[:, 0:2 * L // w],
                                    fv(de + DE_Q, 2 * L).rearrange("p (b s) -> p b s", s=w)[:, :, w - 1])
                    dve.drain()
                    for l in levels(dec):
                        s = LEVELS[l]
                        right = fv(de + DE_R + l * 128, L).rearrange("p (b s) -> p b s", s=s)
                        left = fv(de + DE_L + l * 128, L).rearrange("p (b s) -> p b s", s=s)
                        tt(right, right, halves(q, s)[1], ALU.mult)
                        tt(halves(fv(O_KT + l * 256, 2 * L), s)[0], left, halves(k, s)[0], ALU.mult)
                    tt(fv(de + DE_Q, 2 * L), fv(de + DE_Q, 2 * L), q, ALU.mult)
                    tt(fv(de + DE_K, 2 * L), fv(de + DE_K, 2 * L), k, ALU.mult).then_inc(mul_ready, 1)

                def levels_there(n):
                    dve.wait_ge(vt_ready, n + 1)
                    dve.wait_ge(o_done, n)
                    dve.wait_ge(level_done, n + 1)

                def weights(n, dec):
                    L = DT if dec else C
                    mk = dmask if dec else masks
                    att = fa[0:L, O_ATT:O_ATT + 4 * L]
                    for x, l in enumerate(levels(dec)):
                        s = LEVELS[l]
                        out = att.rearrange("p (a b two s) -> p a b two s", a=2, two=2, s=s)[:, :, :, 1, :]
                        m = mk[0:L, x * 2 * L:(x + 1) * 2 * L].rearrange("p (a b s) -> p a b s", a=2, s=s)
                        bank, col = l * 128 // 512, l * 128 % 512
                        src = ps[0:L, bank:bank + 4:3, col:col + L].rearrange("p a (b s) -> p a b s", s=s)
                        dve.copy_predicated(out, m, src)
                        dve.drain()
                    x = len(levels(dec)) * 2 * L
                    dve.copy_predicated(att.rearrange("p (a n) -> p a n", a=2),
                                        mk[0:L, x:x + 4 * L].rearrange("p (a n) -> p a n", a=2),
                                        ps[0:L, 2:6:3, 0:2 * L]).then_inc(att_ready, 1)

                block_used(half, 3, IT_M1 + 5)
                dve.memset(fv(O_KT, NL * 256 + 512), 0.0)
                if half == 0:
                    dve.memset(gla_s[:, :, :], 0.0).then_inc(s_ready, 1)
                dve.drain()
                n0 = half * (CHUNKS + 1)
                diffs(0, 0, False)

                def chunk(c, par):
                    n = n0 + c
                    last = isinstance(c, int) and c == CHUNKS - 1
                    products(n, par, False)
                    dve.wait_ge(o_done, n)
                    diffs(c + 1, 1 - par, last, lambda: levels_there(n))
                    weights(n, False)
                    dve.wait_ge(sup_done, n + 1)
                    for t in range(2):
                        ins = dve.scalar_tensor_tensor(gla_s[:, t, :], gla_s[:, t, :], decay[:, t:t + 1],
                                                       ps[:, 6, 256 + t * DV:256 + (t + 1) * DV], ALU.mult, ALU.add)
                    ins.then_inc(s_ready, 1)
                    dve.drain()

                for par in range(2):
                    chunk(par, par)
                with dve.Fori(1, CHUNKS // 2 - 1) as i:
                    for par in range(2):
                        chunk(i * 2 + par, par)
                chunk(CHUNKS - 2, 0)
                chunk(CHUNKS - 1, 1)
                dve.memset(fv(O_KT, NL * 256 + 512), 0.0)
                dve.drain()
                n = n0 + CHUNKS
                products(n, 0, True)
                levels_there(n)
                weights(n, True)
                dve.wait_ge(kht_ready, n + 1)
                dve.wait_ge(level_done, n + 1)
                for s in range(DS):
                    ins = dve.tensor_scalar(fa[0:DT, O_KT + s * 256:O_KT + (s + 1) * 256], khT[0:DT, :],
                                            vec[0:DT, V_SEQ + s:V_SEQ + s + 1], None, ALU.mult)
                ins.then_inc(ktm_ready, 1)
                dve.wait_ge(sup_done, n + 1)
                for s in range(DS):
                    for t in range(2):
                        col = (s * 2 + t) * DV
                        ins = dve.scalar_tensor_tensor(fv(O_S0 + col, DV), fv(O_S0 + col, DV),
                                                       decay[:, t * DS + s:t * DS + s + 1],
                                                       ps[:, col // 512, col % 512:col % 512 + DV], ALU.mult, ALU.add)
                ins.then_inc(s0_ready, 1)

            def merge(half):
                for h in range(HEADS):
                    dve.wait_ge(gms_done, half * HEADS + h + 1)
                    dve.drain()
                    mean_square(1, ft(A_G, 1), DV)
                    dve.wait_ge(gstd_ready, half * HEADS + h + 1)
                    dve.reciprocal(ft(A_G, 1), ft(A_G, 1))
                    dve.drain()
                    z = ft(A_Z, 4 + h)
                    dve.scalar_tensor_tensor(z, z, vec[:, V_GLA:V_GLA + 1], ft(A_G, 1), ALU.mult, ALU.mult)
                    dve.wait_ge(set_read[0], set_count(half, 0, "r", h + 1))
                    dve.drain()
                    tt(z, z, ft(A_G, 0), ALU.mult).then_inc(full_ready, 1)
                    low_part(half, SP_OG + h, z, hf(A_O, h), rt(A_O, 4 + h))
                with dve.Fori(0, 2) as i:
                    for q in range(4):
                        m = i * 4 + q
                        dve.wait_ge(set_read[0], set_count(half, 0, "m2", m + 1))
                        block_used(half, (3 * q + 2) % RING, IT_M2 + i * 3 + (3 * q + 2) // RING)
                        g = ft(A_G, q % 2)
                        for src, d in zip(psum_cols(1), cols(g)):
                            last = tt(d, d, src, ALU.mult)
                        last.then_inc(set_read[1], 1)
                        dve.drain()
                        tt(ft(A_M, m), ft(A_M, m), g, ALU.add).then_inc(full_ready, 1)
                        low_part(half, SP_MG + m, ft(A_M, m), hf(A_Z, m), rt(A_M, m))

            def add_tile(s, dst):
                for src, d in zip(psum_cols(s), cols(dst)):
                    last = tt(d, d, src, ALU.add)
                last.then_inc(set_read[s], 1)

            def hidden(half, g, par):
                for q in range(4):
                    dve.wait_ge(hidden_hi, half * FF_GROUPS * 4 + 4 * g + q + 1)
                    r, hb = ft(A_G, q % 2), A_H + 8 * N if par == 0 else A_O
                    tt(r, r, r, ALU.mult)
                    dve.drain()
                    tt(rt(hb, 4 + q), r, hf(hb, q), ALU.subtract).then_inc(hidden_split, 1)

            def outputs(half, g):
                for m in range(KT_D):
                    block_used(half, m % RING, IT_FF + ff_it(g, "down") + m // RING)
                    add_tile(m % 2, ft(A_H, m))

            dve.memset(ones[:, :], 1.0).then_inc(ones_ready, 1)
            trig()
            dve.wait_ge(const_landed, 16 * len(consts))
            dve.tensor_copy(masks[:, :], fv(A_Z, NL * 256 + 512))
            dve.tensor_copy(dmask[:, :], fa[0:DT, A_Z + 4096:A_Z + 4096 + dmask.shape[1]])
            for half in range(HALVES):
                norm(half, 0, A_M, A_M, V_MIX,
                     lambda k: low_part(half, SP_X + k, ft(A_M, k), hf(A_H, k), rt(A_H, 8 + k)))
                up = fv(O_UP, KT_S * J * UC).rearrange("p (m j c) -> p m j c", m=KT_S, j=J)
                dve.memset(up[:, :, DEC_SEQ:J, NC:NC + DS], 0.0).then_inc(u_pad, 1)
                dve.memset(up[:, :, 0:DEC_SEQ, NC + DS:UC], 0.0).then_inc(u_pad, 1)
                dve.wait_ge(wa_landed, (half + 1) * 16)
                dve.tensor_copy(ra[:, O_AH:O_AH + KT_D * P], fv(O_A, KT_D * P))
                dve.drain()
                tt(ra[:, O_AL:O_AL + KT_D * P], fv(O_A, KT_D * P), ra[:, O_AH:O_AH + KT_D * P].bitcast(F32), ALU.subtract
                   ).then_inc(wa_split, 1)
                if half == 0:
                    s5_tables()
                    s5_pairs()
                for t in range(2):
                    dve.wait_ge(gln_ready, half * 2 + t + 1)
                    g = ft(A_G, t)
                    dve.scalar_tensor_tensor(g, g, 0.0, ft(O_T), ALU.min, ALU.subtract).then_inc(gmin_ready, 1)
                    dve.drain()
                    dve.tensor_scalar(g, g, 1.0 / TAU, None, ALU.mult)
                    dve.drain()
                    spans = [(c * C, C) for c in range(CHUNKS)] + [(TP + s * DEC_SEQ, DEC_SEQ) for s in range(DS)]
                    for a, w in spans:
                        last = dve.tensor_tensor_scan(g[:, a:a + w], ones[:, 0:w], g[:, a:a + w], 0.0,
                                                      ALU.mult, ALU.add)
                last.then_inc(b_ready, 1)
                s5(half)
                for m in range(KT_S):
                    low_part(half, SP_Z5 + m, ft(A_M, m), hf(A_O, m), rt(A_O, 4 + m))
                for m in range(KT_S):
                    dve.wait_ge(set_read[m % 2], set_count(half, m % 2, "glu", m // 2 + 1))
                    tt(ft(A_M, m), ft(A_M, m), ft(A_M, 4 + m), ALU.mult).then_inc(full_ready, 1)
                for m in range(KT_S):
                    low_part(half, SP_O5 + m, ft(A_M, m), hf(A_O, m), rt(A_O, 4 + m))
                with dve.Fori(0, 2) as i:
                    for q in range(4):
                        m = i * 4 + q
                        dve.wait_ge(set_read[0], set_count(half, 0, "m1", m + 1))
                        block_used(half, (3 * q + 2) % RING, IT_M1 + i * 3 + (3 * q + 2) // RING)
                        for src, d in zip(psum_cols(1), cols(ft(A_M, m))):
                            last = tt(d, d, src, ALU.mult)
                        last.then_inc(set_read[1], 1)
                gla_all(half)
                merge(half)
                dve.wait_ge(res_landed, (half + 1) * 16)
                for m in range(KT_D):
                    block_used(half, 2 * (m % 2) + 1, IT_OUT + m // 2)
                    add_tile(m % 2, ft(A_H, m))
                norm(half, 1, A_H, A_M, V_FFN,
                     lambda k: low_part(half, SP_H2 + k, ft(A_M, k), hf(A_Z, k), rt(A_M, k)))
                hidden(half, 0, 0)
                hidden(half, 1, 1)
                with dve.Fori(0, FF_GROUPS // 2 - 1) as i:
                    for par in range(2):
                        outputs(half, i * 2 + par)
                        hidden(half, i * 2 + par + 2, par)
                outputs(half, FF_GROUPS - 2)
                outputs(half, FF_GROUPS - 1)
                norm(half, 2, A_H, A_H, V_FIN, lambda k: None)


SMALL = (["lam_re", "lam_im", "logdt", "dt", "lr", "lrdt", "th", "ang", "mag", "sin", "sinh", "cos", "ar", "ai",
          "t0", "t1", "t2", "t3", "fr", "fi"] + ["pr"] + ["pr_"] * J + ["pi"] + ["pi_"] * J)


def lay_out(a):
    f = np.float32

    def halves(prompt, sample):
        xp = prompt.reshape(HALVES, TP, D_MODEL)
        xs = sample.reshape(HALVES, DT, D_MODEL)
        x = np.concatenate([xp, xs], axis=1)
        x = x.reshape(HALVES, N, KT_D, P).transpose(0, 3, 2, 1)
        return np.ascontiguousarray(x.reshape(HALVES, P, KT_D * N))

    def tile_blocks(w):
        k, m = w.shape[0] // P, w.shape[1] // P
        w = w.reshape(k // 4, 4, P, m, P).transpose(3, 0, 2, 1, 4)
        return w.reshape(m, k // 4, P, WB)

    w_in = a["w_in"]
    offs = np.cumsum([0, 512, 256, 256, 512, 512, 16, 1024, 1024])
    u_v, r, low, gs, gg = (w_in[:, offs[0]:offs[4]], w_in[:, offs[4]:offs[5]], w_in[:, offs[5]:offs[6]],
                           w_in[:, offs[6]:offs[7]], w_in[:, offs[7]:offs[8]])
    stages = [tile_blocks(u_v).reshape(-1, P, WB), tile_blocks(a["w_s5_glu"]).reshape(-1, P, WB)]

    def merged(g, br):
        return np.concatenate([tile_blocks(g), tile_blocks(br)], axis=1).reshape(-1, P, WB)
    stages += [merged(gs, a["w_s5_br"]), tile_blocks(r).reshape(-1, P, WB), merged(gg, a["w_gla_br"]),
               tile_blocks(a["w_out"]).reshape(-1, P, WB)]
    up = tile_blocks(a["w_ff1"]).reshape(FF_GROUPS, 8, P, WB)
    down = tile_blocks(a["w_ff2"]).transpose(1, 0, 2, 3)
    stages += [up[0], up[1]]
    for g in range(FF_GROUPS):
        stages.append(down[g])
        if g + 2 < FF_GROUPS:
            stages.append(up[g + 2])
    wpack = np.ascontiguousarray(np.concatenate(stages))
    assert wpack.shape == (ITERS * RING, P, WB), wpack.shape

    wa = np.zeros((P, KT_D, P), f)
    wa[:, :, 0:RANK] = low.reshape(KT_D, P, RANK).transpose(1, 0, 2)
    vec = np.zeros((P, V_ALL), f)
    for at, g in ((V_MIX, "g_mix"), (V_FFN, "g_ffn"), (V_FIN, "g_final")):
        vec[:, at:at + KT_D] = a[g].reshape(KT_D, P).T
    vec[:, V_BG:V_BG + 2] = a["b_gate"].reshape(2, P).T
    vec[:, V_GLA] = a["g_gla_norm"]
    for s in range(DS):
        vec[s * DEC_SEQ:(s + 1) * DEC_SEQ, V_SEQ + s] = 1.0

    def level_masks(L, levels):
        j, out = np.arange(L)[:, None], []
        for s in levels:
            i = np.arange(L // 2)[None, :]
            m = (j // (2 * s) == i // s) & (j % (2 * s) < s)
            out.append(np.tile(m, (1, 4)))
        out.append(np.tile(np.eye(L, dtype=bool), (1, 4)))
        return np.ascontiguousarray(np.concatenate(out, axis=1).astype(f))

    def by_pair(v):
        v = v.reshape(PAIRS, 2, S5_STATE, *v.shape[2:])
        return np.moveaxis(v, 0, 2).reshape(P, PAIRS, *v.shape[3:])

    logdt = np.broadcast_to(a["log_dt"][:, None], (S5_GROUPS, S5_STATE))
    s5small = np.stack([by_pair(a["lam_re"]), by_pair(a["lam_im"]), by_pair(logdt)], axis=1)
    b = np.stack([by_pair(a["b_re"]), by_pair(a["b_im"])], axis=1)
    c = np.stack([by_pair(a["c_re"].transpose(0, 2, 1)), by_pair(a["c_im"].transpose(0, 2, 1))], axis=1)
    cbd = np.zeros((2, S5_STATE, 2, PAIRS, 2, S5_GROUP), f)
    cc = c.reshape(2, S5_STATE, 2, PAIRS, S5_GROUP)
    for g in range(2):
        cbd[g, :, :, :, g, :] = cc[g]
    dcol = np.tile(a["d_skip"].T, (J, 1))

    def s5_states(v):
        v = v.reshape(HALVES, DS, PAIRS, 2, S5_STATE).transpose(0, 3, 4, 2, 1)
        return v.reshape(HALVES, P, PAIRS, DS)
    s5dec = np.stack([s5_states(a["state_s5_re"]), s5_states(a["state_s5_im"])], axis=2)
    gd = a["state_gla"].reshape(HALVES, DS, 2, 2, DK, DV).transpose(0, 3, 4, 1, 2, 5)
    out = {
        "xT": halves(a["x_prompt"], a["x_sample"]), "wpack": wpack, "wa": wa.reshape(P, -1), "wgu_d": a["w_gate_up"],
        "vec_d": vec, "ident_d": np.eye(P, dtype=f), "masks_d": level_masks(C, LEVELS),
        "dmask_d": level_masks(DT, [LEVELS[l] for l in DEC_LEVELS]), "s5small": s5small,
        "b_d": b.reshape(P, -1), "c_d": c.reshape(P, -1), "cbd_d": cbd.reshape(P, -1), "dcol_d": dcol,
        "s5dec_d": s5dec, "gladec_d": gd.reshape(HALVES, P, -1),
    }
    return {k: np.ascontiguousarray(v) for k, v in out.items()}


OUTS = {"yT": (HALVES, P, KT_D * N), "s5_prompt": (P, 2, PAIRS), "gla_prompt": (P, 2, DV),
        "s5_dec_out": (HALVES, P, 2, PAIRS, DS), "gla_dec_out": (HALVES, P, DS * 2 * DV)}


def kernel(**inputs):
    from concourse import bacc
    from concourse.bass_utils import run_bass_kernel_spmd

    nc = bacc.Bacc("TRN2", target_bir_lowering=False, num_devices=1)
    arrays = lay_out({k: np.asarray(v) for k, v in inputs.items()})
    aps = {n: nc.dram_tensor(n, v.shape, mybir.dt.from_np(v.dtype), kind="ExternalInput").ap()
           for n, v in arrays.items()}
    for n, shape in OUTS.items():
        aps[n] = nc.dram_tensor(n, shape, F32, kind="ExternalOutput").ap()
    build(nc, **aps)
    got = run_bass_kernel_spmd(nc, [arrays], core_ids=[0]).results[0]

    y = got["yT"].reshape(HALVES, P, KT_D, N).transpose(0, 3, 2, 1).reshape(HALVES, N, D_MODEL)
    y_prompt = np.ascontiguousarray(y[:, 0:TP].reshape(1, SEQ, D_MODEL))
    y_sample = np.ascontiguousarray(y[:, TP:N].reshape(DEC_BATCH, DEC_SEQ, D_MODEL))
    sp = got["s5_prompt"].reshape(2, S5_STATE, 2, PAIRS).transpose(2, 3, 0, 1).reshape(2, 1, S5_GROUPS, S5_STATE)
    gp = got["gla_prompt"].reshape(2, DK, 2, DV).transpose(2, 0, 1, 3).reshape(1, HEADS, DK, DV)
    sd = got["s5_dec_out"].reshape(HALVES, 2, S5_STATE, 2, PAIRS, DS).transpose(3, 0, 5, 4, 1, 2)
    sd = sd.reshape(2, DEC_BATCH, S5_GROUPS, S5_STATE)
    gd = got["gla_dec_out"].reshape(HALVES, 2, DK, DS, 2, DV).transpose(0, 3, 4, 1, 2, 5)
    gd = gd.reshape(DEC_BATCH, HEADS, DK, DV)
    return tuple(np.ascontiguousarray(v) for v in (y_prompt, y_sample, sp[0], sp[1], gp, sd[0], sd[1], gd))
```

```python
from contextlib import ExitStack

import concourse.bass as bass
import numpy as np
from concourse import mybir

F32 = mybir.dt.float32
F32R = mybir.dt.float32r
U8 = mybir.dt.uint8
ALU = mybir.AluOpType
ACT = mybir.ActivationFunctionType

P = 128
D_MODEL = 1024
SEQ = 2048
DEC_BATCH, DEC_SEQ = 8, 4
S5_WIDTH, S5_GROUP, S5_GROUPS, S5_STATE = 512, 16, 32, 64
HEADS, DK, DV = 4, 64, 128
RANK = 16
TAU = 16.0
D_FF = 4096
EPS = 1e-6

HALVES = 2
TP = SEQ // HALVES
DS = DEC_BATCH // HALVES
DT = DS * DEC_SEQ
N = TP + DT
BLK = [(0, 352), (352, 344), (696, 344)]
KT_D = D_MODEL // P
KT_S = S5_WIDTH // P
WB = 4 * P
RING = 4

J = 8
PAIRS = S5_GROUPS // 2
NC = TP // J
UC = NC + 2 * DS
YC = NC + DS
EC = NC + 2
C_T, C_PR, C_PI, C_QR, C_QI, C_EC, C_ES = 0, 256, 384, 512, 640, 768, 768 + EC
C_W = 768 + 2 * EC
CR = 4
TABLES_OUT_AT = 7

C = 128
CHUNKS = TP // C
LEVELS = [64, 32, 16, 8, 4, 2, 1]
NL = len(LEVELS)
NL_A = 4
DEC_LEVELS = [l for l, s in enumerate(LEVELS) if 2 * s <= DEC_SEQ]
DE_K, DE_Q = NL * 2 * C, (NL + 1) * 2 * C
DE_W = (NL + 2) * 2 * C

IT_A = 0
IT_GLU = IT_A + 6
IT_M1 = IT_GLU + 1
IT_R = IT_M1 + 6
IT_M2 = IT_R + 2
IT_OUT = IT_M2 + 6
IT_FF = IT_OUT + 4
ITERS = IT_FF + 32
FF_GROUPS = 8

A_H = 0
A_O = A_H + 16 * N
A_Z = A_O + 8 * N
A_M = A_Z + 8 * N
A_G = A_M + 8 * N
A_END = A_G + 2 * N
REGIONS = [("h0", A_H, 8 * N), ("h1", A_H + 8 * N, 8 * N), ("o", A_O, 8 * N), ("z", A_Z, 8 * N), ("m", A_M, 8 * N),
           ("g", A_G, 2 * N)]
M_U = A_M
M_TMP = A_M + S5_GROUPS * UC
M_C0 = M_TMP + 1400
O_UP = A_O
O_A = A_O + 4352
O_AH, O_AL = O_A + N, O_A + N + 1024
O_T = O_A + N
O_C0 = A_O + 4352
C_SLOT = [M_C0, M_C0 + C_W, O_C0, O_C0 + C_W]
O_TAB, TAB_W = A_O + 7440, 27
O_STG_T = O_UP
O_STG_P, STG = O_T, 8
O_SHIFT = O_TAB
G_K, G_SKIP = A_G + 1024, A_G + 1536
O_DE = [A_O, A_O + DE_W]
O_ST = [A_O + 2 * DE_W, A_O + 2 * DE_W + 8 * C]
O_ATT = O_ST[1] + 8 * C
O_VT = [O_ATT + HEADS * C, O_ATT + 2 * HEADS * C]
O_S0, O_KTM = O_DE[1], O_DE[1] + 1024

SETS = {"nx": (1, 0), "a": (6, 6), "low": (1, 1), "glu": (2, 2), "m1": (8, 8), "r": (4, 4), "m2": (8, 8),
        "out": (4, 4), "nf": (1, 0), "ff": (48, 48), "ny": (1, 0)}
SET_BASE, SET_TOTAL = {}, [0, 0]
for _name, _n in SETS.items():
    SET_BASE[_name] = tuple(SET_TOTAL)
    SET_TOTAL = [SET_TOTAL[0] + _n[0], SET_TOTAL[1] + _n[1]]
SP_X, SP_Z5, SP_O5, SP_OG, SP_MG, SP_H2, SP_ALL = 0, 8, 12, 16, 20, 28, 36

V_MIX, V_FFN, V_FIN, V_BG, V_GLA, V_SEQ = 0, 8, 16, 24, 26, 27
V_ALL = V_SEQ + DS
MAGIC = 12582912.0
PI2_1, PI2_2, PI2_3 = 6.28125, 0.0019350051879882812, 3.019916050e-07


def ff_before(g, part):
    if part == "down":
        return (min(g + 2, FF_GROUPS) if isinstance(g, int) else g + 2), g
    return g, (max(g - 1, 0) if isinstance(g, int) else g - 1)


def ff_set(g, part):
    ups, downs = ff_before(g, part)
    return ups * 2 + downs * 4


def ff_it(g, part):
    ups, downs = ff_before(g, part)
    return ups * 2 + downs * 2


class Arena:

    def __init__(self, tensors):
        self.tensors = tensors

    def find(self, col):
        for tensor, (_, start, width) in zip(self.tensors, REGIONS):
            if start <= col < start + width:
                return tensor, start
        raise IndexError(col)

    def __getitem__(self, key):
        rows, span = key
        tensor, start = self.find(span.start)
        return tensor[rows, span.start - start:span.stop - start]

    def at(self, col, offset, n):
        tensor, start = self.find(col)
        return tensor[:, bass.ds(col - start + offset, n)]


def build(nc, xT, wpack, wa, wgu_d, vec_d, ident_d, masks_d, dmask_d, s5small, b_d, c_d, cbd_d, dcol_d,
          s5dec_d, gladec_d, yT, s5_prompt, gla_prompt, s5_dec_out, gla_dec_out):
    u_dram = nc.dram_tensor("u_scratch", (KT_S, P, J, UC), F32, kind="Internal").ap()
    y_dram = nc.dram_tensor("y_scratch", (KT_S, P, J, YC), F32, kind="Internal").ap()
    c_dram = nc.dram_tensor("s5_constants", (PAIRS, P, C_W), F32, kind="Internal").ap()

    with ExitStack() as ctx:
        slab_at = (nc.sbuf_usable_end - A_END * 4) // 64 * 64

        def regions(kind, dt):
            return Arena([nc.alloc_sbuf_tensor_at(f"{kind}_{name}", [P, width], dt, offset=slab_at + start * 4)
                          for name, start, width in REGIONS])
        fa, ra = regions("f", F32), regions("r", F32R)

        def sb(name, shape, dt=F32):
            return ctx.enter_context(nc.sbuf_tensor(name, shape, dt))

        def sem(name):
            return ctx.enter_context(nc.semaphore(name))

        w_raw = sb("w_raw", [P, RING, WB])
        w_hi = sb("w_hi", [P, RING, WB], F32R)
        w_lo = sb("w_lo", [P, RING, WB], F32R)
        khT = sb("khT", [P, 256])
        masks = sb("masks", [P, NL * 256 + 512], U8)
        dmask = sb("dmask", [DT, len(DEC_LEVELS) * 32 + 64], U8)
        ident = sb("ident", [P, P])
        ones = sb("ones", [P, P])
        vec = sb("vec", [P, V_ALL])
        wgu = sb("wgu", [RANK, 2 * P])
        dcol = sb("dcol", [P, S5_GROUPS])
        gla_s = sb("gla_s", [P, 2, 2, DV])
        decay = sb("decay", [P, 2, 8])
        s5_carry = sb("s5_carry", [P, 2, PAIRS])
        s5_m8 = sb("s5_m8", [P, PAIRS])
        s5_a4 = sb("s5_a4", [P, 2, PAIRS])
        s5_dec = sb("s5_dec", [P, 2, PAIRS, DS])
        s5_new = sb("s5_new", [P, 2, PAIRS, DS])
        s5_tmp = sb("s5_tmp", [P, 2, PAIRS, DS])
        zero = sb("zero", [P, 1])
        sml = sb("s5_small", [P, len(SMALL), PAIRS])
        assert nc.sbuf_base <= slab_at, (nc.sbuf_base, slab_at)
        ps = ctx.enter_context(nc.psum_tensor("ps", [P, 8, 512], F32))

        w_landed = [sem(f"w_landed{s}") for s in range(RING)]
        w_split = [sem(f"w_split{s}") for s in range(RING)]
        w_used = [sem(f"w_used{s}") for s in range(RING)]
        set_read = [sem("set0_read"), sem("set1_read")]
        const_landed, s5in_landed, bc_landed, cbd_landed = (sem("const_landed"), sem("s5in_landed"),
                                                            sem("bc_landed"), sem("cbd_landed"))
        x_landed, res_landed, wa_landed = sem("x_landed"), sem("res_landed"), sem("wa_landed")
        ones_ready = sem("ones_ready")
        sq_ready, ssum_ready, ms_done, std_ready = sem("sq_ready"), sem("ssum_ready"), sem("ms_done"), sem("std_ready")
        full_ready, hi_ready, split_ready = sem("full_ready"), sem("hi_ready"), sem("split_ready")
        u_pad, u_stored, u_landed = sem("u_pad"), sem("u_stored"), sem("u_landed")
        wa_split, low_done, low_ready, gpre_done = sem("wa_split"), sem("low_done"), sem("low_ready"), sem("gpre_done")
        gln_ready, gmin_ready, b_ready = sem("gln_ready"), sem("gmin_ready"), sem("b_ready")
        dt_ready, trig_in, trig_out = sem("dt_ready"), sem("trig_in"), sem("trig_out")
        qe_ready, qe_stored, g_ready = sem("qe_ready"), sem("qe_stored"), sem("g_ready")
        tp_done, p_ready, t_ready, tp_stored = sem("tp_done"), sem("p_ready"), sem("t_ready"), sem("tp_stored")
        k_done, k_ready, shift_done = sem("k_done"), sem("k_ready"), sem("shift_done")
        c_landed = [sem(f"c_landed{s}") for s in range(CR)]
        chunk_in_done, chunk_in_read = sem("chunk_in_done"), sem("chunk_in_read")
        state_ready, yrow_done, yrow_read = sem("state_ready"), sem("yrow_done"), sem("yrow_read")
        yrow_stored, yperm_landed, gelu_ready = sem("yrow_stored"), sem("yperm_landed"), sem("gelu_ready")
        s5dec_landed, s5dec_ready = sem("s5dec_landed"), sem("s5dec_ready")
        stage_ready, diff_ready, exp_ready, mul_ready = (sem("stage_ready"), sem("diff_ready"), sem("exp_ready"),
                                                         sem("mul_ready"))
        vt_done, kht_done = sem("vt_done"), sem("kht_done")
        level_a_done, level_done = sem("level_a_done"), sem("level_done")
        vt_ready, kht_ready, att_ready = sem("vt_ready"), sem("kht_ready"), sem("att_ready")
        o_done, o_read, sup_done, s_ready = sem("o_done"), sem("o_read"), sem("sup_done"), sem("s_ready")
        s0_landed, ktm_ready, s0_ready = sem("s0_landed"), sem("ktm_ready"), sem("s0_ready")
        osq_ready, gms_done, gstd_ready = sem("osq_ready"), sem("gms_done"), sem("gstd_ready")
        hidden_hi, hidden_split = sem("hidden_hi"), sem("hidden_split")
        y_ready, y_stored, out_stored = sem("y_ready"), sem("y_stored"), sem("out_stored")

        def tile(arena, at, k):
            return arena.at(at + k * N, 0, N) if isinstance(k, int) else arena.at(at, k * N, N)

        def ft(at, k=0):
            return tile(fa, at, k)

        def rt(at, k=0):
            return tile(ra, at, k)

        def hf(at, k=0):
            return tile(ra, at, k).bitcast(F32)

        def fv(at, n):
            return fa[:, at:at + n]

        def cols(tile):
            return [tile[:, 0:352], tile[:, 352:N].rearrange("p (b n) -> p b n", b=2)]

        def psum_cols(s):
            return [ps[:, 3 * s, 0:352], ps[:, 3 * s + 1:3 * s + 3, 0:344]]

        def set_count(half, s, stage, n):
            return half * SET_TOTAL[s] + SET_BASE[stage][s] + n

        def full_count(half, n):
            before_z5 = isinstance(n, int) and n <= SP_Z5
            return half * (SP_ALL - KT_S) + n - (0 if before_z5 else KT_S)

        def small(name, n=1):
            k = SMALL.index(name)
            return sml[:, k:k + n, :] if n > 1 else sml[:, k, :]

        def rows_of(h):
            return slice(64 * (h % 2), 64 * (h % 2) + 64), h // 2, 2 * (h % 2) + h // 2

        consts = [(vec[:, :], vec_d), (ident[:, :], ident_d), (fv(A_Z, NL * 256 + 512), masks_d),
                  (fa[0:DT, A_Z + 4096:A_Z + 4096 + dmask.shape[1]], dmask_d),
                  (wgu[:, :], wgu_d), (dcol[:, :], dcol_d)]
        block = ctx.enter_context(nc.Block())

        @block.sync
        def _(sp):
            def load(s, it):
                block = wpack[it * RING + s] if isinstance(it, int) else wpack[bass.ds(it * RING + s, 1)].rearrange(
                    "o p n -> p (o n)")
                sp.dma_start(w_raw[:, s, :], block).then_inc(w_landed[s], 16)

            for s in range(RING):
                load(s, 0)
            for half in range(HALVES):
                with sp.Fori(0 if half else 1, ITERS) as it:
                    for s in range(RING):
                        sp.wait_ge(w_split[s], half * ITERS + it)
                        load(s, it)

        @block.gpsimd
        def _(pool):
            pool.memset(zero[:, :], 0.0)
            pool.drain()

            def split(s, n):
                pool.wait_ge(w_landed[s], (n + 1) * 16)
                if not isinstance(n, int):
                    pool.wait_ge(w_used[s], n)
                pool.tensor_tensor(w_hi[:, s, :], w_raw[:, s, :], zero[:, :].to_broadcast([P, WB]), ALU.subtract)
                pool.drain()
                pool.tensor_tensor(w_lo[:, s, :], w_raw[:, s, :], w_hi[:, s, :].bitcast(F32),
                                   ALU.subtract).then_inc(w_split[s], 1)

            for s in range(RING):
                split(s, 0)
            with pool.Fori(1, HALVES * ITERS) as n:
                for s in range(RING):
                    split(s, n)

        @block.tensor
        def _(pe):
            def set_free(half, s, stage, n):
                pe.wait_ge(set_read[s], set_count(half, s, stage, n))

            def tiles_of(s, k, total, wh, wl, hi, lo):
                for b, (c0, cn) in enumerate(BLK):
                    out = ps[:, 3 * s + b, 0:cn]
                    h, l = hi(k)[:, c0:c0 + cn], lo(k)[:, c0:c0 + cn]
                    pe.matmul(out, wh, h, start=(k == 0), stop=False)
                    pe.matmul(out, wh, l, start=False, stop=False)
                    last = pe.matmul(out, wl, h, start=False, stop=(k == total - 1))
                return last

            def product(s, blocks, hi, lo):
                for n, (place, it) in enumerate(blocks):
                    pe.wait_ge(w_split[place], it + 1)
                    for q in range(4):
                        last = tiles_of(s, 4 * n + q, 4 * len(blocks), w_hi[:, place, q * P:(q + 1) * P],
                                        w_lo[:, place, q * P:(q + 1) * P], hi, lo)
                    last.then_inc(w_used[place], 1)

            def row_sums(half, stage, n):
                set_free(half, 0, stage, 0)
                pe.wait_ge(ssum_ready, half * 3 + n + 1)
                for b, (c0, cn) in enumerate(BLK):
                    last = pe.matmul(ps[:, b, 0:cn], ones[:, :], fv(A_O + c0, cn), start=True, stop=True)
                last.then_inc(ms_done, 1)

            def tile_pair(half, stage, n, it, hi, lo):
                for s in range(2):
                    set_free(half, s, stage, n)
                    product(s, [(2 * s, it), (2 * s + 1, it)], hi, lo)

            def s5_setup():
                pe.wait_ge(g_ready, 1)
                g_re = fv(A_M, 3840).rearrange("p (t s) -> p t s", t=PAIRS)
                g_im = fv(A_M + 3840, 3840).rearrange("p (t s) -> p t s", t=PAIRS)
                c_re = fv(A_G, 512).rearrange("p (t c) -> p t c", t=PAIRS)
                c_im = fv(A_G + 512, 512).rearrange("p (t c) -> p t c", t=PAIRS)
                set_free(0, 0, "low", 0)
                set_free(0, 1, "low", 0)
                for t in range(PAIRS):
                    out = ps[:, 0, 2 * S5_GROUP * t:2 * S5_GROUP * (t + 1)]
                    pe.matmul(out, g_re[:, t, 0:P], c_re[:, t, :], start=True, stop=False)
                    last = pe.matmul(out, g_im[:, t, 0:P], c_im[:, t, :], start=False, stop=True)
                last.then_inc(k_done, 1)
                for t in range(PAIRS):
                    if t >= 2:
                        pe.wait_ge(p_ready, t - 1)
                    pe.transpose(ps[:, 4 + t % 2, 0:128], g_re[:, t, 0:P], ident[:, :])
                    pe.transpose(ps[:, 4 + t % 2, 128:256], g_im[:, t, 0:P], ident[:, :]).then_inc(tp_done, 1)
                pe.wait_ge(k_ready, 1)
                for j in range(J):
                    if j >= 4:
                        pe.wait_ge(t_ready, j - 3)
                    w0 = S5_GROUP * (J - 1 - j)
                    pe.matmul(ps[:, j % 4, 0:512], fv(O_SHIFT + w0, P), fv(G_K, 512), start=True, stop=True
                              ).then_inc(shift_done, 1)
                pe.wait_ge(p_ready, PAIRS)
                pe.wait_ge(t_ready, J)

            def s5_in(half, t):
                r = t % CR
                pe.wait_ge(c_landed[r], (half * (PAIRS // CR) + t // CR + 1) * 16)
                pe.wait_ge(chunk_in_read, half * PAIRS + max(t - 1, 0))
                for g in range(2):
                    for q, c0 in ((0, C_PR), (1, C_PI)):
                        last = pe.matmul(ps[64 * g:64 * g + 64, 6 + t % 2, q * UC:(q + 1) * UC],
                                         fv(C_SLOT[r] + c0 + 64 * g, 64), fv(M_U + (t * 2 + g) * UC, UC),
                                         start=True, stop=True)
                last.then_inc(chunk_in_done, 1)

            def s5_rows(half, t):
                pe.wait_ge(state_ready, half * PAIRS + t + 1)
                pe.wait_ge(yrow_read, half * PAIRS + max(t - 1, 0))
                at, st = C_SLOT[t % CR], M_TMP + 800 + (t % 2) * 2 * YC
                for g in range(2):
                    out, rows = ps[:, 2 * (t % 2) + g, 0:YC], slice(64 * g, 64 * g + 64)
                    pe.matmul(out, fv(at + C_T + P * g, P), fv(M_U + (t * 2 + g) * UC, YC), start=True, stop=False)
                    pe.matmul(out, fa[rows, at + C_QR:at + C_QR + P], fa[rows, st:st + YC], start=False, stop=False)
                    last = pe.matmul(out, fa[rows, at + C_QI:at + C_QI + P], fa[rows, st + YC:st + 2 * YC],
                                     start=False, stop=True)
                last.then_inc(yrow_done, 1)

            def s5(half):
                set_free(half, 0, "glu", 0)
                set_free(half, 1, "glu", 0)
                pe.wait_ge(u_landed, (half + 1) * 16 * J)
                s5_in(half, 0)
                s5_in(half, 1)
                for t in range(PAIRS):
                    s5_rows(half, t)
                    if t + 2 < PAIRS:
                        s5_in(half, t + 2)
                pe.wait_ge(yrow_read, (half + 1) * PAIRS)

            def merge_products(half, it0, stage, split_count):
                with pe.Fori(0, 2) as i:
                    for q in range(4):
                        b = [((3 * q + x) % RING, half * ITERS + it0 + i * 3 + (3 * q + x) // RING) for x in range(3)]
                        set_free(half, 0, stage, i * 4 + q)
                        product(0, b[0:2], lambda k: rt(A_H, k), lambda k: rt(A_H, 8 + k))
                        pe.wait_ge(split_ready, half * SP_ALL + split_count)
                        set_free(half, 1, stage, i * 4 + q)
                        product(1, b[2:3], lambda k: rt(A_O, k), lambda k: rt(A_O, 4 + k))

            def gla_pre(half, c, par):
                L = DT if isinstance(c, int) and c == CHUNKS else C
                n = half * (CHUNKS + 1) + c
                st, de = O_ST[par], O_DE[par]
                pe.wait_ge(stage_ready, n + 1)
                pe.wait_ge(vt_ready, n)
                for h in range(HEADS):
                    slot = rows_of(h)[2]
                    last = pe.transpose(ps[0:L, 6, slot * DV:(slot + 1) * DV], fv(st + 4 * L + h * L, L), ident[:, :])
                last.then_inc(vt_done, 1)
                pe.wait_ge(mul_ready, n + 1)
                pe.wait_ge(kht_ready, n)
                pe.wait_ge(s_ready, half * CHUNKS + c + 1)
                for t in range(2):
                    last = pe.transpose(ps[0:L, 7, t * P:(t + 1) * P], fv(de + DE_K + t * L, L), ident[:, :])
                last.then_inc(kht_done, 1)

            def gla_sums(half, c, par):
                dec = isinstance(c, int) and c == CHUNKS
                L = DT if dec else C
                for s in range(DS if dec else 1):
                    for h in range(HEADS):
                        _, t, slot = rows_of(h)
                        kk = t * P + (h % 2) * 64
                        keys = fa[0:L, O_KTM + s * 256 + kk:O_KTM + s * 256 + kk + 64] if dec else khT[0:L, kk:kk + 64]
                        bank, col = ((s * 2 + t) * DV // 512, (s * 2 + t) * DV % 512) if dec else (7, 256 + t * DV)
                        last = pe.matmul(ps[64 * (h % 2):64 * (h % 2) + 64, bank, col:col + DV],
                                         keys, fa[0:L, O_VT[par] + slot * DV:O_VT[par] + (slot + 1) * DV],
                                         start=True, stop=True)
                last.then_inc(sup_done, 1)

            def gla(half, c, par):
                dec = isinstance(c, int) and c == CHUNKS
                L = DT if dec else C
                n = half * (CHUNKS + 1) + c
                st, de = O_ST[par], O_DE[par]
                pe.wait_ge(vt_ready, n + 1)
                pe.wait_ge(kht_ready, n + 1)
                if not dec:
                    gla_sums(half, c, par)
                for l in (DEC_LEVELS if dec else range(NL)):
                    for h in (0, 2, 1, 3):
                        rows, t, _ = rows_of(h)
                        col, at = l * 128 + t * (L // 2), de + l * 256 + t * L
                        right = fa[rows, at:at + L].rearrange("p (b two s) -> p b two s", two=2, s=LEVELS[l])[:, :, 1, :]
                        last = pe.matmul(ps[0:L, 2 * (col // 512) + h % 2, col % 512:col % 512 + L // 2],
                                         fa[rows, at:at + L], right, start=True, stop=True)
                    if l == NL_A - 1:
                        last.then_inc(level_a_done, 1)
                pe.wait_ge(o_read, n)
                for h in (0, 2, 1, 3):
                    rows, t, _ = rows_of(h)
                    last = pe.matmul(ps[0:L, 4 + h % 2, t * L:t * L + L],
                                     fa[rows, st + 2 * L + t * L:st + 3 * L + t * L],
                                     fa[rows, st + t * L:st + t * L + L], start=True, stop=True)
                last.then_inc(level_done, 1)
                if not dec:
                    gla_pre(half, c + 1, 1 - par)
                pe.wait_ge(att_ready, n + 1)
                if dec:
                    pe.wait_ge(s0_landed, (half + 1) * 16)
                for h in range(HEADS):
                    rows, t, slot = rows_of(h)
                    bank, o0, qq = 4 + h % 2, 256 + t * L, de + DE_Q + t * L
                    vr = fa[0:L, O_VT[par] + slot * DV:O_VT[par] + (slot + 1) * DV]
                    att = fa[0:L, O_ATT + slot * L:O_ATT + (slot + 1) * L]
                    if dec:
                        last = pe.matmul(ps[:, bank, o0:o0 + L], vr, att, start=True, stop=False, skip_group_check=True)
                        for s in range(DS):
                            s0, a = O_S0 + (s * 2 + t) * DV, s * DEC_SEQ
                            last = pe.matmul(ps[:, bank, o0 + a:o0 + a + DEC_SEQ], fa[rows, s0:s0 + DV],
                                             fa[rows, qq + a:qq + a + DEC_SEQ], start=False, stop=(s == DS - 1),
                                             skip_group_check=True)
                    else:
                        pe.matmul(ps[:, bank, o0:o0 + L], gla_s[rows, par, t, :], fa[rows, qq:qq + L],
                                  start=True, stop=False)
                        last = pe.matmul(ps[:, bank, o0:o0 + L], vr, att, start=False, stop=True)
                last.then_inc(o_done, 1)
                if dec:
                    pe.wait_ge(ktm_ready, half + 1)
                    gla_sums(half, c, par)

            def ff_up(half, g):
                for q in range(2):
                    tile_pair(half, "ff", ff_set(g, "up") + q, half * ITERS + IT_FF + ff_it(g, "up") + q,
                              lambda k: rt(A_Z, k), lambda k: rt(A_M, k))

            def ff_down(half, g, par):
                pe.wait_ge(hidden_split, half * FF_GROUPS * 4 + 4 * g + 4)
                hb = A_H + 8 * N if par == 0 else A_O
                for q in range(2):
                    for s in range(RING):
                        set_free(half, s % 2, "ff", ff_set(g, "down") + 2 * q + s // 2)
                        product(s % 2, [(s, half * ITERS + IT_FF + ff_it(g, "down") + q)],
                                lambda k: rt(hb, k), lambda k: rt(hb, 4 + k))

            def gate_products(half):
                pe.wait_ge(low_ready, half + 1)
                for t in range(2):
                    s = 1 - t
                    set_free(half, s, "low", 0)
                    for b, (c0, cn) in enumerate(BLK):
                        last = pe.matmul(ps[:, 3 * s + b, 0:cn], wgu[:, t * P:(t + 1) * P],
                                         fa[0:RANK, O_A + c0:O_A + c0 + cn], start=True, stop=True)
                    last.then_inc(gpre_done, 1)

            pe.wait_ge(ones_ready, 1)
            pe.wait_ge(const_landed, 16 * len(consts))
            for half in range(HALVES):
                x_hi, x_lo = (lambda k: rt(A_H, k)), (lambda k: rt(A_H, 8 + k))
                row_sums(half, "nx", 0)
                pe.wait_ge(split_ready, half * SP_ALL + SP_X + KT_D)
                tile_pair(half, "a", 0, half * ITERS + IT_A, x_hi, x_lo)
                with pe.Fori(1, 6) as i:
                    tile_pair(half, "a", i, half * ITERS + IT_A + i, x_hi, x_lo)
                set_free(half, 0, "low", 0)
                pe.wait_ge(wa_split, half + 1)
                for k in range(KT_D):
                    last = tiles_of(0, k, KT_D, ra[:, O_AH + k * P:O_AH + (k + 1) * P],
                                    ra[:, O_AL + k * P:O_AL + (k + 1) * P], x_hi, x_lo)
                last.then_inc(low_done, 1)
                if half == 0:
                    pe.wait_ge(low_ready, 1)
                    s5_setup()
                gate_products(half)
                s5(half)
                pe.wait_ge(split_ready, half * SP_ALL + SP_Z5 + KT_S)
                for s in range(RING):
                    set_free(half, s % 2, "glu", s // 2)
                    product(s % 2, [(s, half * ITERS + IT_GLU)], lambda k: rt(A_O, k), lambda k: rt(A_O, 4 + k))
                merge_products(half, IT_M1, "m1", SP_O5 + KT_S)
                set_free(half, 0, "r", 0)
                set_free(half, 1, "r", 0)
                gla_pre(half, 0, 0)
                for par in range(2):
                    gla(half, par, par)
                with pe.Fori(1, CHUNKS // 2 - 1) as i:
                    for par in range(2):
                        gla(half, i * 2 + par, par)
                for c in range(CHUNKS - 2, CHUNKS + 1):
                    gla(half, c, c % 2)
                pe.wait_ge(o_read, (half + 1) * (CHUNKS + 1))
                pe.wait_ge(s0_ready, half + 1)
                for h in range(HEADS):
                    set_free(half, 0, "r", h)
                    b, it = 2 * (h % 2), half * ITERS + IT_R + h // 2
                    product(0, [(b, it), (b + 1, it)], x_hi, x_lo)
                    set_free(half, 1, "r", h)
                    pe.wait_ge(osq_ready, half * HEADS + h + 1)
                    for b, (c0, cn) in enumerate(BLK):
                        last = pe.matmul(ps[:, 3 + b, 0:cn], ones[:, :], ft(A_O, h)[:, c0:c0 + cn],
                                         start=True, stop=True)
                    last.then_inc(gms_done, 1)
                merge_products(half, IT_M2, "m2", SP_OG + HEADS)
                pe.wait_ge(split_ready, half * SP_ALL + SP_MG + KT_D)
                with pe.Fori(0, 4) as i:
                    tile_pair(half, "out", i, half * ITERS + IT_OUT + i, lambda k: rt(A_Z, k), lambda k: rt(A_M, k))
                row_sums(half, "nf", 1)
                pe.wait_ge(split_ready, half * SP_ALL + SP_H2 + KT_D)
                ff_up(half, 0)
                ff_up(half, 1)
                with pe.Fori(0, FF_GROUPS // 2 - 1) as i:
                    for par in range(2):
                        ff_down(half, i * 2 + par, par)
                        ff_up(half, i * 2 + par + 2)
                ff_down(half, FF_GROUPS - 2, 0)
                ff_down(half, FF_GROUPS - 1, 1)
                row_sums(half, "ny", 2)

        @block.scalar
        def _(act):
            def evac(s, dst, func=ACT.Copy, **kw):
                for src, d in zip(psum_cols(s), cols(dst)):
                    last = act.activation(d, src, func, **kw)
                return last

            def block_used(half, place, it):
                act.wait_ge(w_used[place], half * ITERS + it + 1)

            def norm(half, n, stage, src, src_ready):
                for k in range(KT_D):
                    src_ready(k)
                    act.activation(ft(A_O, k), ft(src, k), ACT.Square).then_inc(sq_ready, 1)
                act.wait_ge(set_read[0], set_count(half, 0, stage, 1))
                act.activation(ft(A_G), ft(A_G), ACT.Sqrt).then_inc(std_ready, 1)

            def high_parts(half, first, count, src, dst):
                for k in range(count):
                    act.wait_ge(full_ready, full_count(half, first + k + 1))
                    act.activation(rt(dst, k), ft(src, k), ACT.Copy).then_inc(hi_ready, 1)

            def project(half):
                if half:
                    block_used(half - 1, 3, ITERS - 1)
                    act.wait_ge(ms_done, 3 * half)
                act.dma_start(fv(A_M, 8 * N), xT[half]).then_inc(x_landed, 16)
                act.wait_ge(x_landed, (half + 1) * 16)
                norm(half, 0, "nx", A_M, lambda k: None)
                if half:
                    act.wait_ge(y_stored, half * 16 * KT_D)
                high_parts(half, SP_X, KT_D, A_M, A_H)
                act.dma_start(fv(O_A, KT_D * P), wa).then_inc(wa_landed, 16)
                if half == 0:
                    act.wait_ge(split_ready, SP_X + KT_D)
                    act.dma_start(fv(A_G, 512), b_d).then_inc(bc_landed, 16)
                    act.dma_start(fv(A_G + 512, 512), c_d).then_inc(bc_landed, 16)
                up = fv(O_UP, KT_S * J * UC).rearrange("p (m j c) -> p m j c", m=KT_S, j=J)
                for m in range(KT_S):
                    s = m % 2
                    block_used(half, 2 * s + 1, IT_A + m // 2)
                    for b, (c0, cn) in enumerate(BLK):
                        pn = min(cn, TP - c0)
                        act.activation(up[:, m, :, c0 // J:(c0 + pn) // J],
                                       ps[:, 3 * s + b, 0:pn].rearrange("p (c j) -> p j c", j=J), ACT.Copy)
                    dec = ps[:, 3 * s + 2, TP - BLK[2][0]:N - BLK[2][0]].rearrange("p (q j) -> p j q", j=DEC_SEQ)
                    act.activation(up[:, m, 0:DEC_SEQ, NC:NC + DS], dec, ACT.Copy)
                    act.activation(up[:, m, DEC_SEQ:J, NC + DS:UC], dec, ACT.Copy).then_inc(set_read[s], 1)
                act.wait_ge(u_pad, 2 * (half + 1))
                act.wait_ge(set_read[0], set_count(half, 0, "a", 2))
                act.wait_ge(set_read[1], set_count(half, 1, "a", 2))
                act.dma_start(u_dram.rearrange("m p j c -> p m (j c)"),
                              fv(O_UP, KT_S * J * UC).rearrange("p (m n) -> p m n", m=KT_S)).then_inc(u_stored, 16)
                for m in range(KT_S, 12):
                    s = m % 2
                    block_used(half, 2 * s + 1, IT_A + m // 2)
                    evac(s, ft(A_Z, m - KT_S), scale=DK ** -0.5 if m < KT_S + 2 else 1.0).then_inc(set_read[s], 1)
                    if half == 0 and m == TABLES_OUT_AT:
                        s5_tables_out()
                act.wait_ge(low_done, half + 1)
                for src, d in zip([ps[0:RANK, 0, 0:352], ps[0:RANK, 1:3, 0:344]],
                                  cols(fa[0:RANK, O_A:O_A + N])):
                    last = act.activation(d, src, ACT.Copy)
                last.then_inc(low_ready, 1)

            def log_gates(half):
                for t in range(2):
                    act.wait_ge(gpre_done, half * 2 + t + 1)
                    evac(1 - t, ft(A_G, t), ACT.Identity, bias=vec[:, V_BG + t:V_BG + t + 1]
                         ).then_inc(set_read[1 - t], 1)
                    act.wait_ge(gmin_ready, half * 2 + t)
                    act.drain()
                    act.activation(ft(O_T), ft(A_G, t), ACT.Abs)
                    act.drain()
                    act.activation(ft(O_T), ft(O_T), ACT.Exp, scale=-1.0)
                    act.drain()
                    act.activation(ft(O_T), ft(O_T), ACT.Ln, bias=1.0).then_inc(gln_ready, 1)

            def s5_tables_out():
                act.wait_ge(qe_ready, 1)
                by_pair = c_dram.rearrange("t p c -> p t c")
                act.dma_start(by_pair[:, :, C_QR:C_QR + 2 * P],
                              fv(A_M, 4096).rearrange("p (t c) -> p t c", t=PAIRS)).then_inc(qe_stored, 16)
                act.dma_start(by_pair[:, :, C_EC:C_EC + 2 * EC],
                              fv(A_M + 4096, PAIRS * 2 * EC).rearrange("p (t c) -> p t c", t=PAIRS)).then_inc(qe_stored, 16)
                act.dma_start(fv(A_G, 1024), cbd_d).then_inc(cbd_landed, 16)

            def s5_pairs_out():
                by_pair = c_dram.rearrange("t p c -> p t c")
                for t in range(PAIRS):
                    act.wait_ge(tp_done, t + 1)
                    if t == STG:
                        act.wait_ge(tp_stored, 16)
                    act.activation(fv(O_STG_P + 256 * (t % STG), 256), ps[:, 4 + t % 2, 0:256], ACT.Copy
                                   ).then_inc(p_ready, 1)
                    if t % STG == STG - 1:
                        act.wait_ge(p_ready, t + 1)
                        act.dma_start(by_pair[:, t + 1 - STG:t + 1, C_PR:C_PR + 256],
                                      fv(O_STG_P, STG * 256).rearrange("p (t c) -> p t c", t=STG)).then_inc(tp_stored, 16)
                act.wait_ge(t_ready, J)
                act.dma_start(by_pair[:, :, C_T:C_T + 256],
                              fv(O_STG_T, PAIRS * 256).rearrange("p (t c) -> p t c", t=PAIRS)).then_inc(tp_stored, 16)
                act.wait_ge(tp_stored, 16 * 3)

            def s5(half):
                def load_consts(t, r):
                    src = c_dram[t] if isinstance(t, int) else c_dram[bass.ds(t, 1)].rearrange("o p c -> p (o c)")
                    act.dma_start(fv(C_SLOT[r], C_W), src).then_inc(c_landed[r], 16)

                act.wait_ge(u_stored, (half + 1) * 16)
                act.wait_ge(split_ready, half * SP_ALL + SP_X + KT_D)
                for j in range(J):
                    act.dma_start(fa[j * 16:(j + 1) * 16, M_U:M_U + S5_GROUPS * UC].rearrange("p (g c) -> p g c", c=UC),
                                  u_dram.rearrange("m (g h) j c -> j h (m g) c", h=S5_GROUP)[j]).then_inc(u_landed, 16)
                act.dma_start(s5_dec[:, :, :, :], s5dec_d[half]).then_inc(s5dec_landed, 16)
                act.wait_ge(b_ready, half + 1)
                for r in range(CR):
                    load_consts(r, r)

                def rows(i, r):
                    t = i * CR + r
                    act.wait_ge(yrow_done, half * PAIRS + t + 1)
                    act.activation(fa.at(O_UP, t * 2 * YC, 2 * YC).rearrange("p (g c) -> p g c", g=2),
                                   ps[:, 2 * (r % 2):2 * (r % 2) + 2, 0:YC], ACT.Copy).then_inc(yrow_read, 1)

                with act.Fori(0, PAIRS // CR - 1) as i:
                    for r in range(CR):
                        rows(i, r)
                        load_consts(i * CR + CR + r, r)
                for r in range(CR):
                    rows(PAIRS // CR - 1, r)
                act.wait_ge(yrow_read, (half + 1) * PAIRS)
                for j in range(J):
                    act.dma_start(y_dram.rearrange("m (g h) j c -> j h (m g) c", h=S5_GROUP)[j],
                                  fa[j * 16:(j + 1) * 16, O_UP:O_UP + S5_GROUPS * YC].rearrange("p (g c) -> p g c", c=YC)
                                  ).then_inc(yrow_stored, 16)
                act.wait_ge(yrow_stored, (half + 1) * 16 * J)
                act.dma_start(fv(O_UP, KT_S * J * YC).rearrange("p (m n) -> p m n", m=KT_S),
                              y_dram.rearrange("m p j c -> p m (j c)")).then_inc(yperm_landed, 16)
                act.wait_ge(s5dec_ready, half + 1)
                act.dma_start(s5_dec_out[half], s5_new[:, :, :, :]).then_inc(out_stored, 16)
                act.wait_ge(yperm_landed, (half + 1) * 16)
                yp = fv(O_UP, KT_S * J * YC).rearrange("p (m j c) -> p m j c", m=KT_S, j=J)
                for m in range(KT_S):
                    z = ft(A_M, m)
                    act.activation(z[:, 0:TP].rearrange("p (c j) -> p c j", j=J),
                                   yp[:, m, :, 0:NC].rearrange("p j c -> p c j"), ACT.Gelu_apprx_tanh)
                    act.activation(z[:, TP:N].rearrange("p (q j) -> p q j", j=DEC_SEQ),
                                   yp[:, m, 0:DEC_SEQ, NC:YC].rearrange("p j c -> p c j"),
                                   ACT.Gelu_apprx_tanh).then_inc(gelu_ready, 1)
                act.wait_ge(gelu_ready, (half + 1) * KT_S)
                for m in range(KT_S):
                    act.activation(rt(A_O, m), ft(A_M, m), ACT.Copy).then_inc(hi_ready, 1)
                for m in range(KT_S):
                    block_used(half, m, IT_GLU)
                    evac(m % 2, ft(A_M, 4 + m), ACT.Sigmoid).then_inc(set_read[m % 2], 1)
                high_parts(half, SP_O5, KT_S, A_M, A_O)
                act.wait_ge(split_ready, half * SP_ALL + SP_O5 + KT_S)
                with act.Fori(0, 2) as i:
                    for q in range(4):
                        block_used(half, (3 * q + 1) % RING, IT_M1 + i * 3 + (3 * q + 1) // RING)
                        evac(0, ft(A_M, i * 4 + q), ACT.Sigmoid).then_inc(set_read[0], 1)

            def gla_all(half):
                def stage(c, par, L):
                    src = fa[:, A_Z:A_Z + 8 * N].rearrange("p (k n) -> p k n", k=8)[:, :, bass.ds(c * C, L)]
                    act.activation(fv(O_ST[par], 8 * L).rearrange("p (k n) -> p k n", k=8), src, ACT.Copy
                                   ).then_inc(stage_ready, 1)

                def exps(n, par, dec):
                    act.wait_ge(diff_ready, n + 1)
                    de = O_DE[par]
                    spans = [(0, DE_W)]
                    if dec:
                        spans = [(l * 256, 2 * DT) for l in DEC_LEVELS] + [(DE_K, 2 * DT), (DE_Q, 2 * DT)]
                    for at, w in spans:
                        last = act.activation(fv(de + at, w), fv(de + at, w), ACT.Exp)
                    last.then_inc(exp_ready, 1)

                def rows_out(c, par):
                    L = DT if isinstance(c, int) and c == CHUNKS else C
                    n = n0 + c
                    act.wait_ge(vt_done, n + 1)
                    if not isinstance(c, int) or c >= 2:
                        act.wait_ge(o_done, n - 1)
                    act.activation(fa[0:L, O_VT[par]:O_VT[par] + 512], ps[0:L, 6, :], ACT.Copy).then_inc(vt_ready, 1)
                    act.wait_ge(kht_done, n + 1)
                    act.wait_ge(sup_done, n)
                    act.activation(khT[0:L, :], ps[0:L, 7, 0:256], ACT.Copy).then_inc(kht_ready, 1)

                def chunk(c, par):
                    dec = isinstance(c, int) and c == CHUNKS
                    L = DT if dec else C
                    n = n0 + c
                    last = isinstance(c, int) and c == CHUNKS - 2
                    ahead = not isinstance(c, int) or c + 2 <= CHUNKS
                    if not dec:
                        rows_out(c + 1, 1 - par)
                    if ahead:
                        act.wait_ge(level_done, n + 1)
                        stage(c + 2, par, DT if last else C)
                    act.wait_ge(o_done, n + 1)
                    v_cols = fa[:, A_Z + 4 * N:A_Z + 8 * N].rearrange("p (k n) -> p k n", k=4)[:, :, bass.ds(c * C, L)]
                    act.activation(v_cols.rearrange("p (t a) n -> p a t n", a=2),
                                   ps[:, 4:6, 256:256 + 2 * L].rearrange("p a (t n) -> p a t n", t=2), ACT.Copy
                                   ).then_inc(o_read, 1)
                    if ahead:
                        exps(n + 2, par, last)

                block_used(half, 3, IT_M1 + 5)
                n0 = half * (CHUNKS + 1)
                for c in range(2):
                    stage(c, c, C)
                    exps(n0 + c, c, False)
                rows_out(0, 0)
                for par in range(2):
                    chunk(par, par)
                with act.Fori(1, CHUNKS // 2 - 1) as i:
                    for par in range(2):
                        chunk(i * 2 + par, par)
                chunk(CHUNKS - 2, 0)
                chunk(CHUNKS - 1, 1)
                act.dma_start(fv(O_S0, DS * 2 * DV), gladec_d[half]).then_inc(s0_landed, 16)
                chunk(CHUNKS, 0)
                act.wait_ge(s0_ready, half + 1)
                act.dma_start(gla_dec_out[half], fv(O_S0, DS * 2 * DV)).then_inc(out_stored, 16)
                act.wait_ge(out_stored, (half + 1) * 32)
                act.wait_ge(o_read, (half + 1) * (CHUNKS + 1))
                for h in range(HEADS):
                    act.activation(ft(A_O, h), ft(A_Z, 4 + h), ACT.Square).then_inc(osq_ready, 1)
                for h in range(HEADS):
                    block_used(half, 2 * (h % 2) + 1, IT_R + h // 2)
                    if h:
                        act.wait_ge(full_ready, full_count(half, SP_OG + h))
                    evac(0, ft(A_G, 0), ACT.Silu).then_inc(set_read[0], 1)
                    act.wait_ge(set_read[1], set_count(half, 1, "r", h + 1))
                    act.activation(ft(A_G, 1), ft(A_G, 1), ACT.Sqrt).then_inc(gstd_ready, 1)
                    act.wait_ge(full_ready, full_count(half, SP_OG + h + 1))
                    act.activation(rt(A_O, h), ft(A_Z, 4 + h), ACT.Copy).then_inc(hi_ready, 1)
                act.wait_ge(split_ready, half * SP_ALL + SP_OG + HEADS)
                with act.Fori(0, 2) as i:
                    for q in range(4):
                        block_used(half, (3 * q + 1) % RING, IT_M2 + i * 3 + (3 * q + 1) // RING)
                        evac(0, ft(A_G, q % 2), ACT.Sigmoid).then_inc(set_read[0], 1)
                        act.wait_ge(full_ready, full_count(half, SP_MG + i * 4 + q + 1))
                        act.activation(rt(A_Z, i * 4 + q), ft(A_M, i * 4 + q), ACT.Copy).then_inc(hi_ready, 1)

            def out_and_ff(half):
                block_used(half, 3, IT_M2 + 5)
                act.dma_start(fv(A_H, 8 * N), xT[half]).then_inc(res_landed, 16)
                norm(half, 1, "nf", A_H,
                     lambda k: act.wait_ge(set_read[k % 2], set_count(half, k % 2, "out", k // 2 + 1)))
                high_parts(half, SP_H2, KT_D, A_M, A_Z)

                def hidden(g, par):
                    for q in range(4):
                        block_used(half, 2 * (q % 2) + 1, IT_FF + ff_it(g, "up") + q // 2)
                        before = max(4 * g + q - 1, 0) if isinstance(g, int) else 4 * g + q - 1
                        act.wait_ge(hidden_split, half * FF_GROUPS * 4 + before)
                        evac(q % 2, ft(A_G, q % 2), ACT.Relu).then_inc(set_read[q % 2], 1)
                        act.drain()
                        act.activation(rt(A_H + 8 * N if par == 0 else A_O, q), ft(A_G, q % 2), ACT.Square
                                       ).then_inc(hidden_hi, 1)

                act.wait_ge(split_ready, (half + 1) * SP_ALL)
                hidden(0, 0)
                hidden(1, 1)
                with act.Fori(0, FF_GROUPS // 2 - 1) as i:
                    for par in range(2):
                        hidden(i * 2 + par + 2, par)

                def x2_there(k):
                    if k == 0:
                        act.wait_ge(set_read[0], set_count(half, 0, "ny", 0))
                        act.wait_ge(set_read[1], set_count(half, 1, "ny", 0))
                norm(half, 2, "ny", A_H, x2_there)
                for k in range(KT_D):
                    act.wait_ge(y_ready, half * KT_D + k + 1)
                    act.dma_start(yT[half, :, k * N:(k + 1) * N], ft(A_H, k)).then_inc(y_stored, 16)

            for dst, src in consts:
                act.dma_start(dst, src).then_inc(const_landed, 16)
            act.dma_start(sml[:, 0:3, :], s5small).then_inc(s5in_landed, 16)
            act.wait_ge(s5in_landed, 16)
            act.activation(small("dt"), small("logdt"), ACT.Exp).then_inc(dt_ready, 1)
            act.wait_ge(const_landed, 16 * len(consts))
            act.wait_ge(trig_in, 1)
            act.activation(small("mag"), small("lrdt"), ACT.Exp)
            act.activation(small("sin"), small("ang"), ACT.Sin)
            act.activation(small("sinh"), small("ang"), ACT.Sin, scale=0.5).then_inc(trig_out, 1)
            for half in range(HALVES):
                project(half)
                if half == 0:
                    s5_pairs_out()
                log_gates(half)
                s5(half)
                gla_all(half)
                out_and_ff(half)
            act.dma_start(s5_prompt, s5_carry[:, :, :]).then_inc(out_stored, 16)
            act.dma_start(gla_prompt, gla_s[:, 0, :, :]).then_inc(out_stored, 16)
            act.wait_ge(out_stored, 16 * (2 * HALVES + 2))
            act.wait_ge(y_stored, 16 * HALVES * KT_D)

        @block.vector
        def _(dve):
            def tt(out, a, b, op):
                return dve.tensor_tensor(out, a, b, op)

            def block_used(half, place, it):
                dve.wait_ge(w_used[place], half * ITERS + it + 1)

            def low_part(half, n, full, hi, lo):
                dve.wait_ge(hi_ready, half * SP_ALL + n + 1)
                tt(lo, full, hi, ALU.subtract).then_inc(split_ready, 1)

            def mean_square(s, dst, width):
                for src, d in zip(psum_cols(s), cols(dst)):
                    last = dve.tensor_scalar(d, src, 1.0 / width, EPS, ALU.mult, ALU.add)
                last.then_inc(set_read[s], 1)

            def norm(half, n, src, full, gain, each):
                for k in range(KT_D):
                    dve.wait_ge(sq_ready, (half * 3 + n) * KT_D + k + 1)
                    if k:
                        dve.drain()
                        last = tt(ft(A_O), ft(A_O), ft(A_O, k), ALU.add)
                last.then_inc(ssum_ready, 1)
                dve.wait_ge(ms_done, half * 3 + n + 1)
                mean_square(0, ft(A_G), D_MODEL)
                dve.wait_ge(std_ready, half * 3 + n + 1)
                dve.reciprocal(ft(A_G), ft(A_G))
                dve.drain()
                for k in range(KT_D):
                    last = dve.scalar_tensor_tensor(ft(full, k), ft(src, k), vec[:, gain + k:gain + k + 1], ft(A_G),
                                                    ALU.mult, ALU.mult)
                    last.then_inc(full_ready if n < 2 else y_ready, 1)
                    if k:
                        each(k - 1)
                each(KT_D - 1)

            def trig():
                s = small
                dve.wait_ge(dt_ready, 1)
                steps = [
                    lambda: dve.tensor_scalar(s("lr"), s("lam_re"), -1e-4, None, ALU.min),
                    lambda: tt(s("lrdt"), s("lr"), s("dt"), ALU.mult),
                    lambda: tt(s("th"), s("lam_im"), s("dt"), ALU.mult),
                    lambda: dve.tensor_scalar(s("t0"), s("th"), float(0.5 / np.pi), MAGIC, ALU.mult, ALU.add),
                    lambda: dve.tensor_scalar(s("t0"), s("t0"), MAGIC, None, ALU.subtract),
                    lambda: dve.scalar_tensor_tensor(s("th"), s("t0"), -PI2_1, s("th"), ALU.mult, ALU.add),
                    lambda: dve.scalar_tensor_tensor(s("th"), s("t0"), -PI2_2, s("th"), ALU.mult, ALU.add),
                    lambda: dve.scalar_tensor_tensor(s("th"), s("t0"), -PI2_3, s("th"), ALU.mult, ALU.add),
                ]
                for f in steps:
                    f()
                    dve.drain()
                dve.tensor_scalar(s("ang"), s("th"), 3.1415925, -3.1415925, ALU.min, ALU.max).then_inc(trig_in, 1)
                dve.wait_ge(trig_out, 1)

                def seq(*ops):
                    for out, a, b, op in ops:
                        tt(out, a, b, op)
                        dve.drain()
                seq((s("t0"), s("sinh"), s("sinh"), ALU.mult))
                dve.tensor_scalar(s("cos"), s("t0"), -2.0, 1.0, ALU.mult, ALU.add)
                dve.drain()
                seq((s("ar"), s("mag"), s("cos"), ALU.mult), (s("ai"), s("mag"), s("sin"), ALU.mult),
                    (s("t0"), s("lr"), s("lr"), ALU.mult), (s("t1"), s("lam_im"), s("lam_im"), ALU.mult),
                    (s("t0"), s("t0"), s("t1"), ALU.add))
                dve.reciprocal(s("t0"), s("t0"))
                dve.tensor_scalar(s("t1"), s("ar"), -1.0, None, ALU.add)
                dve.drain()
                seq((s("fr"), s("t1"), s("lr"), ALU.mult), (s("t2"), s("ai"), s("lam_im"), ALU.mult),
                    (s("fr"), s("fr"), s("t2"), ALU.add), (s("fr"), s("fr"), s("t0"), ALU.mult),
                    (s("fi"), s("ai"), s("lr"), ALU.mult), (s("t2"), s("t1"), s("lam_im"), ALU.mult),
                    (s("fi"), s("fi"), s("t2"), ALU.subtract), (s("fi"), s("fi"), s("t0"), ALU.mult))
                pr, pi = (lambda k: sml[:, SMALL.index("pr") + k, :]), (lambda k: sml[:, SMALL.index("pi") + k, :])
                dve.memset(pr(0), 1.0)
                dve.memset(pi(0), 0.0)
                dve.drain()
                for k in range(J):
                    seq((s("t0"), pr(k), s("ar"), ALU.mult), (s("t1"), pi(k), s("ai"), ALU.mult),
                        (pr(k + 1), s("t0"), s("t1"), ALU.subtract),
                        (s("t0"), pr(k), s("ai"), ALU.mult), (s("t1"), pi(k), s("ar"), ALU.mult),
                        (pi(k + 1), s("t0"), s("t1"), ALU.add))
                for q, p4 in ((0, pr(4)), (1, pi(4))):
                    dve.tensor_copy(s5_a4[:, q, :], p4)
                seq((s5_m8[:, :], s("mag"), s("mag"), ALU.mult), (s5_m8[:, :], s5_m8[:, :], s5_m8[:, :], ALU.mult),
                    (s5_m8[:, :], s5_m8[:, :], s5_m8[:, :], ALU.mult))
                for _ in range(3):
                    square_phasor(s("cos"), s("sin"), s("cos"), s("sin"))

            def square_phasor(oc, os_, c, s_):
                t0, t1, t2 = small("t0"), small("t1"), small("t2")
                for out, a, b, op in ((t0, c, c, ALU.mult), (t1, s_, s_, ALU.mult), (t2, c, s_, ALU.mult),
                                      (t0, t0, t1, ALU.subtract)):
                    tt(out, a, b, op)
                    dve.drain()
                dve.tensor_scalar(t1, t2, 2.0, None, ALU.mult)
                dve.drain()
                tt(t2, t0, t0, ALU.mult)
                dve.drain()
                tt(small("t3"), t1, t1, ALU.mult)
                dve.drain()
                tt(t2, t2, small("t3"), ALU.add)
                dve.drain()
                dve.tensor_scalar(t2, t2, -0.5, 1.5, ALU.mult, ALU.add)
                dve.drain()
                tt(oc, t0, t2, ALU.mult)
                tt(os_, t1, t2, ALU.mult)
                dve.drain()

            def cmul(o_re, o_im, a_re, a_im, b_re, b_im, t0, t1, conj_sum=False):
                tt(t0, a_re, b_re, ALU.mult)
                tt(t1, a_im, b_im, ALU.mult)
                dve.drain()
                tt(o_re, t0, t1, ALU.subtract)
                dve.drain()
                tt(t0, a_re, b_im, ALU.mult)
                tt(t1, a_im, b_re, ALU.mult)
                dve.drain()
                tt(o_im, t0, t1, ALU.add)
                dve.drain()

            def s5_tables():
                pr, pi = (lambda k: sml[:, SMALL.index("pr") + k, :]), (lambda k: sml[:, SMALL.index("pi") + k, :])

                def g3(at):
                    return fv(at, 256).rearrange("p (t h) -> p t h", t=PAIRS)

                def over_h(a):
                    return a.unsqueeze(2).to_broadcast([P, PAIRS, S5_GROUP])
                b_re, b_im, c_re, c_im = (g3(A_G + 256 * q) for q in range(4))
                bb_re, bb_im, t0, t1 = (g3(A_G + 1024 + 256 * q) for q in range(4))
                dve.wait_ge(bc_landed, 32)
                cmul(bb_re, bb_im, over_h(small("fr")), over_h(small("fi")), b_re, b_im, t0, t1)
                q_all = fv(A_M, 4096).rearrange("p (t q j h) -> p t q j h", t=PAIRS, q=2, j=J)
                for j in range(J):
                    cmul(q_all[:, :, 0, j, :], q_all[:, :, 1, j, :], over_h(pr(j + 1)), over_h(pi(j + 1)),
                         c_re, c_im, t0, t1)
                    dve.tensor_scalar(q_all[:, :, 1, j, :], q_all[:, :, 1, j, :], -1.0, None, ALU.mult)
                e = fv(A_M + 4096, PAIRS * 2 * EC).rearrange("p (t q c) -> p t q c", t=PAIRS, q=2)
                dve.memset(e[:, :, 0, 0:1], 1.0)
                dve.memset(e[:, :, 1, 0:1], 0.0)
                cc, ss = small("cos"), small("sin")
                tmp = [fv(O_TAB + TAB_W * PAIRS * q, TAB_W * PAIRS) for q in range(2)]
                n = 1
                while n <= NC:
                    dve.tensor_copy(e[:, :, 0, n:n + 1], cc.unsqueeze(2))
                    dve.tensor_copy(e[:, :, 1, n:n + 1], ss.unsqueeze(2))
                    dve.drain()
                    for a in range(1, min(n, NC + 1 - n), TAB_W):
                        m = min(TAB_W, min(n, NC + 1 - n) - a)
                        wc, ws = (x.unsqueeze(2).to_broadcast([P, PAIRS, m]) for x in (cc, ss))
                        t0w, t1w = (x[:, 0:PAIRS * m].rearrange("p (t m) -> p t m", t=PAIRS) for x in tmp)
                        cmul(e[:, :, 0, n + a:n + a + m], e[:, :, 1, n + a:n + a + m], wc, ws,
                             e[:, :, 0, a:a + m], e[:, :, 1, a:a + m], t0w, t1w)
                    n *= 2
                    if n <= NC:
                        square_phasor(cc, ss, cc, ss)
                dve.memset(e[:, :, :, NC + 1:EC], 0.0).then_inc(qe_ready, 1)
                dve.wait_ge(qe_stored, 32)
                g_re, g_im = (fv(A_M + 3840 * q, 3840).rearrange("p (t s h) -> p t s h", t=PAIRS, s=15)
                              for q in range(2))
                dve.memset(fv(A_M, 2 * 3840), 0.0)
                dve.drain()
                for s in range(J):
                    cmul(g_re[:, :, s, :], g_im[:, :, s, :], over_h(pr(J - 1 - s)), over_h(pi(J - 1 - s)),
                         bb_re, bb_im, t0, t1)
                dve.wait_ge(cbd_landed, 16)
                dve.tensor_scalar(fv(A_G + 512, 512), fv(A_G + 512, 512), -1.0, None, ALU.mult).then_inc(g_ready, 1)

            def s5_pairs():
                dve.tensor_copy(fv(O_SHIFT, P), ident[:, :])
                dve.memset(fv(O_SHIFT + P, P), 0.0)
                def by_group(at):
                    return fv(at, 512).rearrange("p (g h) -> p g h", h=S5_GROUP)
                tt(by_group(G_SKIP), ident[:, P - S5_GROUP:P].unsqueeze(1).to_broadcast([P, S5_GROUPS, S5_GROUP]),
                   dcol[:, :].unsqueeze(2).to_broadcast([P, S5_GROUPS, S5_GROUP]), ALU.mult)
                dve.drain()
                dve.wait_ge(k_done, 1)
                tt(fv(G_K, 512), ps[:, 0, 0:512], fv(G_SKIP, 512), ALU.add).then_inc(k_ready, 1)
                dve.wait_ge(u_stored, 16)
                for j in range(J):
                    dve.wait_ge(shift_done, j + 1)
                    out = fv(O_STG_T, PAIRS * 256).rearrange("p (g j h) -> p g j h", g=S5_GROUPS, j=J)[:, :, j, :]
                    dve.tensor_copy(out, ps[:, j % 4, 0:512].rearrange("p (g h) -> p g h", h=S5_GROUP)
                                    ).then_inc(t_ready, 1)

            def s5(half):
                T = [M_TMP + 130 * q for q in range(4)]
                W = [M_TMP + 520 + 130 * q for q in range(2)]

                def pair(i, r):
                    t = i * CR + r
                    st = M_TMP + 800 + (r % 2) * 2 * YC
                    at = C_SLOT[r]

                    def ec(a, n):
                        return fv(at + C_EC + a, n)

                    def es(a, n):
                        return fv(at + C_ES + a, n)
                    col = (lambda q: s5_carry[:, q, t:t + 1]) if isinstance(t, int) else (
                        lambda q: s5_carry[:, q, bass.ds(t, 1)])
                    dve.wait_ge(chunk_in_done, half * PAIRS + t + 1)
                    xr, xi = ps[:, 6 + r % 2, 0:NC], ps[:, 6 + r % 2, UC:UC + NC]
                    tt(fv(T[0], NC), ec(1, NC), xr, ALU.mult)
                    tt(fv(T[1], NC), es(1, NC), xi, ALU.mult)
                    tt(fv(T[2], NC), ec(1, NC), xi, ALU.mult)
                    tt(fv(T[3], NC), es(1, NC), xr, ALU.mult)
                    dx = ps[:, 6 + r % 2, 0:2 * UC].rearrange("p (q c) -> p q c", q=2)[:, :, NC + DS:UC]
                    tb = bass.ds(t, 1)
                    dve.tensor_copy(s5_new[:, :, tb, :].rearrange("p q o s -> p q (o s)"), dx
                                    ).then_inc(chunk_in_read, 1)
                    for q in range(2):
                        dve.tensor_copy(fv(W[q], 1), col(q))
                    dve.drain()
                    tt(fv(T[0], NC), fv(T[0], NC), fv(T[1], NC), ALU.add)
                    tt(fv(T[2], NC), fv(T[2], NC), fv(T[3], NC), ALU.subtract)
                    dve.drain()
                    m8 = s5_m8[:, bass.ds(t, 1)].to_broadcast([P, NC])
                    for q in range(2):
                        dve.tensor_tensor_scan(fv(W[q] + 1, NC), m8, fv(T[2 * q], NC), fv(W[q], 1), ALU.mult, ALU.add)
                    dve.drain()
                    tt(fv(T[0], NC + 1), ec(0, NC + 1), fv(W[0], NC + 1), ALU.mult)
                    tt(fv(T[1], NC + 1), es(0, NC + 1), fv(W[1], NC + 1), ALU.mult)
                    tt(fv(T[2], NC + 1), es(0, NC + 1), fv(W[0], NC + 1), ALU.mult)
                    tt(fv(T[3], NC + 1), ec(0, NC + 1), fv(W[1], NC + 1), ALU.mult)
                    dve.drain()
                    dve.wait_ge(yrow_done, half * PAIRS + (max(t - 1, 0) if isinstance(t, int) else t - 1))
                    for q, op in ((0, ALU.subtract), (1, ALU.add)):
                        tt(col(q), fv(T[2 * q] + NC, 1), fv(T[2 * q + 1] + NC, 1), op)
                        dve.tensor_copy(fv(st + q * YC + NC, DS), s5_dec[:, q, tb, :].rearrange("p o s -> p (o s)"))
                        last = tt(fv(st + q * YC, NC), fv(T[2 * q], NC), fv(T[2 * q + 1], NC), op)
                    last.then_inc(state_ready, 1)
                    dve.drain()

                dve.wait_ge(s5dec_landed, (half + 1) * 16)
                if half == 0:
                    dve.memset(s5_carry[:, :, :], 0.0)
                    dve.drain()
                else:
                    dve.wait_ge(out_stored, 32)
                for r in range(CR):
                    pair(0, r)
                with dve.Fori(1, PAIRS // CR) as i:
                    for r in range(CR):
                        pair(i, r)

                def wide(q):
                    return s5_a4[:, q, :].unsqueeze(2).to_broadcast([P, PAIRS, DS])
                dre, dim = s5_dec[:, 0, :, :], s5_dec[:, 1, :, :]
                nre, nim = s5_new[:, 0, :, :], s5_new[:, 1, :, :]
                t0, t1 = s5_tmp[:, 0, :, :], s5_tmp[:, 1, :, :]
                tt(t0, wide(0), dre, ALU.mult)
                tt(t1, wide(1), dim, ALU.mult)
                dve.drain()
                tt(nre, nre, t0, ALU.add)
                dve.drain()
                tt(nre, nre, t1, ALU.subtract)
                tt(t0, wide(0), dim, ALU.mult)
                dve.drain()
                tt(t1, wide(1), dre, ALU.mult)
                tt(nim, nim, t0, ALU.add)
                dve.drain()
                tt(nim, nim, t1, ALU.add).then_inc(s5dec_ready, 1)

            def gla_all(half):
                def halves(ap, s):
                    v = ap.rearrange("p t (b two s) -> p t b two s", two=2, s=s)
                    return v[:, :, :, 0, :], v[:, :, :, 1, :]

                def two(at, L):
                    return fv(at, 2 * L).rearrange("p (t n) -> p t n", t=2)

                def levels(dec):
                    return DEC_LEVELS if dec else range(NL)

                def log_sums(c, L):
                    return fa[:, A_G:A_G + 2 * N].rearrange("p (t n) -> p t n", t=2)[:, :, bass.ds(c * C, L)]

                def diffs(c, par, dec, some=None):
                    L = DT if dec else C
                    for l in (levels(dec) if some is None else some):
                        s = LEVELS[l]
                        bl, br = halves(log_sums(c, L), s)
                        mid = bl[:, :, :, s - 1:s].to_broadcast([P, 2, L // (2 * s), s])
                        left, right = halves(two(O_DE[par] + l * 256, L), s)
                        tt(right, br, mid, ALU.subtract)
                        tt(left, mid, bl, ALU.subtract)

                def end_diffs(c, par, dec):
                    L = DT if dec else C
                    w = DEC_SEQ if dec else C
                    b = log_sums(c, L)
                    bb = b.rearrange("p t (b s) -> p t b s", s=w)
                    tt(two(O_DE[par] + DE_K, L).rearrange("p t (b s) -> p t b s", s=w),
                       bb[:, :, :, w - 1:w].to_broadcast([P, 2, L // w, w]), bb, ALU.subtract)
                    dve.tensor_copy(two(O_DE[par] + DE_Q, L), b).then_inc(diff_ready, 1)

                def products(c, par, dec):
                    L = DT if dec else C
                    n, de = n0 + c, O_DE[par]
                    q, k = two(O_ST[par], L), two(O_ST[par] + 2 * L, L)
                    dve.wait_ge(exp_ready, n + 1)
                    dve.wait_ge(stage_ready, n + 1)
                    w = DEC_SEQ if dec else C
                    dve.tensor_copy(decay[:, par, 0:2 * L // w],
                                    fv(de + DE_Q, 2 * L).rearrange("p (b s) -> p b s", s=w)[:, :, w - 1])
                    dve.drain()
                    for l in levels(dec):
                        left, right = halves(two(de + l * 256, L), LEVELS[l])
                        tt(right, right, halves(q, LEVELS[l])[1], ALU.mult)
                        tt(left, left, halves(k, LEVELS[l])[0], ALU.mult)
                    tt(two(de + DE_Q, L), two(de + DE_Q, L), q, ALU.mult)
                    tt(two(de + DE_K, L), two(de + DE_K, L), k, ALU.mult).then_inc(mul_ready, 1)

                def weights(dec, some, diagonal):
                    L = DT if dec else C
                    mk = dmask if dec else masks
                    att = fa[0:L, O_ATT:O_ATT + 4 * L]
                    for l in some:
                        s, x = LEVELS[l], list(levels(dec)).index(l)
                        out = att.rearrange("p (a b two s) -> p a b two s", a=2, two=2, s=s)[:, :, :, 1, :]
                        m = mk[0:L, x * 2 * L:(x + 1) * 2 * L].rearrange("p (a b s) -> p a b s", a=2, s=s)
                        bank, col = 2 * (l * 128 // 512), l * 128 % 512
                        src = ps[0:L, bank:bank + 2, col:col + L].rearrange("p a (b s) -> p a b s", s=s)
                        dve.copy_predicated(out, m, src)
                        dve.drain()
                    if diagonal:
                        x = len(levels(dec)) * 2 * L
                        dve.copy_predicated(att.rearrange("p (a n) -> p a n", a=2),
                                            mk[0:L, x:x + 4 * L].rearrange("p (a n) -> p a n", a=2),
                                            ps[0:L, 4:6, 0:2 * L]).then_inc(att_ready, 1)

                block_used(half, 3, IT_M1 + 5)
                dve.memset(fv(O_ATT, HEADS * C), 0.0)
                if half == 0:
                    dve.memset(gla_s[:, 0, :, :], 0.0).then_inc(s_ready, 1)
                n0 = half * (CHUNKS + 1)
                for c in range(2):
                    diffs(c, c, False)
                    end_diffs(c, c, False)
                products(0, 0, False)

                def chunk(c, par):
                    n = n0 + c
                    known = isinstance(c, int)
                    products(c + 1, 1 - par, known and c == CHUNKS - 1)
                    dve.drain()
                    dve.wait_ge(o_done, n)
                    dve.wait_ge(sup_done, n + 1)
                    dve.wait_ge(level_a_done, half * CHUNKS + c + 1)
                    for t in range(2):
                        ins = dve.scalar_tensor_tensor(gla_s[:, 1 - par, t, :], gla_s[:, par, t, :],
                                                       decay[:, par, t:t + 1],
                                                       ps[:, 7, 256 + t * DV:256 + (t + 1) * DV], ALU.mult, ALU.add)
                    ins.then_inc(s_ready, 1)
                    weights(False, range(NL_A), False)
                    dve.wait_ge(level_done, n + 1)
                    ahead, dec = not known or c + 2 <= CHUNKS, known and c + 2 == CHUNKS
                    if ahead:
                        diffs(c + 2, par, dec, [NL - 1])
                    weights(False, range(NL_A, NL), True)
                    if ahead:
                        diffs(c + 2, par, dec, list(levels(dec))[:-1])
                        dve.wait_ge(o_done, n + 1)
                        end_diffs(c + 2, par, dec)

                for par in range(2):
                    chunk(par, par)
                with dve.Fori(1, CHUNKS // 2 - 1) as i:
                    for par in range(2):
                        chunk(i * 2 + par, par)
                chunk(CHUNKS - 2, 0)
                chunk(CHUNKS - 1, 1)
                n = n0 + CHUNKS
                dve.wait_ge(o_done, n)
                dve.wait_ge(level_done, n + 1)
                dve.memset(fv(O_ATT, HEADS * C), 0.0)
                dve.drain()
                weights(True, DEC_LEVELS, True)
                dve.wait_ge(kht_ready, n + 1)
                for s in range(DS):
                    ins = dve.tensor_scalar(fa[0:DT, O_KTM + s * 256:O_KTM + (s + 1) * 256], khT[0:DT, :],
                                            vec[0:DT, V_SEQ + s:V_SEQ + s + 1], None, ALU.mult)
                ins.then_inc(ktm_ready, 1)
                dve.wait_ge(sup_done, n + 1)
                for s in range(DS):
                    for t in range(2):
                        col = (s * 2 + t) * DV
                        ins = dve.scalar_tensor_tensor(fv(O_S0 + col, DV), fv(O_S0 + col, DV),
                                                       decay[:, 0, t * DS + s:t * DS + s + 1],
                                                       ps[:, col // 512, col % 512:col % 512 + DV], ALU.mult, ALU.add)
                ins.then_inc(s0_ready, 1)

            def merge(half):
                for h in range(HEADS):
                    dve.wait_ge(gms_done, half * HEADS + h + 1)
                    dve.drain()
                    mean_square(1, ft(A_G, 1), DV)
                    dve.wait_ge(gstd_ready, half * HEADS + h + 1)
                    dve.reciprocal(ft(A_G, 1), ft(A_G, 1))
                    dve.drain()
                    z = ft(A_Z, 4 + h)
                    dve.scalar_tensor_tensor(z, z, vec[:, V_GLA:V_GLA + 1], ft(A_G, 1), ALU.mult, ALU.mult)
                    dve.wait_ge(set_read[0], set_count(half, 0, "r", h + 1))
                    dve.drain()
                    tt(z, z, ft(A_G, 0), ALU.mult).then_inc(full_ready, 1)
                    low_part(half, SP_OG + h, z, hf(A_O, h), rt(A_O, 4 + h))
                with dve.Fori(0, 2) as i:
                    for q in range(4):
                        m = i * 4 + q
                        dve.wait_ge(set_read[0], set_count(half, 0, "m2", m + 1))
                        block_used(half, (3 * q + 2) % RING, IT_M2 + i * 3 + (3 * q + 2) // RING)
                        g = ft(A_G, q % 2)
                        for src, d in zip(psum_cols(1), cols(g)):
                            last = tt(d, d, src, ALU.mult)
                        last.then_inc(set_read[1], 1)
                        dve.drain()
                        tt(ft(A_M, m), ft(A_M, m), g, ALU.add).then_inc(full_ready, 1)
                        low_part(half, SP_MG + m, ft(A_M, m), hf(A_Z, m), rt(A_M, m))

            def add_tile(s, dst):
                for src, d in zip(psum_cols(s), cols(dst)):
                    last = tt(d, d, src, ALU.add)
                last.then_inc(set_read[s], 1)

            def hidden(half, g, par):
                for q in range(4):
                    dve.wait_ge(hidden_hi, half * FF_GROUPS * 4 + 4 * g + q + 1)
                    r, hb = ft(A_G, q % 2), A_H + 8 * N if par == 0 else A_O
                    tt(r, r, r, ALU.mult)
                    dve.drain()
                    tt(rt(hb, 4 + q), r, hf(hb, q), ALU.subtract).then_inc(hidden_split, 1)

            def outputs(half, g):
                for m in range(KT_D):
                    block_used(half, m % RING, IT_FF + ff_it(g, "down") + m // RING)
                    add_tile(m % 2, ft(A_H, m))

            dve.memset(ones[:, :], 1.0).then_inc(ones_ready, 1)
            trig()
            dve.wait_ge(const_landed, 16 * len(consts))
            dve.tensor_copy(masks[:, :], fv(A_Z, NL * 256 + 512))
            dve.tensor_copy(dmask[:, :], fa[0:DT, A_Z + 4096:A_Z + 4096 + dmask.shape[1]])
            for half in range(HALVES):
                norm(half, 0, A_M, A_M, V_MIX,
                     lambda k: low_part(half, SP_X + k, ft(A_M, k), hf(A_H, k), rt(A_H, 8 + k)))
                up = fv(O_UP, KT_S * J * UC).rearrange("p (m j c) -> p m j c", m=KT_S, j=J)
                dve.memset(up[:, :, DEC_SEQ:J, NC:NC + DS], 0.0).then_inc(u_pad, 1)
                dve.memset(up[:, :, 0:DEC_SEQ, NC + DS:UC], 0.0).then_inc(u_pad, 1)
                dve.wait_ge(wa_landed, (half + 1) * 16)
                dve.tensor_copy(ra[:, O_AH:O_AH + KT_D * P], fv(O_A, KT_D * P))
                dve.drain()
                tt(ra[:, O_AL:O_AL + KT_D * P], fv(O_A, KT_D * P), ra[:, O_AH:O_AH + KT_D * P].bitcast(F32), ALU.subtract
                   ).then_inc(wa_split, 1)
                if half == 0:
                    s5_tables()
                    s5_pairs()
                for t in range(2):
                    dve.wait_ge(gln_ready, half * 2 + t + 1)
                    g = ft(A_G, t)
                    dve.scalar_tensor_tensor(g, g, 0.0, ft(O_T), ALU.min, ALU.subtract).then_inc(gmin_ready, 1)
                    dve.drain()
                    dve.tensor_scalar(g, g, 1.0 / TAU, None, ALU.mult)
                    dve.drain()
                    spans = [(c * C, C) for c in range(CHUNKS)] + [(TP + s * DEC_SEQ, DEC_SEQ) for s in range(DS)]
                    for a, w in spans:
                        last = dve.tensor_tensor_scan(g[:, a:a + w], ones[:, 0:w], g[:, a:a + w], 0.0,
                                                      ALU.mult, ALU.add)
                last.then_inc(b_ready, 1)
                s5(half)
                for m in range(KT_S):
                    low_part(half, SP_Z5 + m, ft(A_M, m), hf(A_O, m), rt(A_O, 4 + m))
                for m in range(KT_S):
                    dve.wait_ge(set_read[m % 2], set_count(half, m % 2, "glu", m // 2 + 1))
                    tt(ft(A_M, m), ft(A_M, m), ft(A_M, 4 + m), ALU.mult).then_inc(full_ready, 1)
                for m in range(KT_S):
                    low_part(half, SP_O5 + m, ft(A_M, m), hf(A_O, m), rt(A_O, 4 + m))
                with dve.Fori(0, 2) as i:
                    for q in range(4):
                        m = i * 4 + q
                        dve.wait_ge(set_read[0], set_count(half, 0, "m1", m + 1))
                        block_used(half, (3 * q + 2) % RING, IT_M1 + i * 3 + (3 * q + 2) // RING)
                        for src, d in zip(psum_cols(1), cols(ft(A_M, m))):
                            last = tt(d, d, src, ALU.mult)
                        last.then_inc(set_read[1], 1)
                gla_all(half)
                merge(half)
                dve.wait_ge(res_landed, (half + 1) * 16)
                for m in range(KT_D):
                    block_used(half, 2 * (m % 2) + 1, IT_OUT + m // 2)
                    add_tile(m % 2, ft(A_H, m))
                norm(half, 1, A_H, A_M, V_FFN,
                     lambda k: low_part(half, SP_H2 + k, ft(A_M, k), hf(A_Z, k), rt(A_M, k)))
                hidden(half, 0, 0)
                hidden(half, 1, 1)
                with dve.Fori(0, FF_GROUPS // 2 - 1) as i:
                    for par in range(2):
                        outputs(half, i * 2 + par)
                        hidden(half, i * 2 + par + 2, par)
                outputs(half, FF_GROUPS - 2)
                outputs(half, FF_GROUPS - 1)
                norm(half, 2, A_H, A_H, V_FIN, lambda k: None)


SMALL = (["lam_re", "lam_im", "logdt", "dt", "lr", "lrdt", "th", "ang", "mag", "sin", "sinh", "cos", "ar", "ai",
          "t0", "t1", "t2", "t3", "fr", "fi"] + ["pr"] + ["pr_"] * J + ["pi"] + ["pi_"] * J)


def lay_out(a):
    f = np.float32

    def halves(prompt, sample):
        xp = prompt.reshape(HALVES, TP, D_MODEL)
        xs = sample.reshape(HALVES, DT, D_MODEL)
        x = np.concatenate([xp, xs], axis=1)
        x = x.reshape(HALVES, N, KT_D, P).transpose(0, 3, 2, 1)
        return np.ascontiguousarray(x.reshape(HALVES, P, KT_D * N))

    def tile_blocks(w):
        k, m = w.shape[0] // P, w.shape[1] // P
        w = w.reshape(k // 4, 4, P, m, P).transpose(3, 0, 2, 1, 4)
        return w.reshape(m, k // 4, P, WB)

    w_in = a["w_in"]
    offs = np.cumsum([0, 512, 256, 256, 512, 512, 16, 1024, 1024])
    u_v, r, low, gs, gg = (w_in[:, offs[0]:offs[4]], w_in[:, offs[4]:offs[5]], w_in[:, offs[5]:offs[6]],
                           w_in[:, offs[6]:offs[7]], w_in[:, offs[7]:offs[8]])
    stages = [tile_blocks(u_v).reshape(-1, P, WB), tile_blocks(a["w_s5_glu"]).reshape(-1, P, WB)]

    def merged(g, br):
        return np.concatenate([tile_blocks(g), tile_blocks(br)], axis=1).reshape(-1, P, WB)
    stages += [merged(gs, a["w_s5_br"]), tile_blocks(r).reshape(-1, P, WB), merged(gg, a["w_gla_br"]),
               tile_blocks(a["w_out"]).reshape(-1, P, WB)]
    up = tile_blocks(a["w_ff1"]).reshape(FF_GROUPS, 8, P, WB)
    down = tile_blocks(a["w_ff2"]).transpose(1, 0, 2, 3)
    stages += [up[0], up[1]]
    for g in range(FF_GROUPS):
        stages.append(down[g])
        if g + 2 < FF_GROUPS:
            stages.append(up[g + 2])
    wpack = np.ascontiguousarray(np.concatenate(stages))
    assert wpack.shape == (ITERS * RING, P, WB), wpack.shape

    wa = np.zeros((P, KT_D, P), f)
    wa[:, :, 0:RANK] = low.reshape(KT_D, P, RANK).transpose(1, 0, 2)
    vec = np.zeros((P, V_ALL), f)
    for at, g in ((V_MIX, "g_mix"), (V_FFN, "g_ffn"), (V_FIN, "g_final")):
        vec[:, at:at + KT_D] = a[g].reshape(KT_D, P).T
    vec[:, V_BG:V_BG + 2] = a["b_gate"].reshape(2, P).T
    vec[:, V_GLA] = a["g_gla_norm"]
    for s in range(DS):
        vec[s * DEC_SEQ:(s + 1) * DEC_SEQ, V_SEQ + s] = 1.0

    def level_masks(L, levels):
        j, out = np.arange(L)[:, None], []
        for s in levels:
            i = np.arange(L // 2)[None, :]
            m = (j // (2 * s) == i // s) & (j % (2 * s) < s)
            out.append(np.tile(m, (1, 4)))
        out.append(np.tile(np.eye(L, dtype=bool), (1, 4)))
        return np.ascontiguousarray(np.concatenate(out, axis=1).astype(f))

    def by_pair(v):
        v = v.reshape(PAIRS, 2, S5_STATE, *v.shape[2:])
        return np.moveaxis(v, 0, 2).reshape(P, PAIRS, *v.shape[3:])

    logdt = np.broadcast_to(a["log_dt"][:, None], (S5_GROUPS, S5_STATE))
    s5small = np.stack([by_pair(a["lam_re"]), by_pair(a["lam_im"]), by_pair(logdt)], axis=1)
    b = np.stack([by_pair(a["b_re"]), by_pair(a["b_im"])], axis=1)
    c = np.stack([by_pair(a["c_re"].transpose(0, 2, 1)), by_pair(a["c_im"].transpose(0, 2, 1))], axis=1)
    cbd = np.zeros((2, S5_STATE, 2, PAIRS, 2, S5_GROUP), f)
    cc = c.reshape(2, S5_STATE, 2, PAIRS, S5_GROUP)
    for g in range(2):
        cbd[g, :, :, :, g, :] = cc[g]
    dcol = np.tile(a["d_skip"].T, (J, 1))

    def s5_states(v):
        v = v.reshape(HALVES, DS, PAIRS, 2, S5_STATE).transpose(0, 3, 4, 2, 1)
        return v.reshape(HALVES, P, PAIRS, DS)
    s5dec = np.stack([s5_states(a["state_s5_re"]), s5_states(a["state_s5_im"])], axis=2)
    gd = a["state_gla"].reshape(HALVES, DS, 2, 2, DK, DV).transpose(0, 3, 4, 1, 2, 5)
    out = {
        "xT": halves(a["x_prompt"], a["x_sample"]), "wpack": wpack, "wa": wa.reshape(P, -1), "wgu_d": a["w_gate_up"],
        "vec_d": vec, "ident_d": np.eye(P, dtype=f), "masks_d": level_masks(C, LEVELS),
        "dmask_d": level_masks(DT, [LEVELS[l] for l in DEC_LEVELS]), "s5small": s5small,
        "b_d": b.reshape(P, -1), "c_d": c.reshape(P, -1), "cbd_d": cbd.reshape(P, -1), "dcol_d": dcol,
        "s5dec_d": s5dec, "gladec_d": gd.reshape(HALVES, P, -1),
    }
    return {k: np.ascontiguousarray(v) for k, v in out.items()}


OUTS = {"yT": (HALVES, P, KT_D * N), "s5_prompt": (P, 2, PAIRS), "gla_prompt": (P, 2, DV),
        "s5_dec_out": (HALVES, P, 2, PAIRS, DS), "gla_dec_out": (HALVES, P, DS * 2 * DV)}


def kernel(**inputs):
    from concourse import bacc
    from concourse.bass_utils import run_bass_kernel_spmd

    nc = bacc.Bacc("TRN2", target_bir_lowering=False, num_devices=1)
    arrays = lay_out({k: np.asarray(v) for k, v in inputs.items()})
    aps = {n: nc.dram_tensor(n, v.shape, mybir.dt.from_np(v.dtype), kind="ExternalInput").ap()
           for n, v in arrays.items()}
    for n, shape in OUTS.items():
        aps[n] = nc.dram_tensor(n, shape, F32, kind="ExternalOutput").ap()
    build(nc, **aps)
    got = run_bass_kernel_spmd(nc, [arrays], core_ids=[0]).results[0]

    y = got["yT"].reshape(HALVES, P, KT_D, N).transpose(0, 3, 2, 1).reshape(HALVES, N, D_MODEL)
    y_prompt = np.ascontiguousarray(y[:, 0:TP].reshape(1, SEQ, D_MODEL))
    y_sample = np.ascontiguousarray(y[:, TP:N].reshape(DEC_BATCH, DEC_SEQ, D_MODEL))
    sp = got["s5_prompt"].reshape(2, S5_STATE, 2, PAIRS).transpose(2, 3, 0, 1).reshape(2, 1, S5_GROUPS, S5_STATE)
    gp = got["gla_prompt"].reshape(2, DK, 2, DV).transpose(2, 0, 1, 3).reshape(1, HEADS, DK, DV)
    sd = got["s5_dec_out"].reshape(HALVES, 2, S5_STATE, 2, PAIRS, DS).transpose(3, 0, 5, 4, 1, 2)
    sd = sd.reshape(2, DEC_BATCH, S5_GROUPS, S5_STATE)
    gd = got["gla_dec_out"].reshape(HALVES, 2, DK, DS, 2, DV).transpose(0, 3, 4, 1, 2, 5)
    gd = gd.reshape(DEC_BATCH, HEADS, DK, DV)
    return tuple(np.ascontiguousarray(v) for v in (y_prompt, y_sample, sp[0], sp[1], gp, sd[0], sd[1], gd))
```

```python
from contextlib import ExitStack

import concourse.bass as bass
import numpy as np
from concourse import mybir

F32 = mybir.dt.float32
F32R = mybir.dt.float32r
U8 = mybir.dt.uint8
ALU = mybir.AluOpType
ACT = mybir.ActivationFunctionType

P = 128
D_MODEL = 1024
SEQ = 2048
DEC_BATCH, DEC_SEQ = 8, 4
S5_WIDTH, S5_GROUP, S5_GROUPS, S5_STATE = 512, 16, 32, 64
HEADS, DK, DV = 4, 64, 128
RANK = 16
TAU = 16.0
D_FF = 4096
EPS = 1e-6

HALVES = 2
TP = SEQ // HALVES
DS = DEC_BATCH // HALVES
DT = DS * DEC_SEQ
N = TP + DT
BLK = [(0, 352), (352, 344), (696, 344)]
KT_D = D_MODEL // P
KT_S = S5_WIDTH // P
WB = 4 * P
RING = 4

J = 8
PAIRS = S5_GROUPS // 2
NC = TP // J
UC = NC + 2 * DS
YC = NC + DS
EC = NC + 2
C_T, C_PR, C_PI, C_QR, C_QI, C_EC, C_ES = 0, 256, 384, 512, 640, 768, 768 + EC
C_W = 768 + 2 * EC
X_PIECE = 2
CR = 4
OUTPUTS_OUT_AT = 5
TABLES_OUT_AT = 7

C = 128
CHUNKS = TP // C
LEVELS = [64, 32, 16, 8, 4, 2, 1]
NL = len(LEVELS)
NL_A = 4
DEC_LEVELS = [l for l, s in enumerate(LEVELS) if 2 * s <= DEC_SEQ]
DE_K, DE_Q = NL * 2 * C, (NL + 1) * 2 * C
DE_W = (NL + 2) * 2 * C

IT_A = 0
IT_GLU = IT_A + 6
IT_M1 = IT_GLU + 1
IT_R = IT_M1 + 6
IT_M2 = IT_R + 2
IT_OUT = IT_M2 + 6
IT_FF = IT_OUT + 4
ITERS = IT_FF + 32
FF_GROUPS = D_FF // (4 * P)

A_H = 0
A_H1 = A_H + 8 * N
A_O = A_H1 + 8 * N
A_Z = A_O + 8 * N
A_M = A_Z + 8 * N
A_G = A_M + 8 * N
A_END = A_G + 2 * N
REGIONS = [("h0", A_H, 8 * N), ("h1", A_H1, 8 * N), ("o", A_O, 8 * N), ("z", A_Z, 8 * N), ("m", A_M, 8 * N),
           ("g", A_G, 2 * N)]
X_HI = [A_H, A_Z]
X_LO = [A_H1, A_M]
QKV = [A_Z, A_H1]
WORK = [A_M, A_H]
WORK_TMP = S5_GROUPS * UC
WORK_C = WORK_TMP + 1400
O_UP = A_O
O_A = A_O + 4352
O_AH, O_AL = O_A + N, O_A + N + 1024
O_T = O_A + N
O_C0 = A_O + 4352
C_SLOT = [[w + WORK_C, w + WORK_C + C_W, O_C0, O_C0 + C_W] for w in WORK]
O_TAB, TAB_W = A_O + 7440, 27
O_STG_T = O_UP
O_STG_P, STG = O_T, 8
O_SHIFT = O_TAB
G_K, G_SKIP = A_G + 1024, A_G + 1536
O_DE = [A_O, A_O + DE_W]
O_ST = [A_O + 2 * DE_W, A_O + 2 * DE_W + 8 * C]
O_ATT = O_ST[1] + 8 * C
O_VT = [O_ATT + HEADS * C, O_ATT + 2 * HEADS * C]
O_S0, O_KTM = O_DE[1], O_DE[1] + 1024

SETS = {"uqk": (4, 4), "low": (1, 1), "v": (2, 2), "glu": (2, 2), "m1": (8, 8), "r": (4, 4), "m2": (8, 8),
        "out": (4, 4), "ff": (48, 48)}
ORDER = [["uqk", "v", "low"] + list(SETS)[3:], list(SETS)]
SET_BASE, SET_TOTAL = [{}, {}], [0, 0]
for _base, _order in zip(SET_BASE, ORDER):
    SET_TOTAL = [0, 0]
    for _name in _order:
        _base[_name] = tuple(SET_TOTAL)
        SET_TOTAL = [a + b for a, b in zip(SET_TOTAL, SETS[_name])]
NORM = [{"x": 0, "ffn": 1, "y": 3}, {"x": 2, "ffn": 4, "y": 5}]
SP_X, SP_Z5, SP_O5, SP_OG, SP_MG, SP_H2, SP_ALL = 0, 8, 12, 16, 20, 28, 36

V_MIX, V_FFN, V_FIN, V_BG, V_GLA, V_SEQ = 0, 8, 16, 24, 26, 27
V_ALL = V_SEQ + DS
MAGIC = 12582912.0
PI2_1, PI2_2, PI2_3 = 6.28125, 0.0019350051879882812, 3.019916050e-07


def ff_before(g, part):
    if part == "down":
        return (min(g + 2, FF_GROUPS) if isinstance(g, int) else g + 2), g
    return g, (max(g - 1, 0) if isinstance(g, int) else g - 1)


def ff_set(g, part):
    ups, downs = ff_before(g, part)
    return ups * 2 + downs * 4


def ff_it(g, part):
    ups, downs = ff_before(g, part)
    return ups * 2 + downs * 2


class Arena:

    def __init__(self, tensors):
        self.tensors = tensors

    def find(self, col):
        for tensor, (_, start, width) in zip(self.tensors, REGIONS):
            if start <= col < start + width:
                return tensor, start
        raise IndexError(col)

    def __getitem__(self, key):
        rows, span = key
        tensor, start = self.find(span.start)
        return tensor[rows, span.start - start:span.stop - start]

    def at(self, col, offset, n):
        tensor, start = self.find(col)
        return tensor[:, bass.ds(col - start + offset, n)]


def build(nc, xT, wpack, wa, wgu_d, vec_d, ident_d, masks_d, dmask_d, s5small, b_d, c_d, cbd_d, dcol_d,
          s5dec_d, gladec_d, yT, s5_prompt, gla_prompt, s5_dec_out, gla_dec_out):
    u_dram = nc.dram_tensor("u_scratch", (KT_S, P, J, UC), F32, kind="Internal").ap()
    y_dram = nc.dram_tensor("y_scratch", (KT_S, P, J, YC), F32, kind="Internal").ap()
    c_dram = nc.dram_tensor("s5_constants", (PAIRS, P, C_W), F32, kind="Internal").ap()

    with ExitStack() as ctx:
        slab_at = (nc.sbuf_usable_end - A_END * 4) // 64 * 64

        def regions(kind, dt):
            return Arena([nc.alloc_sbuf_tensor_at(f"{kind}_{name}", [P, width], dt, offset=slab_at + start * 4)
                          for name, start, width in REGIONS])
        fa, ra = regions("f", F32), regions("r", F32R)

        def sb(name, shape, dt=F32):
            return ctx.enter_context(nc.sbuf_tensor(name, shape, dt))

        def sem(name):
            return ctx.enter_context(nc.semaphore(name))

        w_raw = sb("w_raw", [P, RING, WB])
        w_hi = sb("w_hi", [P, RING, WB], F32R)
        w_lo = sb("w_lo", [P, RING, WB], F32R)
        khT = sb("khT", [P, 256])
        masks = sb("masks", [P, NL * 256 + 512], U8)
        dmask = sb("dmask", [DT, len(DEC_LEVELS) * 32 + 64], U8)
        ident = sb("ident", [P, P])
        ones = sb("ones", [P, P])
        vec = sb("vec", [P, V_ALL])
        wgu = sb("wgu", [RANK, 2 * P])
        dcol = sb("dcol", [P, S5_GROUPS])
        gla_s = sb("gla_s", [P, 2, 2, DV])
        decay = sb("decay", [P, 2, 8])
        s5_carry = sb("s5_carry", [P, 2, PAIRS])
        s5_m8 = sb("s5_m8", [P, PAIRS])
        s5_a4 = sb("s5_a4", [P, 2, PAIRS])
        s5_dec = sb("s5_dec", [P, 2, PAIRS, DS])
        s5_new = sb("s5_new", [P, 2, PAIRS, DS])
        s5_tmp = sb("s5_tmp", [P, 2, PAIRS, DS])
        zero = sb("zero", [P, 1])
        sml = sb("s5_small", [P, len(SMALL), PAIRS])
        assert nc.sbuf_base <= slab_at, (nc.sbuf_base, slab_at)
        ps = ctx.enter_context(nc.psum_tensor("ps", [P, 8, 512], F32))

        w_landed = [sem(f"w_landed{s}") for s in range(RING)]
        w_split = [sem(f"w_split{s}") for s in range(RING)]
        w_used = [sem(f"w_used{s}") for s in range(RING)]
        set_read = [sem("set0_read"), sem("set1_read")]
        const_landed, s5in_landed, bc_landed, cbd_landed = (sem("const_landed"), sem("s5in_landed"),
                                                            sem("bc_landed"), sem("cbd_landed"))
        masks_landed = sem("masks_landed")
        x_landed = [sem(f"x_landed{n}") for n in range(KT_D // X_PIECE)]
        res_landed, wa_landed = sem("res_landed"), sem("wa_landed")
        ones_ready = sem("ones_ready")
        sq_ready, ssum_ready, ms_done = sem("sq_ready"), sem("ssum_ready"), sem("ms_done")
        ms_read, std_ready = sem("ms_read"), sem("std_ready")
        full_ready, hi_ready, split_ready = sem("full_ready"), sem("hi_ready"), sem("split_ready")
        u_pad, u_stored, u_landed = sem("u_pad"), sem("u_stored"), sem("u_landed")
        wa_split, low_done, low_ready, gpre_done = sem("wa_split"), sem("low_done"), sem("low_ready"), sem("gpre_done")
        gln_ready, gmin_ready, b_ready = sem("gln_ready"), sem("gmin_ready"), sem("b_ready")
        dt_ready, trig_in, trig_out = sem("dt_ready"), sem("trig_in"), sem("trig_out")
        qe_ready, qe_stored, g_ready = sem("qe_ready"), sem("qe_stored"), sem("g_ready")
        tp_done, p_ready, t_ready, tp_stored = sem("tp_done"), sem("p_ready"), sem("t_ready"), sem("tp_stored")
        t_stored = sem("t_stored")
        k_done, k_ready, shift_done = sem("k_done"), sem("k_ready"), sem("shift_done")
        c_landed = [sem(f"c_landed{s}") for s in range(CR)]
        chunk_in_done, chunk_in_read = sem("chunk_in_done"), sem("chunk_in_read")
        state_ready, yrow_done, yrow_read = sem("state_ready"), sem("yrow_done"), sem("yrow_read")
        yrow_stored, yperm_landed, gelu_ready = sem("yrow_stored"), sem("yperm_landed"), sem("gelu_ready")
        s5dec_landed, s5dec_ready = sem("s5dec_landed"), sem("s5dec_ready")
        stage_ready, diff_ready, exp_ready, mul_ready = (sem("stage_ready"), sem("diff_ready"), sem("exp_ready"),
                                                         sem("mul_ready"))
        vt_done, kht_done = sem("vt_done"), sem("kht_done")
        level_a_done, level_done = sem("level_a_done"), sem("level_done")
        vt_ready, kht_ready, att_ready = sem("vt_ready"), sem("kht_ready"), sem("att_ready")
        o_done, o_read, sup_done, s_ready = sem("o_done"), sem("o_read"), sem("sup_done"), sem("s_ready")
        s0_landed, ktm_ready, s0_ready = sem("s0_landed"), sem("ktm_ready"), sem("s0_ready")
        osq_ready, gms_done, gstd_ready = sem("osq_ready"), sem("gms_done"), sem("gstd_ready")
        hidden_hi, hidden_split = sem("hidden_hi"), sem("hidden_split")
        y_ready, y_stored, out_stored = sem("y_ready"), sem("y_stored"), sem("out_stored")

        def tile(arena, at, k):
            return arena.at(at + k * N, 0, N) if isinstance(k, int) else arena.at(at, k * N, N)

        def ft(at, k=0):
            return tile(fa, at, k)

        def rt(at, k=0):
            return tile(ra, at, k)

        def hf(at, k=0):
            return tile(ra, at, k).bitcast(F32)

        def fv(at, n):
            return fa[:, at:at + n]

        def cols(tile):
            return [tile[:, 0:352], tile[:, 352:N].rearrange("p (b n) -> p b n", b=2)]

        def psum_cols(s):
            return [ps[:, 3 * s, 0:352], ps[:, 3 * s + 1:3 * s + 3, 0:344]]

        def set_count(half, s, stage, n):
            return half * SET_TOTAL[s] + SET_BASE[half][stage][s] + n

        def full_count(half, n):
            before_z5 = isinstance(n, int) and n <= SP_Z5
            return half * (SP_ALL - KT_S) + n - (0 if before_z5 else KT_S)

        def small(name, n=1):
            k = SMALL.index(name)
            return sml[:, k:k + n, :] if n > 1 else sml[:, k, :]

        def rows_of(h):
            return slice(64 * (h % 2), 64 * (h % 2) + 64), h // 2, 2 * (h % 2) + h // 2

        consts = [(vec[:, :], vec_d), (ident[:, :], ident_d), (wgu[:, :], wgu_d), (dcol[:, :], dcol_d)]
        mask_floats = [(fv(A_Z, NL * 256 + 512), masks_d),
                       (fa[0:DT, A_Z + 4096:A_Z + 4096 + dmask.shape[1]], dmask_d)]
        block = ctx.enter_context(nc.Block())

        @block.sync
        def _(sp):
            def load(s, it):
                block = wpack[it * RING + s] if isinstance(it, int) else wpack[bass.ds(it * RING + s, 1)].rearrange(
                    "o p n -> p (o n)")
                sp.dma_start(w_raw[:, s, :], block).then_inc(w_landed[s], 16)

            for s in range(RING):
                load(s, 0)
            for half in range(HALVES):
                with sp.Fori(0 if half else 1, ITERS) as it:
                    for s in range(RING):
                        sp.wait_ge(w_split[s], half * ITERS + it)
                        load(s, it)

        @block.gpsimd
        def _(pool):
            pool.memset(zero[:, :], 0.0)
            pool.drain()

            def split(s, n):
                pool.wait_ge(w_landed[s], (n + 1) * 16)
                if not isinstance(n, int):
                    pool.wait_ge(w_used[s], n)
                pool.tensor_tensor(w_hi[:, s, :], w_raw[:, s, :], zero[:, :].to_broadcast([P, WB]), ALU.subtract)
                pool.drain()
                pool.tensor_tensor(w_lo[:, s, :], w_raw[:, s, :], w_hi[:, s, :].bitcast(F32),
                                   ALU.subtract).then_inc(w_split[s], 1)

            for s in range(RING):
                split(s, 0)
            with pool.Fori(1, HALVES * ITERS) as n:
                for s in range(RING):
                    split(s, n)

        @block.tensor
        def _(pe):
            def set_free(half, s, stage, n):
                pe.wait_ge(set_read[s], set_count(half, s, stage, n))

            def tiles_of(s, k, total, wh, wl, hi, lo):
                for b, (c0, cn) in enumerate(BLK):
                    out = ps[:, 3 * s + b, 0:cn]
                    h, l = hi(k)[:, c0:c0 + cn], lo(k)[:, c0:c0 + cn]
                    pe.matmul(out, wh, h, start=(k == 0), stop=False)
                    pe.matmul(out, wh, l, start=False, stop=False)
                    last = pe.matmul(out, wl, h, start=False, stop=(k == total - 1))
                return last

            def product(s, blocks, hi, lo):
                for n, (place, it) in enumerate(blocks):
                    pe.wait_ge(w_split[place], it + 1)
                    for q in range(4):
                        last = tiles_of(s, 4 * n + q, 4 * len(blocks), w_hi[:, place, q * P:(q + 1) * P],
                                        w_lo[:, place, q * P:(q + 1) * P], hi, lo)
                    last.then_inc(w_used[place], 1)

            def row_sums(n, squares):
                pe.wait_ge(ssum_ready, n + 1)
                for b, (c0, cn) in enumerate(BLK):
                    if n or b == 2:
                        pe.wait_ge(ms_read, 3 * n + (1 if b == 2 else 0))
                    pe.matmul(ps[:, 6 + b % 2, 0:cn], ones[:, :], fv(squares + c0, cn), start=True, stop=True
                              ).then_inc(ms_done, 1)

            def tile_pair(half, stage, n, it, hi, lo):
                for s in range(2):
                    set_free(half, s, stage, n)
                    product(s, [(2 * s, it), (2 * s + 1, it)], hi, lo)

            def first_pair(half, stage, it, split, blocks, hi, lo):
                for s in range(2):
                    set_free(half, s, stage, 0)
                for n in range(blocks):
                    for s in range(2):
                        pe.wait_ge(w_split[blocks * s + n], it + 1)
                    for q in range(4):
                        k = 4 * n + q
                        pe.wait_ge(split_ready, half * SP_ALL + split + k + 1)
                        for s in range(2):
                            place = blocks * s + n
                            last = tiles_of(s, k, 4 * blocks, w_hi[:, place, q * P:(q + 1) * P],
                                            w_lo[:, place, q * P:(q + 1) * P], hi, lo)
                            if q == 3:
                                last.then_inc(w_used[place], 1)

            def s5_setup():
                pe.wait_ge(g_ready, 1)
                g_re = fv(A_M, 3840).rearrange("p (t s) -> p t s", t=PAIRS)
                g_im = fv(A_M + 3840, 3840).rearrange("p (t s) -> p t s", t=PAIRS)
                c_re = fv(A_G, 512).rearrange("p (t c) -> p t c", t=PAIRS)
                c_im = fv(A_G + 512, 512).rearrange("p (t c) -> p t c", t=PAIRS)
                set_free(0, 0, "low", 0)
                set_free(0, 1, "low", 0)
                for t in range(PAIRS):
                    out = ps[:, 0, 2 * S5_GROUP * t:2 * S5_GROUP * (t + 1)]
                    pe.matmul(out, g_re[:, t, 0:P], c_re[:, t, :], start=True, stop=False)
                    last = pe.matmul(out, g_im[:, t, 0:P], c_im[:, t, :], start=False, stop=True)
                last.then_inc(k_done, 1)
                for t in range(PAIRS):
                    if t >= 2:
                        pe.wait_ge(p_ready, t - 1)
                    pe.transpose(ps[:, 4 + t % 2, 0:128], g_re[:, t, 0:P], ident[:, :])
                    pe.transpose(ps[:, 4 + t % 2, 128:256], g_im[:, t, 0:P], ident[:, :]).then_inc(tp_done, 1)
                pe.wait_ge(k_ready, 1)
                for j in range(J):
                    if j >= 4:
                        pe.wait_ge(t_ready, j - 3)
                    w0 = S5_GROUP * (J - 1 - j)
                    pe.matmul(ps[:, j % 4, 0:512], fv(O_SHIFT + w0, P), fv(G_K, 512), start=True, stop=True
                              ).then_inc(shift_done, 1)
                pe.wait_ge(p_ready, PAIRS)
                pe.wait_ge(t_ready, J)

            def s5_in(half, t):
                r = t % CR
                pe.wait_ge(c_landed[r], (half * (PAIRS // CR) + t // CR + 1) * 16)
                pe.wait_ge(chunk_in_read, half * PAIRS + max(t - 1, 0))
                for g in range(2):
                    for q, c0 in ((0, C_PR), (1, C_PI)):
                        last = pe.matmul(ps[64 * g:64 * g + 64, 6 + t % 2, q * UC:(q + 1) * UC],
                                         fv(C_SLOT[half][r] + c0 + 64 * g, 64), fv(WORK[half] + (t * 2 + g) * UC, UC),
                                         start=True, stop=True)
                last.then_inc(chunk_in_done, 1)

            def s5_rows(half, t):
                pe.wait_ge(state_ready, half * PAIRS + t + 1)
                pe.wait_ge(yrow_read, half * PAIRS + max(t - 1, 0))
                at, st = C_SLOT[half][t % CR], WORK[half] + WORK_TMP + 800 + (t % 2) * 2 * YC
                for g in range(2):
                    out, rows = ps[:, 2 * (t % 2) + g, 0:YC], slice(64 * g, 64 * g + 64)
                    pe.matmul(out, fv(at + C_T + P * g, P), fv(WORK[half] + (t * 2 + g) * UC, YC), start=True, stop=False)
                    pe.matmul(out, fa[rows, at + C_QR:at + C_QR + P], fa[rows, st:st + YC], start=False, stop=False)
                    last = pe.matmul(out, fa[rows, at + C_QI:at + C_QI + P], fa[rows, st + YC:st + 2 * YC],
                                     start=False, stop=True)
                last.then_inc(yrow_done, 1)

            def s5(half):
                set_free(half, 0, "glu", 0)
                set_free(half, 1, "glu", 0)
                pe.wait_ge(ms_read, 3 * (NORM[half - 1]["y"] + 1 if half else 1))
                pe.wait_ge(u_landed, (half + 1) * 16 * J)
                s5_in(half, 0)
                s5_in(half, 1)
                for t in range(PAIRS):
                    s5_rows(half, t)
                    if t + 2 < PAIRS:
                        s5_in(half, t + 2)
                pe.wait_ge(yrow_read, (half + 1) * PAIRS)

            def merge_products(half, it0, stage, split_count):
                with pe.Fori(0, 2) as i:
                    for q in range(4):
                        b = [((3 * q + x) % RING, half * ITERS + it0 + i * 3 + (3 * q + x) // RING) for x in range(3)]
                        set_free(half, 0, stage, i * 4 + q)
                        product(0, b[0:2], lambda k: rt(X_HI[half], k), lambda k: rt(X_LO[half], k))
                        pe.wait_ge(split_ready, half * SP_ALL + split_count)
                        set_free(half, 1, stage, i * 4 + q)
                        product(1, b[2:3], lambda k: rt(A_O, k), lambda k: rt(A_O, 4 + k))

            def gla_pre(half, c, par):
                L = DT if isinstance(c, int) and c == CHUNKS else C
                n = half * (CHUNKS + 1) + c
                st, de = O_ST[par], O_DE[par]
                pe.wait_ge(stage_ready, n + 1)
                pe.wait_ge(vt_ready, n)
                for h in range(HEADS):
                    slot = rows_of(h)[2]
                    last = pe.transpose(ps[0:L, 6, slot * DV:(slot + 1) * DV], fv(st + 4 * L + h * L, L), ident[:, :])
                last.then_inc(vt_done, 1)
                pe.wait_ge(mul_ready, n + 1)
                pe.wait_ge(kht_ready, n)
                pe.wait_ge(s_ready, half * CHUNKS + c + 1)
                for t in range(2):
                    last = pe.transpose(ps[0:L, 7, t * P:(t + 1) * P], fv(de + DE_K + t * L, L), ident[:, :])
                last.then_inc(kht_done, 1)

            def gla_sums(half, c, par):
                dec = isinstance(c, int) and c == CHUNKS
                L = DT if dec else C
                for s in range(DS if dec else 1):
                    for h in range(HEADS):
                        _, t, slot = rows_of(h)
                        kk = t * P + (h % 2) * 64
                        keys = fa[0:L, O_KTM + s * 256 + kk:O_KTM + s * 256 + kk + 64] if dec else khT[0:L, kk:kk + 64]
                        bank, col = ((s * 2 + t) * DV // 512, (s * 2 + t) * DV % 512) if dec else (7, 256 + t * DV)
                        last = pe.matmul(ps[64 * (h % 2):64 * (h % 2) + 64, bank, col:col + DV],
                                         keys, fa[0:L, O_VT[par] + slot * DV:O_VT[par] + (slot + 1) * DV],
                                         start=True, stop=True)
                last.then_inc(sup_done, 1)

            def gla(half, c, par):
                dec = isinstance(c, int) and c == CHUNKS
                L = DT if dec else C
                n = half * (CHUNKS + 1) + c
                st, de = O_ST[par], O_DE[par]
                pe.wait_ge(vt_ready, n + 1)
                pe.wait_ge(kht_ready, n + 1)
                if not dec:
                    gla_sums(half, c, par)
                for l in (DEC_LEVELS if dec else range(NL)):
                    for h in (0, 2, 1, 3):
                        rows, t, _ = rows_of(h)
                        col, at = l * 128 + t * (L // 2), de + l * 256 + t * L
                        right = fa[rows, at:at + L].rearrange("p (b two s) -> p b two s", two=2, s=LEVELS[l])[:, :, 1, :]
                        last = pe.matmul(ps[0:L, 2 * (col // 512) + h % 2, col % 512:col % 512 + L // 2],
                                         fa[rows, at:at + L], right, start=True, stop=True)
                    if l == NL_A - 1:
                        last.then_inc(level_a_done, 1)
                pe.wait_ge(o_read, n)
                for h in (0, 2, 1, 3):
                    rows, t, _ = rows_of(h)
                    last = pe.matmul(ps[0:L, 4 + h % 2, t * L:t * L + L],
                                     fa[rows, st + 2 * L + t * L:st + 3 * L + t * L],
                                     fa[rows, st + t * L:st + t * L + L], start=True, stop=True)
                last.then_inc(level_done, 1)
                if not dec:
                    gla_pre(half, c + 1, 1 - par)
                pe.wait_ge(att_ready, n + 1)
                if dec:
                    pe.wait_ge(s0_landed, (half + 1) * 16)
                for h in range(HEADS):
                    rows, t, slot = rows_of(h)
                    bank, o0, qq = 4 + h % 2, 256 + t * L, de + DE_Q + t * L
                    vr = fa[0:L, O_VT[par] + slot * DV:O_VT[par] + (slot + 1) * DV]
                    att = fa[0:L, O_ATT + slot * L:O_ATT + (slot + 1) * L]
                    if dec:
                        last = pe.matmul(ps[:, bank, o0:o0 + L], vr, att, start=True, stop=False, skip_group_check=True)
                        for s in range(DS):
                            s0, a = O_S0 + (s * 2 + t) * DV, s * DEC_SEQ
                            last = pe.matmul(ps[:, bank, o0 + a:o0 + a + DEC_SEQ], fa[rows, s0:s0 + DV],
                                             fa[rows, qq + a:qq + a + DEC_SEQ], start=False, stop=(s == DS - 1),
                                             skip_group_check=True)
                    else:
                        pe.matmul(ps[:, bank, o0:o0 + L], gla_s[rows, par, t, :], fa[rows, qq:qq + L],
                                  start=True, stop=False)
                        last = pe.matmul(ps[:, bank, o0:o0 + L], vr, att, start=False, stop=True)
                last.then_inc(o_done, 1)
                if dec:
                    pe.wait_ge(ktm_ready, half + 1)
                    gla_sums(half, c, par)

            def ff_up(half, g):
                for q in range(2):
                    tile_pair(half, "ff", ff_set(g, "up") + q, half * ITERS + IT_FF + ff_it(g, "up") + q,
                              lambda k: rt(QKV[half], k), lambda k: rt(WORK[half], k))

            def ff_down(half, g, par, between=None):
                pe.wait_ge(hidden_split, half * FF_GROUPS * 4 + 4 * g + 4)
                hb = X_LO[half] if par == 0 else A_O
                for m in range(KT_D):
                    set_free(half, m % 2, "ff", ff_set(g, "down") + m // 2)
                    product(m % 2, [(m % RING, half * ITERS + IT_FF + ff_it(g, "down") + m // RING)],
                            lambda k: rt(hb, k), lambda k: rt(hb, 4 + k))
                    if between and m == 1:
                        between()

            def gate_products(half):
                pe.wait_ge(low_ready, half + 1)
                for t in range(2):
                    s = 1 - t
                    set_free(half, s, "low", 0)
                    for b, (c0, cn) in enumerate(BLK):
                        last = pe.matmul(ps[:, 3 * s + b, 0:cn], wgu[:, t * P:(t + 1) * P],
                                         fa[0:RANK, O_A + c0:O_A + c0 + cn], start=True, stop=True)
                    last.then_inc(gpre_done, 1)

            def low_rank(half):
                set_free(half, 0, "low", 0)
                pe.wait_ge(wa_split, half + 1)
                for k in range(KT_D):
                    last = tiles_of(0, k, KT_D, ra[:, O_AH + k * P:O_AH + (k + 1) * P],
                                    ra[:, O_AL + k * P:O_AL + (k + 1) * P],
                                    lambda k: rt(X_HI[half], k), lambda k: rt(X_LO[half], k))
                last.then_inc(low_done, 1)

            pe.wait_ge(ones_ready, 1)
            pe.wait_ge(const_landed, 16 * len(consts))
            for half in range(HALVES):
                x_hi, x_lo = (lambda k: rt(X_HI[half], k)), (lambda k: rt(X_LO[half], k))
                if half == 0:
                    row_sums(NORM[0]["x"], X_HI[0])
                first_pair(half, "uqk", half * ITERS + IT_A, SP_X, 2, x_hi, x_lo)
                if half:
                    row_sums(NORM[half - 1]["y"], X_LO[half - 1])
                with pe.Fori(1, 4) as i:
                    tile_pair(half, "uqk", i, half * ITERS + IT_A + i, x_hi, x_lo)
                if half:
                    low_rank(half)
                    gate_products(half)
                with pe.Fori(0, 2) as i:
                    tile_pair(half, "v", i, half * ITERS + IT_A + 4 + i, x_hi, x_lo)
                if half == 0:
                    low_rank(half)
                    pe.wait_ge(low_ready, 1)
                    s5_setup()
                    gate_products(half)
                s5(half)
                first_pair(half, "glu", half * ITERS + IT_GLU, SP_Z5, 1, lambda k: rt(A_O, k), lambda k: rt(A_O, 4 + k))
                for s in range(2, RING):
                    set_free(half, s % 2, "glu", s // 2)
                    product(s % 2, [(s, half * ITERS + IT_GLU)], lambda k: rt(A_O, k), lambda k: rt(A_O, 4 + k))
                merge_products(half, IT_M1, "m1", SP_O5 + KT_S)
                set_free(half, 0, "r", 0)
                set_free(half, 1, "r", 0)
                gla_pre(half, 0, 0)
                for par in range(2):
                    gla(half, par, par)
                with pe.Fori(1, CHUNKS // 2 - 1) as i:
                    for par in range(2):
                        gla(half, i * 2 + par, par)
                for c in range(CHUNKS - 2, CHUNKS + 1):
                    gla(half, c, c % 2)
                pe.wait_ge(o_read, (half + 1) * (CHUNKS + 1))
                pe.wait_ge(s0_ready, half + 1)
                for h in range(HEADS):
                    set_free(half, 0, "r", h)
                    b, it = 2 * (h % 2), half * ITERS + IT_R + h // 2
                    product(0, [(b, it), (b + 1, it)], x_hi, x_lo)
                    set_free(half, 1, "r", h)
                    pe.wait_ge(osq_ready, half * HEADS + h + 1)
                    for b, (c0, cn) in enumerate(BLK):
                        last = pe.matmul(ps[:, 3 + b, 0:cn], ones[:, :], ft(A_O, h)[:, c0:c0 + cn],
                                         start=True, stop=True)
                    last.then_inc(gms_done, 1)
                merge_products(half, IT_M2, "m2", SP_OG + HEADS)
                n_hi, n_lo = (lambda k: rt(QKV[half], k)), (lambda k: rt(WORK[half], k))
                first_pair(half, "out", half * ITERS + IT_OUT, SP_MG, 2, n_hi, n_lo)
                with pe.Fori(1, 4) as i:
                    tile_pair(half, "out", i, half * ITERS + IT_OUT + i, n_hi, n_lo)
                row_sums(NORM[half]["ffn"], A_O)
                first_pair(half, "ff", half * ITERS + IT_FF, SP_H2, 2, n_hi, n_lo)
                tile_pair(half, "ff", 1, half * ITERS + IT_FF + 1, n_hi, n_lo)
                ff_up(half, 1)
                with pe.Fori(0, FF_GROUPS // 2 - 1) as i:
                    for par in range(2):
                        ff_down(half, i * 2 + par, par)
                        ff_up(half, i * 2 + par + 2)
                ff_down(half, FF_GROUPS - 2, 0)
                ff_down(half, FF_GROUPS - 1, 1,
                        (lambda: row_sums(NORM[half + 1]["x"], X_HI[half + 1])) if half + 1 < HALVES else None)
            row_sums(NORM[HALVES - 1]["y"], X_LO[HALVES - 1])

        @block.scalar
        def _(act):
            def evac(s, dst, func=ACT.Copy, **kw):
                for src, d in zip(psum_cols(s), cols(dst)):
                    last = act.activation(d, src, func, **kw)
                return last

            def block_used(half, place, it):
                act.wait_ge(w_used[place], half * ITERS + it + 1)

            def norm_squares(src, dst, src_ready=None):
                for k in range(KT_D):
                    if src_ready:
                        src_ready(k)
                    act.activation(ft(dst, k), ft(src, k), ACT.Square).then_inc(sq_ready, 1)

            def norm_root(n):
                act.wait_ge(ms_read, 3 * (n + 1))
                act.activation(ft(A_G), ft(A_G), ACT.Sqrt).then_inc(std_ready, 1)

            def high_parts(half, first, count, src, dst):
                for k in range(count):
                    act.wait_ge(full_ready, full_count(half, first + k + 1))
                    act.activation(rt(dst, k), ft(src, k), ACT.Copy).then_inc(hi_ready, 1)

            def input_load(half):
                for n, landed in enumerate(x_landed):
                    w = X_PIECE * N
                    act.dma_start(fv(X_LO[half] + n * w, w), xT[half, :, n * w:(n + 1) * w]).then_inc(landed, 16)

            def input_norm(half):
                norm_squares(X_LO[half], X_HI[half],
                             lambda k: None if k % X_PIECE else act.wait_ge(x_landed[k // X_PIECE], (half + 1) * 16))
                norm_root(NORM[half]["x"])
                high_parts(half, SP_X, KT_D, X_LO[half], X_HI[half])

            def u_by_chunks(half):
                act.wait_ge(u_stored, (half + 1) * 16)
                if half:
                    act.wait_ge(y_stored, half * 16 * KT_D)
                for j in range(J):
                    act.dma_start(fa[j * 16:(j + 1) * 16, WORK[half]:WORK[half] + S5_GROUPS * UC].rearrange(
                        "p (g c) -> p g c", c=UC),
                        u_dram.rearrange("m (g h) j c -> j h (m g) c", h=S5_GROUP)[j]).then_inc(u_landed, 16)
                act.dma_start(s5_dec[:, :, :, :], s5dec_d[half]).then_inc(s5dec_landed, 16)

            def store_output(half):
                for k in range(KT_D):
                    act.wait_ge(y_ready, half * KT_D + k + 1)
                    act.dma_start(yT[half, :, k * N:(k + 1) * N], ft(X_HI[half], k)).then_inc(y_stored, 16)

            def project(half):
                if half:
                    block_used(half - 1, 3, ITERS - 1)
                act.dma_start(fv(O_A, KT_D * P), wa).then_inc(wa_landed, 16)
                if half:
                    for s in range(2):
                        act.wait_ge(set_read[s], half * SET_TOTAL[s])
                    norm_squares(X_HI[half - 1], X_LO[half - 1])
                if half == 0:
                    act.wait_ge(split_ready, SP_X + KT_D)
                    act.dma_start(fv(A_G, 512), b_d).then_inc(bc_landed, 16)
                    act.dma_start(fv(A_G + 512, 512), c_d).then_inc(bc_landed, 16)
                up = fv(O_UP, KT_S * J * UC).rearrange("p (m j c) -> p m j c", m=KT_S, j=J)
                for m in range(KT_S):
                    s = m % 2
                    if half and m == 2:
                        norm_root(NORM[half - 1]["y"])
                    block_used(half, 2 * s + 1, IT_A + m // 2)
                    for b, (c0, cn) in enumerate(BLK):
                        pn = min(cn, TP - c0)
                        act.activation(up[:, m, :, c0 // J:(c0 + pn) // J],
                                       ps[:, 3 * s + b, 0:pn].rearrange("p (c j) -> p j c", j=J), ACT.Copy)
                    dec = ps[:, 3 * s + 2, TP - BLK[2][0]:N - BLK[2][0]].rearrange("p (q j) -> p j q", j=DEC_SEQ)
                    act.activation(up[:, m, 0:DEC_SEQ, NC:NC + DS], dec, ACT.Copy)
                    act.activation(up[:, m, DEC_SEQ:J, NC + DS:UC], dec, ACT.Copy).then_inc(set_read[s], 1)
                act.wait_ge(u_pad, 2 * (half + 1))
                act.wait_ge(set_read[0], set_count(half, 0, "uqk", 2))
                act.wait_ge(set_read[1], set_count(half, 1, "uqk", 2))
                act.dma_start(u_dram.rearrange("m p j c -> p m (j c)"),
                              fv(O_UP, KT_S * J * UC).rearrange("p (m n) -> p m n", m=KT_S)).then_inc(u_stored, 16)
                if half:
                    store_output(half - 1)
                for m in range(KT_S, 12):
                    s = m % 2
                    block_used(half, 2 * s + 1, IT_A + m // 2)
                    evac(s, ft(QKV[half], m - KT_S), scale=DK ** -0.5 if m < KT_S + 2 else 1.0).then_inc(set_read[s], 1)
                    if half == 0 and m == TABLES_OUT_AT:
                        s5_tables_out()
                    if half == 0 and m == OUTPUTS_OUT_AT:
                        s5_outputs_out()
                    if half and m == 7:
                        low_rank_out(half)
                        u_by_chunks(half)
                        log_gates(half)
                if half == 0:
                    low_rank_out(half)

            def low_rank_out(half):
                act.wait_ge(low_done, half + 1)
                for src, d in zip([ps[0:RANK, 0, 0:352], ps[0:RANK, 1:3, 0:344]],
                                  cols(fa[0:RANK, O_A:O_A + N])):
                    last = act.activation(d, src, ACT.Copy)
                last.then_inc(low_ready, 1)

            def log_gates(half):
                if half == 0:
                    act.wait_ge(tp_stored, 16 * (PAIRS // STG))
                for t in range(2):
                    act.wait_ge(gpre_done, half * 2 + t + 1)
                    evac(1 - t, ft(A_G, t), ACT.Identity, bias=vec[:, V_BG + t:V_BG + t + 1]
                         ).then_inc(set_read[1 - t], 1)
                for t in range(2):
                    act.wait_ge(gmin_ready, half * 2 + t)
                    act.drain()
                    act.activation(ft(O_T), ft(A_G, t), ACT.Abs)
                    act.drain()
                    act.activation(ft(O_T), ft(O_T), ACT.Exp, scale=-1.0)
                    act.drain()
                    act.activation(ft(O_T), ft(O_T), ACT.Ln, bias=1.0).then_inc(gln_ready, 1)

            def s5_outputs_out():
                act.wait_ge(qe_ready, 1)
                act.dma_start(c_dram.rearrange("t p c -> p t c")[:, :, C_QR:C_QR + 2 * P],
                              fv(A_M, 4096).rearrange("p (t c) -> p t c", t=PAIRS)).then_inc(qe_stored, 16)

            def s5_tables_out():
                act.wait_ge(qe_ready, 2)
                by_pair = c_dram.rearrange("t p c -> p t c")
                act.dma_start(by_pair[:, :, C_EC:C_EC + 2 * EC],
                              fv(A_M + 4096, PAIRS * 2 * EC).rearrange("p (t c) -> p t c", t=PAIRS)).then_inc(qe_stored, 16)
                act.dma_start(fv(A_G, 1024), cbd_d).then_inc(cbd_landed, 16)

            def s5_pairs_out():
                by_pair = c_dram.rearrange("t p c -> p t c")
                for t in range(PAIRS):
                    act.wait_ge(tp_done, t + 1)
                    if t == STG:
                        act.wait_ge(tp_stored, 16)
                    act.activation(fv(O_STG_P + 256 * (t % STG), 256), ps[:, 4 + t % 2, 0:256], ACT.Copy
                                   ).then_inc(p_ready, 1)
                    if t % STG == STG - 1:
                        act.wait_ge(p_ready, t + 1)
                        act.dma_start(by_pair[:, t + 1 - STG:t + 1, C_PR:C_PR + 256],
                                      fv(O_STG_P, STG * 256).rearrange("p (t c) -> p t c", t=STG)).then_inc(tp_stored, 16)
                act.wait_ge(t_ready, J)
                act.dma_start(by_pair[:, :, C_T:C_T + 256],
                              fv(O_STG_T, PAIRS * 256).rearrange("p (t c) -> p t c", t=PAIRS)).then_inc(t_stored, 16)

            def load_consts(half, t, r):
                src = c_dram[t] if isinstance(t, int) else c_dram[bass.ds(t, 1)].rearrange("o p c -> p (o c)")
                act.dma_start(fv(C_SLOT[half][r], C_W), src).then_inc(c_landed[r], 16)

            def s5(half):
                if half == 0:
                    act.wait_ge(t_stored, 16)
                for r in range(2):
                    load_consts(half, r, r)
                act.wait_ge(b_ready, half + 1)
                for r in range(2, CR):
                    load_consts(half, r, r)

                def rows(i, r):
                    t = i * CR + r
                    act.wait_ge(yrow_done, half * PAIRS + t + 1)
                    act.activation(fa.at(O_UP, t * 2 * YC, 2 * YC).rearrange("p (g c) -> p g c", g=2),
                                   ps[:, 2 * (r % 2):2 * (r % 2) + 2, 0:YC], ACT.Copy).then_inc(yrow_read, 1)

                def tile_loaded(m):
                    act.wait_ge(yrow_stored, (half * KT_S + m + 1) * 16 * J)
                    act.dma_start(fa.at(O_UP, m * J * YC, J * YC),
                                  one(y_dram, m).rearrange("m p j c -> p (m j c)")).then_inc(yperm_landed, 16)

                def one(tensor, m):
                    return tensor[m:m + 1] if isinstance(m, int) else tensor[bass.ds(m, 1)]

                def pairs_of(m, first, last):
                    for r in range(CR):
                        rows(m, r)
                        if not last:
                            load_consts(half, m * CR + CR + r, r)
                    if not first:
                        tile_loaded(m - 1)
                    act.wait_ge(yrow_read, half * PAIRS + (m + 1) * CR)
                    for j in range(J):
                        tensor, start = fa.find(O_UP)
                        src = tensor[j * 16:(j + 1) * 16, bass.ds(O_UP - start + m * J * YC, J * YC)]
                        act.dma_start(one(y_dram, m).rearrange("m (g h) j c -> j h (m g) c", h=S5_GROUP)[j],
                                      src.rearrange("p (g c) -> p g c", c=YC)).then_inc(yrow_stored, 16)

                pairs_of(0, True, False)
                with act.Fori(1, KT_S - 1) as m:
                    pairs_of(m, False, False)
                pairs_of(KT_S - 1, False, True)
                tile_loaded(KT_S - 1)
                act.wait_ge(s5dec_ready, half + 1)
                act.dma_start(s5_dec_out[half], s5_new[:, :, :, :]).then_inc(out_stored, 16)
                act.wait_ge(yperm_landed, (half + 1) * 16 * KT_S)
                yp = fv(O_UP, KT_S * J * YC).rearrange("p (m j c) -> p m j c", m=KT_S, j=J)
                for m in range(KT_S):
                    z = ft(WORK[half], m)
                    act.activation(z[:, 0:TP].rearrange("p (c j) -> p c j", j=J),
                                   yp[:, m, :, 0:NC].rearrange("p j c -> p c j"), ACT.Gelu_apprx_tanh)
                    act.activation(z[:, TP:N].rearrange("p (q j) -> p q j", j=DEC_SEQ),
                                   yp[:, m, 0:DEC_SEQ, NC:YC].rearrange("p j c -> p c j"),
                                   ACT.Gelu_apprx_tanh).then_inc(gelu_ready, 1)
                act.wait_ge(gelu_ready, (half + 1) * KT_S)
                for m in range(KT_S):
                    act.activation(rt(A_O, m), ft(WORK[half], m), ACT.Copy).then_inc(hi_ready, 1)
                for m in range(KT_S):
                    block_used(half, m, IT_GLU)
                    evac(m % 2, ft(WORK[half], 4 + m), ACT.Sigmoid).then_inc(set_read[m % 2], 1)
                high_parts(half, SP_O5, KT_S, WORK[half], A_O)
                act.wait_ge(split_ready, half * SP_ALL + SP_O5 + KT_S)
                with act.Fori(0, 2) as i:
                    for q in range(4):
                        block_used(half, (3 * q + 1) % RING, IT_M1 + i * 3 + (3 * q + 1) // RING)
                        evac(0, ft(WORK[half], i * 4 + q), ACT.Sigmoid).then_inc(set_read[0], 1)

            def gla_all(half):
                def stage(c, par, L):
                    src = fa[:, QKV[half]:QKV[half] + 8 * N].rearrange("p (k n) -> p k n", k=8)[:, :, bass.ds(c * C, L)]
                    act.activation(fv(O_ST[par], 8 * L).rearrange("p (k n) -> p k n", k=8), src, ACT.Copy
                                   ).then_inc(stage_ready, 1)

                def exps(n, par, dec):
                    act.wait_ge(diff_ready, n + 1)
                    de = O_DE[par]
                    spans = [(0, DE_W)]
                    if dec:
                        spans = [(l * 256, 2 * DT) for l in DEC_LEVELS] + [(DE_K, 2 * DT), (DE_Q, 2 * DT)]
                    for at, w in spans:
                        last = act.activation(fv(de + at, w), fv(de + at, w), ACT.Exp)
                    last.then_inc(exp_ready, 1)

                def rows_out(c, par):
                    L = DT if isinstance(c, int) and c == CHUNKS else C
                    n = n0 + c
                    act.wait_ge(vt_done, n + 1)
                    if not isinstance(c, int) or c >= 2:
                        act.wait_ge(o_done, n - 1)
                    act.activation(fa[0:L, O_VT[par]:O_VT[par] + 512], ps[0:L, 6, :], ACT.Copy).then_inc(vt_ready, 1)
                    act.wait_ge(kht_done, n + 1)
                    act.wait_ge(sup_done, n)
                    act.activation(khT[0:L, :], ps[0:L, 7, 0:256], ACT.Copy).then_inc(kht_ready, 1)

                def chunk(c, par):
                    dec = isinstance(c, int) and c == CHUNKS
                    L = DT if dec else C
                    n = n0 + c
                    last = isinstance(c, int) and c == CHUNKS - 2
                    ahead = not isinstance(c, int) or c + 2 <= CHUNKS
                    if not dec:
                        rows_out(c + 1, 1 - par)
                    if ahead:
                        act.wait_ge(level_done, n + 1)
                        stage(c + 2, par, DT if last else C)
                    act.wait_ge(o_done, n + 1)
                    v_cols = fa[:, QKV[half] + 4 * N:QKV[half] + 8 * N].rearrange("p (k n) -> p k n", k=4)[:, :, bass.ds(c * C, L)]
                    act.activation(v_cols.rearrange("p (t a) n -> p a t n", a=2),
                                   ps[:, 4:6, 256:256 + 2 * L].rearrange("p a (t n) -> p a t n", t=2), ACT.Copy
                                   ).then_inc(o_read, 1)
                    if ahead:
                        exps(n + 2, par, last)

                block_used(half, 3, IT_M1 + 5)
                n0 = half * (CHUNKS + 1)
                for c in range(2):
                    stage(c, c, C)
                    exps(n0 + c, c, False)
                rows_out(0, 0)
                for par in range(2):
                    chunk(par, par)
                with act.Fori(1, CHUNKS // 2 - 1) as i:
                    for par in range(2):
                        chunk(i * 2 + par, par)
                chunk(CHUNKS - 2, 0)
                chunk(CHUNKS - 1, 1)
                act.dma_start(fv(O_S0, DS * 2 * DV), gladec_d[half]).then_inc(s0_landed, 16)
                chunk(CHUNKS, 0)
                act.wait_ge(s0_ready, half + 1)
                act.dma_start(gla_dec_out[half], fv(O_S0, DS * 2 * DV)).then_inc(out_stored, 16)
                act.wait_ge(out_stored, (half + 1) * 32)
                act.wait_ge(o_read, (half + 1) * (CHUNKS + 1))
                for h in range(HEADS):
                    act.activation(ft(A_O, h), ft(QKV[half], 4 + h), ACT.Square).then_inc(osq_ready, 1)
                for h in range(HEADS):
                    block_used(half, 2 * (h % 2) + 1, IT_R + h // 2)
                    if h:
                        act.wait_ge(full_ready, full_count(half, SP_OG + h))
                    evac(0, ft(A_G, 0), ACT.Silu).then_inc(set_read[0], 1)
                    act.wait_ge(set_read[1], set_count(half, 1, "r", h + 1))
                    act.activation(ft(A_G, 1), ft(A_G, 1), ACT.Sqrt).then_inc(gstd_ready, 1)
                    act.wait_ge(full_ready, full_count(half, SP_OG + h + 1))
                    act.activation(rt(A_O, h), ft(QKV[half], 4 + h), ACT.Copy).then_inc(hi_ready, 1)
                act.wait_ge(split_ready, half * SP_ALL + SP_OG + HEADS)
                with act.Fori(0, 2) as i:
                    for q in range(4):
                        block_used(half, (3 * q + 1) % RING, IT_M2 + i * 3 + (3 * q + 1) // RING)
                        evac(0, ft(A_G, q % 2), ACT.Sigmoid).then_inc(set_read[0], 1)
                        act.wait_ge(full_ready, full_count(half, SP_MG + i * 4 + q + 1))
                        act.activation(rt(QKV[half], i * 4 + q), ft(WORK[half], i * 4 + q), ACT.Copy).then_inc(hi_ready, 1)

            def out_and_ff(half):
                block_used(half, 3, IT_M2 + 5)
                act.dma_start(fv(X_HI[half], 8 * N), xT[half]).then_inc(res_landed, 16)
                norm_squares(X_HI[half], A_O,
                             lambda k: act.wait_ge(set_read[k % 2], set_count(half, k % 2, "out", k // 2 + 1)))
                norm_root(NORM[half]["ffn"])
                high_parts(half, SP_H2, KT_D, WORK[half], QKV[half])

                def hidden(g, par):
                    for q in range(4):
                        block_used(half, 2 * (q % 2) + 1, IT_FF + ff_it(g, "up") + q // 2)
                        before = max(4 * g + q - 1, 0) if isinstance(g, int) else 4 * g + q - 1
                        act.wait_ge(hidden_split, half * FF_GROUPS * 4 + before)
                        evac(q % 2, ft(A_G, q % 2), ACT.Relu).then_inc(set_read[q % 2], 1)
                        act.drain()
                        act.activation(rt(X_LO[half] if par == 0 else A_O, q), ft(A_G, q % 2), ACT.Square
                                       ).then_inc(hidden_hi, 1)

                act.wait_ge(split_ready, (half + 1) * SP_ALL)
                hidden(0, 0)
                hidden(1, 1)
                with act.Fori(0, FF_GROUPS // 2 - 1) as i:
                    for par in range(2):
                        hidden(i * 2 + par + 2, par)

                if half + 1 < HALVES:
                    input_load(half + 1)
                    input_norm(half + 1)
                    return
                norm_squares(X_HI[half], X_LO[half],
                             lambda k: act.wait_ge(set_read[k % 2], (half + 1) * SET_TOTAL[k % 2] - 3 + k // 2))
                norm_root(NORM[half]["y"])
                store_output(half)

            act.dma_start(sml[:, 0:3, :], s5small).then_inc(s5in_landed, 16)
            for dst, src in consts:
                act.dma_start(dst, src).then_inc(const_landed, 16)
            input_load(0)
            for dst, src in mask_floats:
                act.dma_start(dst, src).then_inc(masks_landed, 16)
            act.wait_ge(s5in_landed, 16)
            act.activation(small("dt"), small("logdt"), ACT.Exp).then_inc(dt_ready, 1)
            act.wait_ge(trig_in, 1)
            act.activation(small("mag"), small("lrdt"), ACT.Exp)
            act.activation(small("sin"), small("ang"), ACT.Sin)
            act.activation(small("sinh"), small("ang"), ACT.Sin, scale=0.5).then_inc(trig_out, 1)
            input_norm(0)
            for half in range(HALVES):
                project(half)
                if half == 0:
                    s5_pairs_out()
                    u_by_chunks(0)
                    log_gates(0)
                s5(half)
                gla_all(half)
                out_and_ff(half)
            act.dma_start(s5_prompt, s5_carry[:, :, :]).then_inc(out_stored, 16)
            act.dma_start(gla_prompt, gla_s[:, 0, :, :]).then_inc(out_stored, 16)
            act.wait_ge(out_stored, 16 * (2 * HALVES + 2))
            act.wait_ge(y_stored, 16 * HALVES * KT_D)

        @block.vector
        def _(dve):
            def tt(out, a, b, op):
                return dve.tensor_tensor(out, a, b, op)

            def block_used(half, place, it):
                dve.wait_ge(w_used[place], half * ITERS + it + 1)

            def low_part(half, n, full, hi, lo):
                dve.wait_ge(hi_ready, half * SP_ALL + n + 1)
                tt(lo, full, hi, ALU.subtract).then_inc(split_ready, 1)

            def mean_square(s, dst, width):
                for src, d in zip(psum_cols(s), cols(dst)):
                    last = dve.tensor_scalar(d, src, 1.0 / width, EPS, ALU.mult, ALU.add)
                last.then_inc(set_read[s], 1)

            def norm_add(n, squares, k):
                dve.wait_ge(sq_ready, n * KT_D + k + 1)
                if k:
                    dve.drain()
                    last = tt(ft(squares), ft(squares), ft(squares, k), ALU.add)
                    if k == KT_D - 1:
                        last.then_inc(ssum_ready, 1)

            def norm_root(n):
                for b, (c0, cn) in enumerate(BLK):
                    dve.wait_ge(ms_done, 3 * n + b + 1)
                    dve.tensor_scalar(ft(A_G)[:, c0:c0 + cn], ps[:, 6 + b % 2, 0:cn], 1.0 / D_MODEL, EPS,
                                      ALU.mult, ALU.add).then_inc(ms_read, 1)
                dve.wait_ge(std_ready, n + 1)
                dve.reciprocal(ft(A_G), ft(A_G))
                dve.drain()

            def norm_scale(src, full, gain, k):
                return dve.scalar_tensor_tensor(ft(full, k), ft(src, k), vec[:, gain + k:gain + k + 1], ft(A_G),
                                                ALU.mult, ALU.mult)

            def input_tile(half, k):
                if k < KT_D:
                    norm_scale(X_LO[half], X_LO[half], V_MIX, k).then_inc(full_ready, 1)
                if k:
                    low_part(half, SP_X + k - 1, ft(X_LO[half], k - 1), hf(X_HI[half], k - 1), rt(X_LO[half], k - 1))

            def output_norm(half):
                for k in range(KT_D):
                    norm_add(NORM[half]["y"], X_LO[half], k)
                output_scale(half)

            def output_scale(half):
                norm_root(NORM[half]["y"])
                for k in range(KT_D):
                    norm_scale(X_HI[half], X_HI[half], V_FIN, k).then_inc(y_ready, 1)

            def trig_angles():
                s = small
                dve.wait_ge(dt_ready, 1)
                steps = [
                    lambda: dve.tensor_scalar(s("lr"), s("lam_re"), -1e-4, None, ALU.min),
                    lambda: tt(s("lrdt"), s("lr"), s("dt"), ALU.mult),
                    lambda: tt(s("th"), s("lam_im"), s("dt"), ALU.mult),
                    lambda: dve.tensor_scalar(s("t0"), s("th"), float(0.5 / np.pi), MAGIC, ALU.mult, ALU.add),
                    lambda: dve.tensor_scalar(s("t0"), s("t0"), MAGIC, None, ALU.subtract),
                    lambda: dve.scalar_tensor_tensor(s("th"), s("t0"), -PI2_1, s("th"), ALU.mult, ALU.add),
                    lambda: dve.scalar_tensor_tensor(s("th"), s("t0"), -PI2_2, s("th"), ALU.mult, ALU.add),
                    lambda: dve.scalar_tensor_tensor(s("th"), s("t0"), -PI2_3, s("th"), ALU.mult, ALU.add),
                ]
                for f in steps:
                    f()
                    dve.drain()
                dve.tensor_scalar(s("ang"), s("th"), 3.1415925, -3.1415925, ALU.min, ALU.max).then_inc(trig_in, 1)

            def trig():
                s = small
                dve.wait_ge(trig_out, 1)

                def seq(*ops):
                    for out, a, b, op in ops:
                        tt(out, a, b, op)
                        dve.drain()
                seq((s("t0"), s("sinh"), s("sinh"), ALU.mult))
                dve.tensor_scalar(s("cos"), s("t0"), -2.0, 1.0, ALU.mult, ALU.add)
                dve.drain()
                seq((s("ar"), s("mag"), s("cos"), ALU.mult), (s("ai"), s("mag"), s("sin"), ALU.mult),
                    (s("t0"), s("lr"), s("lr"), ALU.mult), (s("t1"), s("lam_im"), s("lam_im"), ALU.mult),
                    (s("t0"), s("t0"), s("t1"), ALU.add))
                dve.reciprocal(s("t0"), s("t0"))
                dve.tensor_scalar(s("t1"), s("ar"), -1.0, None, ALU.add)
                dve.drain()
                seq((s("fr"), s("t1"), s("lr"), ALU.mult), (s("t2"), s("ai"), s("lam_im"), ALU.mult),
                    (s("fr"), s("fr"), s("t2"), ALU.add), (s("fr"), s("fr"), s("t0"), ALU.mult),
                    (s("fi"), s("ai"), s("lr"), ALU.mult), (s("t2"), s("t1"), s("lam_im"), ALU.mult),
                    (s("fi"), s("fi"), s("t2"), ALU.subtract), (s("fi"), s("fi"), s("t0"), ALU.mult))
                pr, pi = (lambda k: sml[:, SMALL.index("pr") + k, :]), (lambda k: sml[:, SMALL.index("pi") + k, :])
                dve.memset(pr(0), 1.0)
                dve.memset(pi(0), 0.0)
                dve.drain()
                for k in range(J):
                    seq((s("t0"), pr(k), s("ar"), ALU.mult), (s("t1"), pi(k), s("ai"), ALU.mult),
                        (pr(k + 1), s("t0"), s("t1"), ALU.subtract),
                        (s("t0"), pr(k), s("ai"), ALU.mult), (s("t1"), pi(k), s("ar"), ALU.mult),
                        (pi(k + 1), s("t0"), s("t1"), ALU.add))
                for q, p4 in ((0, pr(4)), (1, pi(4))):
                    dve.tensor_copy(s5_a4[:, q, :], p4)
                seq((s5_m8[:, :], s("mag"), s("mag"), ALU.mult), (s5_m8[:, :], s5_m8[:, :], s5_m8[:, :], ALU.mult),
                    (s5_m8[:, :], s5_m8[:, :], s5_m8[:, :], ALU.mult))
                for _ in range(3):
                    square_phasor(s("cos"), s("sin"), s("cos"), s("sin"))

            def square_phasor(oc, os_, c, s_):
                t0, t1, t2 = small("t0"), small("t1"), small("t2")
                for out, a, b, op in ((t0, c, c, ALU.mult), (t1, s_, s_, ALU.mult), (t2, c, s_, ALU.mult),
                                      (t0, t0, t1, ALU.subtract)):
                    tt(out, a, b, op)
                    dve.drain()
                dve.tensor_scalar(t1, t2, 2.0, None, ALU.mult)
                dve.drain()
                tt(t2, t0, t0, ALU.mult)
                dve.drain()
                tt(small("t3"), t1, t1, ALU.mult)
                dve.drain()
                tt(t2, t2, small("t3"), ALU.add)
                dve.drain()
                dve.tensor_scalar(t2, t2, -0.5, 1.5, ALU.mult, ALU.add)
                dve.drain()
                tt(oc, t0, t2, ALU.mult)
                tt(os_, t1, t2, ALU.mult)
                dve.drain()

            def cmul(o_re, o_im, a_re, a_im, b_re, b_im, t0, t1, conj_sum=False):
                tt(t0, a_re, b_re, ALU.mult)
                tt(t1, a_im, b_im, ALU.mult)
                dve.drain()
                tt(o_re, t0, t1, ALU.subtract)
                dve.drain()
                tt(t0, a_re, b_im, ALU.mult)
                tt(t1, a_im, b_re, ALU.mult)
                dve.drain()
                tt(o_im, t0, t1, ALU.add)
                dve.drain()

            def s5_tables():
                pr, pi = (lambda k: sml[:, SMALL.index("pr") + k, :]), (lambda k: sml[:, SMALL.index("pi") + k, :])

                def g3(at):
                    return fv(at, 256).rearrange("p (t h) -> p t h", t=PAIRS)

                def over_h(a):
                    return a.unsqueeze(2).to_broadcast([P, PAIRS, S5_GROUP])
                b_re, b_im, c_re, c_im = (g3(A_G + 256 * q) for q in range(4))
                bb_re, bb_im, t0, t1 = (g3(A_G + 1024 + 256 * q) for q in range(4))
                dve.wait_ge(bc_landed, 32)
                cmul(bb_re, bb_im, over_h(small("fr")), over_h(small("fi")), b_re, b_im, t0, t1)
                q_all = fv(A_M, 4096).rearrange("p (t q j h) -> p t q j h", t=PAIRS, q=2, j=J)
                for j in range(J):
                    cmul(q_all[:, :, 0, j, :], q_all[:, :, 1, j, :], over_h(pr(j + 1)), over_h(pi(j + 1)),
                         c_re, c_im, t0, t1)
                    last = dve.tensor_scalar(q_all[:, :, 1, j, :], q_all[:, :, 1, j, :], -1.0, None, ALU.mult)
                last.then_inc(qe_ready, 1)
                e = fv(A_M + 4096, PAIRS * 2 * EC).rearrange("p (t q c) -> p t q c", t=PAIRS, q=2)
                dve.memset(e[:, :, 0, 0:1], 1.0)
                dve.memset(e[:, :, 1, 0:1], 0.0)
                cc, ss = small("cos"), small("sin")
                tmp = [fv(O_TAB + TAB_W * PAIRS * q, TAB_W * PAIRS) for q in range(2)]
                n = 1
                while n <= NC:
                    dve.tensor_copy(e[:, :, 0, n:n + 1], cc.unsqueeze(2))
                    dve.tensor_copy(e[:, :, 1, n:n + 1], ss.unsqueeze(2))
                    dve.drain()
                    for a in range(1, min(n, NC + 1 - n), TAB_W):
                        m = min(TAB_W, min(n, NC + 1 - n) - a)
                        wc, ws = (x.unsqueeze(2).to_broadcast([P, PAIRS, m]) for x in (cc, ss))
                        t0w, t1w = (x[:, 0:PAIRS * m].rearrange("p (t m) -> p t m", t=PAIRS) for x in tmp)
                        cmul(e[:, :, 0, n + a:n + a + m], e[:, :, 1, n + a:n + a + m], wc, ws,
                             e[:, :, 0, a:a + m], e[:, :, 1, a:a + m], t0w, t1w)
                    n *= 2
                    if n <= NC:
                        square_phasor(cc, ss, cc, ss)
                dve.memset(e[:, :, :, NC + 1:EC], 0.0).then_inc(qe_ready, 1)
                dve.wait_ge(qe_stored, 32)
                g_re, g_im = (fv(A_M + 3840 * q, 3840).rearrange("p (t s h) -> p t s h", t=PAIRS, s=15)
                              for q in range(2))
                dve.memset(fv(A_M, 2 * 3840), 0.0)
                dve.drain()
                for s in range(J):
                    cmul(g_re[:, :, s, :], g_im[:, :, s, :], over_h(pr(J - 1 - s)), over_h(pi(J - 1 - s)),
                         bb_re, bb_im, t0, t1)
                dve.wait_ge(cbd_landed, 16)
                dve.tensor_scalar(fv(A_G + 512, 512), fv(A_G + 512, 512), -1.0, None, ALU.mult).then_inc(g_ready, 1)

            def s5_pairs():
                dve.tensor_copy(fv(O_SHIFT, P), ident[:, :])
                dve.memset(fv(O_SHIFT + P, P), 0.0)
                def by_group(at):
                    return fv(at, 512).rearrange("p (g h) -> p g h", h=S5_GROUP)
                tt(by_group(G_SKIP), ident[:, P - S5_GROUP:P].unsqueeze(1).to_broadcast([P, S5_GROUPS, S5_GROUP]),
                   dcol[:, :].unsqueeze(2).to_broadcast([P, S5_GROUPS, S5_GROUP]), ALU.mult)
                dve.drain()
                dve.wait_ge(k_done, 1)
                tt(fv(G_K, 512), ps[:, 0, 0:512], fv(G_SKIP, 512), ALU.add).then_inc(k_ready, 1)
                dve.wait_ge(u_stored, 16)
                for j in range(J):
                    dve.wait_ge(shift_done, j + 1)
                    out = fv(O_STG_T, PAIRS * 256).rearrange("p (g j h) -> p g j h", g=S5_GROUPS, j=J)[:, :, j, :]
                    dve.tensor_copy(out, ps[:, j % 4, 0:512].rearrange("p (g h) -> p g h", h=S5_GROUP)
                                    ).then_inc(t_ready, 1)

            def s5(half):
                T = [WORK[half] + WORK_TMP + 130 * q for q in range(4)]
                W = [WORK[half] + WORK_TMP + 520 + 130 * q for q in range(2)]

                def pair(i, r):
                    t = i * CR + r
                    st = WORK[half] + WORK_TMP + 800 + (r % 2) * 2 * YC
                    at = C_SLOT[half][r]

                    def ec(a, n):
                        return fv(at + C_EC + a, n)

                    def es(a, n):
                        return fv(at + C_ES + a, n)
                    col = (lambda q: s5_carry[:, q, t:t + 1]) if isinstance(t, int) else (
                        lambda q: s5_carry[:, q, bass.ds(t, 1)])
                    dve.wait_ge(chunk_in_done, half * PAIRS + t + 1)
                    xr, xi = ps[:, 6 + r % 2, 0:NC], ps[:, 6 + r % 2, UC:UC + NC]
                    tt(fv(T[0], NC), ec(1, NC), xr, ALU.mult)
                    tt(fv(T[1], NC), es(1, NC), xi, ALU.mult)
                    tt(fv(T[2], NC), ec(1, NC), xi, ALU.mult)
                    tt(fv(T[3], NC), es(1, NC), xr, ALU.mult)
                    dx = ps[:, 6 + r % 2, 0:2 * UC].rearrange("p (q c) -> p q c", q=2)[:, :, NC + DS:UC]
                    tb = bass.ds(t, 1)
                    dve.tensor_copy(s5_new[:, :, tb, :].rearrange("p q o s -> p q (o s)"), dx
                                    ).then_inc(chunk_in_read, 1)
                    for q in range(2):
                        dve.tensor_copy(fv(W[q], 1), col(q))
                    dve.drain()
                    tt(fv(T[0], NC), fv(T[0], NC), fv(T[1], NC), ALU.add)
                    tt(fv(T[2], NC), fv(T[2], NC), fv(T[3], NC), ALU.subtract)
                    dve.drain()
                    m8 = s5_m8[:, bass.ds(t, 1)].to_broadcast([P, NC])
                    for q in range(2):
                        dve.tensor_tensor_scan(fv(W[q] + 1, NC), m8, fv(T[2 * q], NC), fv(W[q], 1), ALU.mult, ALU.add)
                    dve.drain()
                    tt(fv(T[0], NC + 1), ec(0, NC + 1), fv(W[0], NC + 1), ALU.mult)
                    tt(fv(T[1], NC + 1), es(0, NC + 1), fv(W[1], NC + 1), ALU.mult)
                    tt(fv(T[2], NC + 1), es(0, NC + 1), fv(W[0], NC + 1), ALU.mult)
                    tt(fv(T[3], NC + 1), ec(0, NC + 1), fv(W[1], NC + 1), ALU.mult)
                    dve.drain()
                    dve.wait_ge(yrow_done, half * PAIRS + (max(t - 1, 0) if isinstance(t, int) else t - 1))
                    for q, op in ((0, ALU.subtract), (1, ALU.add)):
                        tt(col(q), fv(T[2 * q] + NC, 1), fv(T[2 * q + 1] + NC, 1), op)
                        dve.tensor_copy(fv(st + q * YC + NC, DS), s5_dec[:, q, tb, :].rearrange("p o s -> p (o s)"))
                        last = tt(fv(st + q * YC, NC), fv(T[2 * q], NC), fv(T[2 * q + 1], NC), op)
                    last.then_inc(state_ready, 1)
                    dve.drain()

                dve.wait_ge(s5dec_landed, (half + 1) * 16)
                if half == 0:
                    dve.memset(s5_carry[:, :, :], 0.0)
                    dve.drain()
                else:
                    dve.wait_ge(out_stored, 32)
                for r in range(CR):
                    pair(0, r)
                with dve.Fori(1, PAIRS // CR) as i:
                    for r in range(CR):
                        pair(i, r)

                def wide(q):
                    return s5_a4[:, q, :].unsqueeze(2).to_broadcast([P, PAIRS, DS])
                dre, dim = s5_dec[:, 0, :, :], s5_dec[:, 1, :, :]
                nre, nim = s5_new[:, 0, :, :], s5_new[:, 1, :, :]
                t0, t1 = s5_tmp[:, 0, :, :], s5_tmp[:, 1, :, :]
                tt(t0, wide(0), dre, ALU.mult)
                tt(t1, wide(1), dim, ALU.mult)
                dve.drain()
                tt(nre, nre, t0, ALU.add)
                dve.drain()
                tt(nre, nre, t1, ALU.subtract)
                tt(t0, wide(0), dim, ALU.mult)
                dve.drain()
                tt(t1, wide(1), dre, ALU.mult)
                tt(nim, nim, t0, ALU.add)
                dve.drain()
                tt(nim, nim, t1, ALU.add).then_inc(s5dec_ready, 1)

            def gla_all(half):
                def halves(ap, s):
                    v = ap.rearrange("p t (b two s) -> p t b two s", two=2, s=s)
                    return v[:, :, :, 0, :], v[:, :, :, 1, :]

                def two(at, L):
                    return fv(at, 2 * L).rearrange("p (t n) -> p t n", t=2)

                def levels(dec):
                    return DEC_LEVELS if dec else range(NL)

                def log_sums(c, L):
                    return fa[:, A_G:A_G + 2 * N].rearrange("p (t n) -> p t n", t=2)[:, :, bass.ds(c * C, L)]

                def diffs(c, par, dec, some=None):
                    L = DT if dec else C
                    for l in (levels(dec) if some is None else some):
                        s = LEVELS[l]
                        bl, br = halves(log_sums(c, L), s)
                        mid = bl[:, :, :, s - 1:s].to_broadcast([P, 2, L // (2 * s), s])
                        left, right = halves(two(O_DE[par] + l * 256, L), s)
                        tt(right, br, mid, ALU.subtract)
                        tt(left, mid, bl, ALU.subtract)

                def end_diffs(c, par, dec):
                    L = DT if dec else C
                    w = DEC_SEQ if dec else C
                    b = log_sums(c, L)
                    bb = b.rearrange("p t (b s) -> p t b s", s=w)
                    tt(two(O_DE[par] + DE_K, L).rearrange("p t (b s) -> p t b s", s=w),
                       bb[:, :, :, w - 1:w].to_broadcast([P, 2, L // w, w]), bb, ALU.subtract)
                    dve.tensor_copy(two(O_DE[par] + DE_Q, L), b).then_inc(diff_ready, 1)

                def products(c, par, dec):
                    L = DT if dec else C
                    n, de = n0 + c, O_DE[par]
                    q, k = two(O_ST[par], L), two(O_ST[par] + 2 * L, L)
                    dve.wait_ge(exp_ready, n + 1)
                    dve.wait_ge(stage_ready, n + 1)
                    w = DEC_SEQ if dec else C
                    dve.tensor_copy(decay[:, par, 0:2 * L // w],
                                    fv(de + DE_Q, 2 * L).rearrange("p (b s) -> p b s", s=w)[:, :, w - 1])
                    dve.drain()
                    for l in levels(dec):
                        left, right = halves(two(de + l * 256, L), LEVELS[l])
                        tt(right, right, halves(q, LEVELS[l])[1], ALU.mult)
                        tt(left, left, halves(k, LEVELS[l])[0], ALU.mult)
                    tt(two(de + DE_Q, L), two(de + DE_Q, L), q, ALU.mult)
                    tt(two(de + DE_K, L), two(de + DE_K, L), k, ALU.mult).then_inc(mul_ready, 1)

                def weights(dec, some, diagonal):
                    L = DT if dec else C
                    mk = dmask if dec else masks
                    att = fa[0:L, O_ATT:O_ATT + 4 * L]
                    for l in some:
                        s, x = LEVELS[l], list(levels(dec)).index(l)
                        out = att.rearrange("p (a b two s) -> p a b two s", a=2, two=2, s=s)[:, :, :, 1, :]
                        m = mk[0:L, x * 2 * L:(x + 1) * 2 * L].rearrange("p (a b s) -> p a b s", a=2, s=s)
                        bank, col = 2 * (l * 128 // 512), l * 128 % 512
                        src = ps[0:L, bank:bank + 2, col:col + L].rearrange("p a (b s) -> p a b s", s=s)
                        dve.copy_predicated(out, m, src)
                        dve.drain()
                    if diagonal:
                        x = len(levels(dec)) * 2 * L
                        dve.copy_predicated(att.rearrange("p (a n) -> p a n", a=2),
                                            mk[0:L, x:x + 4 * L].rearrange("p (a n) -> p a n", a=2),
                                            ps[0:L, 4:6, 0:2 * L]).then_inc(att_ready, 1)

                block_used(half, 3, IT_M1 + 5)
                dve.memset(fv(O_ATT, HEADS * C), 0.0)
                if half == 0:
                    dve.memset(gla_s[:, 0, :, :], 0.0).then_inc(s_ready, 1)
                n0 = half * (CHUNKS + 1)
                for c in range(2):
                    diffs(c, c, False)
                    end_diffs(c, c, False)
                products(0, 0, False)

                def chunk(c, par):
                    n = n0 + c
                    known = isinstance(c, int)
                    products(c + 1, 1 - par, known and c == CHUNKS - 1)
                    dve.drain()
                    dve.wait_ge(o_done, n)
                    dve.wait_ge(sup_done, n + 1)
                    dve.wait_ge(level_a_done, half * CHUNKS + c + 1)
                    for t in range(2):
                        ins = dve.scalar_tensor_tensor(gla_s[:, 1 - par, t, :], gla_s[:, par, t, :],
                                                       decay[:, par, t:t + 1],
                                                       ps[:, 7, 256 + t * DV:256 + (t + 1) * DV], ALU.mult, ALU.add)
                    ins.then_inc(s_ready, 1)
                    weights(False, range(NL_A), False)
                    dve.wait_ge(level_done, n + 1)
                    ahead, dec = not known or c + 2 <= CHUNKS, known and c + 2 == CHUNKS
                    if ahead:
                        diffs(c + 2, par, dec, [NL - 1])
                    weights(False, range(NL_A, NL), True)
                    if ahead:
                        diffs(c + 2, par, dec, list(levels(dec))[:-1])
                        dve.wait_ge(o_done, n + 1)
                        end_diffs(c + 2, par, dec)

                for par in range(2):
                    chunk(par, par)
                with dve.Fori(1, CHUNKS // 2 - 1) as i:
                    for par in range(2):
                        chunk(i * 2 + par, par)
                chunk(CHUNKS - 2, 0)
                chunk(CHUNKS - 1, 1)
                n = n0 + CHUNKS
                dve.wait_ge(o_done, n)
                dve.wait_ge(level_done, n + 1)
                dve.memset(fv(O_ATT, HEADS * C), 0.0)
                dve.drain()
                weights(True, DEC_LEVELS, True)
                dve.wait_ge(kht_ready, n + 1)
                for s in range(DS):
                    ins = dve.tensor_scalar(fa[0:DT, O_KTM + s * 256:O_KTM + (s + 1) * 256], khT[0:DT, :],
                                            vec[0:DT, V_SEQ + s:V_SEQ + s + 1], None, ALU.mult)
                ins.then_inc(ktm_ready, 1)
                dve.wait_ge(sup_done, n + 1)
                for s in range(DS):
                    for t in range(2):
                        col = (s * 2 + t) * DV
                        ins = dve.scalar_tensor_tensor(fv(O_S0 + col, DV), fv(O_S0 + col, DV),
                                                       decay[:, 0, t * DS + s:t * DS + s + 1],
                                                       ps[:, col // 512, col % 512:col % 512 + DV], ALU.mult, ALU.add)
                ins.then_inc(s0_ready, 1)

            def merge(half):
                for h in range(HEADS):
                    dve.wait_ge(gms_done, half * HEADS + h + 1)
                    dve.drain()
                    mean_square(1, ft(A_G, 1), DV)
                    dve.wait_ge(gstd_ready, half * HEADS + h + 1)
                    dve.reciprocal(ft(A_G, 1), ft(A_G, 1))
                    dve.drain()
                    z = ft(QKV[half], 4 + h)
                    dve.scalar_tensor_tensor(z, z, vec[:, V_GLA:V_GLA + 1], ft(A_G, 1), ALU.mult, ALU.mult)
                    dve.wait_ge(set_read[0], set_count(half, 0, "r", h + 1))
                    dve.drain()
                    tt(z, z, ft(A_G, 0), ALU.mult).then_inc(full_ready, 1)
                    low_part(half, SP_OG + h, z, hf(A_O, h), rt(A_O, 4 + h))
                with dve.Fori(0, 2) as i:
                    for q in range(4):
                        m = i * 4 + q
                        dve.wait_ge(set_read[0], set_count(half, 0, "m2", m + 1))
                        block_used(half, (3 * q + 2) % RING, IT_M2 + i * 3 + (3 * q + 2) // RING)
                        g = ft(A_G, q % 2)
                        for src, d in zip(psum_cols(1), cols(g)):
                            last = tt(d, d, src, ALU.mult)
                        last.then_inc(set_read[1], 1)
                        dve.drain()
                        tt(ft(WORK[half], m), ft(WORK[half], m), g, ALU.add).then_inc(full_ready, 1)
                        low_part(half, SP_MG + m, ft(WORK[half], m), hf(QKV[half], m), rt(WORK[half], m))

            def add_tile(s, dst):
                for src, d in zip(psum_cols(s), cols(dst)):
                    last = tt(d, d, src, ALU.add)
                last.then_inc(set_read[s], 1)

            def hidden(half, g, par):
                for q in range(4):
                    dve.wait_ge(hidden_hi, half * FF_GROUPS * 4 + 4 * g + q + 1)
                    r, hb = ft(A_G, q % 2), X_LO[half] if par == 0 else A_O
                    tt(r, r, r, ALU.mult)
                    dve.drain()
                    tt(rt(hb, 4 + q), r, hf(hb, q), ALU.subtract).then_inc(hidden_split, 1)

            def output_tile(half, g, m):
                block_used(half, m % RING, IT_FF + ff_it(g, "down") + m // RING)
                add_tile(m % 2, ft(X_HI[half], m))

            def outputs(half, g):
                for m in range(KT_D):
                    output_tile(half, g, m)

            dve.memset(ones[:, :], 1.0).then_inc(ones_ready, 1)
            trig_angles()
            for half in range(HALVES):
                if half == 0:
                    for k in range(KT_D):
                        norm_add(NORM[0]["x"], X_HI[0], k)
                    norm_root(NORM[0]["x"])
                    dve.wait_ge(const_landed, 16 * len(consts))
                    for k in range(KT_D + 1):
                        input_tile(0, k)
                    dve.wait_ge(masks_landed, 16 * len(mask_floats))
                    dve.tensor_copy(masks[:, :], fv(A_Z, NL * 256 + 512))
                    dve.tensor_copy(dmask[:, :], fa[0:DT, A_Z + 4096:A_Z + 4096 + dmask.shape[1]])
                up = fv(O_UP, KT_S * J * UC).rearrange("p (m j c) -> p m j c", m=KT_S, j=J)
                dve.memset(up[:, :, DEC_SEQ:J, NC:NC + DS], 0.0).then_inc(u_pad, 1)
                dve.memset(up[:, :, 0:DEC_SEQ, NC + DS:UC], 0.0).then_inc(u_pad, 1)
                if half:
                    output_norm(half - 1)
                dve.wait_ge(wa_landed, (half + 1) * 16)
                dve.tensor_copy(ra[:, O_AH:O_AH + KT_D * P], fv(O_A, KT_D * P))
                dve.drain()
                tt(ra[:, O_AL:O_AL + KT_D * P], fv(O_A, KT_D * P), ra[:, O_AH:O_AH + KT_D * P].bitcast(F32), ALU.subtract
                   ).then_inc(wa_split, 1)
                if half == 0:
                    trig()
                    s5_tables()
                    s5_pairs()
                for t in range(2):
                    dve.wait_ge(gln_ready, half * 2 + t + 1)
                    g = ft(A_G, t)
                    dve.scalar_tensor_tensor(g, g, 0.0, ft(O_T), ALU.min, ALU.subtract).then_inc(gmin_ready, 1)
                    dve.drain()
                    dve.tensor_scalar(g, g, 1.0 / TAU, None, ALU.mult)
                    dve.drain()
                    spans = [(c * C, C) for c in range(CHUNKS)] + [(TP + s * DEC_SEQ, DEC_SEQ) for s in range(DS)]
                    for a, w in spans:
                        last = dve.tensor_tensor_scan(g[:, a:a + w], ones[:, 0:w], g[:, a:a + w], 0.0,
                                                      ALU.mult, ALU.add)
                last.then_inc(b_ready, 1)
                s5(half)
                for m in range(KT_S):
                    low_part(half, SP_Z5 + m, ft(WORK[half], m), hf(A_O, m), rt(A_O, 4 + m))
                for m in range(KT_S):
                    dve.wait_ge(set_read[m % 2], set_count(half, m % 2, "glu", m // 2 + 1))
                    tt(ft(WORK[half], m), ft(WORK[half], m), ft(WORK[half], 4 + m), ALU.mult).then_inc(full_ready, 1)
                for m in range(KT_S):
                    low_part(half, SP_O5 + m, ft(WORK[half], m), hf(A_O, m), rt(A_O, 4 + m))
                with dve.Fori(0, 2) as i:
                    for q in range(4):
                        m = i * 4 + q
                        dve.wait_ge(set_read[0], set_count(half, 0, "m1", m + 1))
                        block_used(half, (3 * q + 2) % RING, IT_M1 + i * 3 + (3 * q + 2) // RING)
                        for src, d in zip(psum_cols(1), cols(ft(WORK[half], m))):
                            last = tt(d, d, src, ALU.mult)
                        last.then_inc(set_read[1], 1)
                gla_all(half)
                merge(half)
                dve.wait_ge(res_landed, (half + 1) * 16)
                for m in range(KT_D):
                    block_used(half, 2 * (m % 2) + 1, IT_OUT + m // 2)
                    add_tile(m % 2, ft(X_HI[half], m))
                    if m:
                        norm_add(NORM[half]["ffn"], A_O, m - 1)
                norm_add(NORM[half]["ffn"], A_O, KT_D - 1)
                norm_root(NORM[half]["ffn"])
                for k in range(KT_D + 1):
                    if k < KT_D:
                        norm_scale(X_HI[half], WORK[half], V_FFN, k).then_inc(full_ready, 1)
                    if k:
                        low_part(half, SP_H2 + k - 1, ft(WORK[half], k - 1), hf(QKV[half], k - 1),
                                 rt(WORK[half], k - 1))
                hidden(half, 0, 0)
                hidden(half, 1, 1)
                with dve.Fori(0, FF_GROUPS // 2 - 1) as i:
                    for par in range(2):
                        outputs(half, i * 2 + par)
                        hidden(half, i * 2 + par + 2, par)
                if half + 1 == HALVES:
                    outputs(half, FF_GROUPS - 2)
                    for m in range(KT_D):
                        output_tile(half, FF_GROUPS - 1, m)
                        if m:
                            norm_add(NORM[half]["y"], X_LO[half], m - 1)
                    norm_add(NORM[half]["y"], X_LO[half], KT_D - 1)
                    output_scale(half)
                    continue
                n = NORM[half + 1]["x"]
                for m in range(KT_D):
                    output_tile(half, FF_GROUPS - 2, m)
                    for k in range(2 * (m - 4), 2 * (m - 3)) if m >= 4 else ():
                        norm_add(n, X_HI[half + 1], k)
                done = 0
                for m in range(KT_D):
                    output_tile(half, FF_GROUPS - 1, m)
                    if m == 1:
                        norm_root(n)
                    while m >= 2 and done < (m - 1) * (KT_D + 1) // 6:
                        input_tile(half + 1, done)
                        done += 1


SMALL = (["lam_re", "lam_im", "logdt", "dt", "lr", "lrdt", "th", "ang", "mag", "sin", "sinh", "cos", "ar", "ai",
          "t0", "t1", "t2", "t3", "fr", "fi"] + ["pr"] + ["pr_"] * J + ["pi"] + ["pi_"] * J)


def lay_out(a):
    f = np.float32

    def halves(prompt, sample):
        xp = prompt.reshape(HALVES, TP, D_MODEL)
        xs = sample.reshape(HALVES, DT, D_MODEL)
        x = np.concatenate([xp, xs], axis=1)
        x = x.reshape(HALVES, N, KT_D, P).transpose(0, 3, 2, 1)
        return np.ascontiguousarray(x.reshape(HALVES, P, KT_D * N))

    def tile_blocks(w):
        k, m = w.shape[0] // P, w.shape[1] // P
        w = w.reshape(k // 4, 4, P, m, P).transpose(3, 0, 2, 1, 4)
        return w.reshape(m, k // 4, P, WB)

    w_in = a["w_in"]
    offs = np.cumsum([0, 512, 256, 256, 512, 512, 16, 1024, 1024])
    u_v, r, low, gs, gg = (w_in[:, offs[0]:offs[4]], w_in[:, offs[4]:offs[5]], w_in[:, offs[5]:offs[6]],
                           w_in[:, offs[6]:offs[7]], w_in[:, offs[7]:offs[8]])
    stages = [tile_blocks(u_v).reshape(-1, P, WB), tile_blocks(a["w_s5_glu"]).reshape(-1, P, WB)]

    def merged(g, br):
        return np.concatenate([tile_blocks(g), tile_blocks(br)], axis=1).reshape(-1, P, WB)
    stages += [merged(gs, a["w_s5_br"]), tile_blocks(r).reshape(-1, P, WB), merged(gg, a["w_gla_br"]),
               tile_blocks(a["w_out"]).reshape(-1, P, WB)]
    up = tile_blocks(a["w_ff1"]).reshape(FF_GROUPS, 8, P, WB)
    down = tile_blocks(a["w_ff2"]).transpose(1, 0, 2, 3)
    stages += [up[0], up[1]]
    for g in range(FF_GROUPS):
        stages.append(down[g])
        if g + 2 < FF_GROUPS:
            stages.append(up[g + 2])
    wpack = np.ascontiguousarray(np.concatenate(stages))
    assert wpack.shape == (ITERS * RING, P, WB), wpack.shape

    wa = np.zeros((P, KT_D, P), f)
    wa[:, :, 0:RANK] = low.reshape(KT_D, P, RANK).transpose(1, 0, 2)
    vec = np.zeros((P, V_ALL), f)
    for at, g in ((V_MIX, "g_mix"), (V_FFN, "g_ffn"), (V_FIN, "g_final")):
        vec[:, at:at + KT_D] = a[g].reshape(KT_D, P).T
    vec[:, V_BG:V_BG + 2] = a["b_gate"].reshape(2, P).T
    vec[:, V_GLA] = a["g_gla_norm"]
    for s in range(DS):
        vec[s * DEC_SEQ:(s + 1) * DEC_SEQ, V_SEQ + s] = 1.0

    def level_masks(L, levels):
        j, out = np.arange(L)[:, None], []
        for s in levels:
            i = np.arange(L // 2)[None, :]
            m = (j // (2 * s) == i // s) & (j % (2 * s) < s)
            out.append(np.tile(m, (1, 4)))
        out.append(np.tile(np.eye(L, dtype=bool), (1, 4)))
        return np.ascontiguousarray(np.concatenate(out, axis=1).astype(f))

    def by_pair(v):
        v = v.reshape(PAIRS, 2, S5_STATE, *v.shape[2:])
        return np.moveaxis(v, 0, 2).reshape(P, PAIRS, *v.shape[3:])

    logdt = np.broadcast_to(a["log_dt"][:, None], (S5_GROUPS, S5_STATE))
    s5small = np.stack([by_pair(a["lam_re"]), by_pair(a["lam_im"]), by_pair(logdt)], axis=1)
    b = np.stack([by_pair(a["b_re"]), by_pair(a["b_im"])], axis=1)
    c = np.stack([by_pair(a["c_re"].transpose(0, 2, 1)), by_pair(a["c_im"].transpose(0, 2, 1))], axis=1)
    cbd = np.zeros((2, S5_STATE, 2, PAIRS, 2, S5_GROUP), f)
    cc = c.reshape(2, S5_STATE, 2, PAIRS, S5_GROUP)
    for g in range(2):
        cbd[g, :, :, :, g, :] = cc[g]
    dcol = np.tile(a["d_skip"].T, (J, 1))

    def s5_states(v):
        v = v.reshape(HALVES, DS, PAIRS, 2, S5_STATE).transpose(0, 3, 4, 2, 1)
        return v.reshape(HALVES, P, PAIRS, DS)
    s5dec = np.stack([s5_states(a["state_s5_re"]), s5_states(a["state_s5_im"])], axis=2)
    gd = a["state_gla"].reshape(HALVES, DS, 2, 2, DK, DV).transpose(0, 3, 4, 1, 2, 5)
    out = {
        "xT": halves(a["x_prompt"], a["x_sample"]), "wpack": wpack, "wa": wa.reshape(P, -1), "wgu_d": a["w_gate_up"],
        "vec_d": vec, "ident_d": np.eye(P, dtype=f), "masks_d": level_masks(C, LEVELS),
        "dmask_d": level_masks(DT, [LEVELS[l] for l in DEC_LEVELS]), "s5small": s5small,
        "b_d": b.reshape(P, -1), "c_d": c.reshape(P, -1), "cbd_d": cbd.reshape(P, -1), "dcol_d": dcol,
        "s5dec_d": s5dec, "gladec_d": gd.reshape(HALVES, P, -1),
    }
    return {k: np.ascontiguousarray(v) for k, v in out.items()}


OUTS = {"yT": (HALVES, P, KT_D * N), "s5_prompt": (P, 2, PAIRS), "gla_prompt": (P, 2, DV),
        "s5_dec_out": (HALVES, P, 2, PAIRS, DS), "gla_dec_out": (HALVES, P, DS * 2 * DV)}


def kernel(**inputs):
    from concourse import bacc
    from concourse.bass_utils import run_bass_kernel_spmd

    nc = bacc.Bacc("TRN2", target_bir_lowering=False, num_devices=1)
    arrays = lay_out({k: np.asarray(v) for k, v in inputs.items()})
    aps = {n: nc.dram_tensor(n, v.shape, mybir.dt.from_np(v.dtype), kind="ExternalInput").ap()
           for n, v in arrays.items()}
    for n, shape in OUTS.items():
        aps[n] = nc.dram_tensor(n, shape, F32, kind="ExternalOutput").ap()
    build(nc, **aps)
    got = run_bass_kernel_spmd(nc, [arrays], core_ids=[0]).results[0]

    y = got["yT"].reshape(HALVES, P, KT_D, N).transpose(0, 3, 2, 1).reshape(HALVES, N, D_MODEL)
    y_prompt = np.ascontiguousarray(y[:, 0:TP].reshape(1, SEQ, D_MODEL))
    y_sample = np.ascontiguousarray(y[:, TP:N].reshape(DEC_BATCH, DEC_SEQ, D_MODEL))
    sp = got["s5_prompt"].reshape(2, S5_STATE, 2, PAIRS).transpose(2, 3, 0, 1).reshape(2, 1, S5_GROUPS, S5_STATE)
    gp = got["gla_prompt"].reshape(2, DK, 2, DV).transpose(2, 0, 1, 3).reshape(1, HEADS, DK, DV)
    sd = got["s5_dec_out"].reshape(HALVES, 2, S5_STATE, 2, PAIRS, DS).transpose(3, 0, 5, 4, 1, 2)
    sd = sd.reshape(2, DEC_BATCH, S5_GROUPS, S5_STATE)
    gd = got["gla_dec_out"].reshape(HALVES, 2, DK, DS, 2, DV).transpose(0, 3, 4, 1, 2, 5)
    gd = gd.reshape(DEC_BATCH, HEADS, DK, DV)
    return tuple(np.ascontiguousarray(v) for v in (y_prompt, y_sample, sp[0], sp[1], gp, sd[0], sd[1], gd))
```
